# Optimizing a Trainium2 kernel written in Bass

```python
import jax, jax.numpy as jnp
from jax import lax
import numpy as np

D_MODEL = 1024
BATCH = 1
SEQ = 256
DEPTH = 2

N_Q_HEADS = 16
N_KV_HEADS = 2
HEAD_DIM = 64
WINDOW = 128
ATT_BLOCK = 128
GLA_HEADS = 4
GLA_DK = 128
GLA_DV = 256
GLA_RANK = 16
GLA_GATE_NORMALIZER = 16.0
GLA_CHUNK = 16
D_FF = 2816
N_MOD = 9
EPS = 1e-6

ATT_Q_W = N_Q_HEADS * HEAD_DIM
ATT_KV_W = N_KV_HEADS * HEAD_DIM
GLA_K_W = GLA_HEADS * GLA_DK
GLA_V_W = GLA_HEADS * GLA_DV
IN_SPLIT_SIZES = (ATT_Q_W, ATT_KV_W, ATT_KV_W, GLA_K_W, GLA_K_W, GLA_V_W, GLA_RANK, GLA_V_W, D_MODEL, D_MODEL)
IN_COLS = ATT_Q_W + 2 * ATT_KV_W + 2 * GLA_K_W + 2 * GLA_V_W + GLA_RANK + 2 * D_MODEL

kernel_name = 'hybrid_swa_gla_macaron_adaln'

def rmsnorm(x, gain):
    xf = x.astype(jnp.float32)
    y = xf * lax.rsqrt(jnp.mean(xf * xf, axis=-1, keepdims=True) + EPS)
    return (y * gain.astype(jnp.float32)).astype(x.dtype)

def modulate(h, shift, scale):
    return h * (1 + scale[:, None, :]) + shift[:, None, :]

def swiglu(h, w_in, w_out):
    gate, up = jnp.split(h @ w_in, 2, axis=-1)
    return (jax.nn.silu(gate) * up) @ w_out

def sliding_window_attention(q, k, v, sinks):
    B, S = q.shape[:2]
    nb = S // ATT_BLOCK
    grp = N_Q_HEADS // N_KV_HEADS
    qb = q.reshape(B, nb, ATT_BLOCK, N_KV_HEADS, grp, HEAD_DIM)

    def band(t):
        tb = t.reshape(B, nb, ATT_BLOCK, N_KV_HEADS, HEAD_DIM)
        prev = jnp.concatenate([jnp.zeros_like(tb[:, :1]), tb[:, :-1]], axis=1)
        return jnp.concatenate([prev, tb], axis=2)

    kb, vb = band(k), band(v)
    s = jnp.einsum('bnqhgd,bnkhd->bnhgqk', qb, kb).astype(jnp.float32) * (HEAD_DIM ** -0.5)
    q_pos = jnp.arange(ATT_BLOCK)[:, None] + ATT_BLOCK
    k_pos = jnp.arange(2 * ATT_BLOCK)[None, :]
    dist = q_pos - k_pos
    in_window = (dist >= 0) & (dist < WINDOW)
    key_abs = (jnp.arange(nb)[:, None] - 1) * ATT_BLOCK + k_pos
    mask = in_window[None] & (key_abs >= 0)[:, None, :]
    s = jnp.where(mask[None, :, None, None], s, -jnp.inf)
    sink = sinks.astype(jnp.float32).reshape(N_KV_HEADS, grp)[None, None, :, :, None, None]
    m = jnp.maximum(jnp.max(s, axis=-1, keepdims=True), sink)
    p = jnp.exp(s - m)
    p = p / (jnp.sum(p, axis=-1, keepdims=True) + jnp.exp(sink - m))
    o = jnp.einsum('bnhgqk,bnkhd->bnqhgd', p.astype(v.dtype), vb)
    return o.reshape(B, S, N_Q_HEADS * HEAD_DIM)

def gated_linear_attention(q, k, v, log_a):
    B, S, H, dk = q.shape
    nc = S // GLA_CHUNK

    def chunks(t):
        return t.reshape(B, nc, GLA_CHUNK, H, t.shape[-1]).astype(jnp.float32)

    q = chunks(q) * (dk ** -0.5)
    k, v, g = chunks(k), chunks(v), chunks(log_a)
    G = jnp.cumsum(g, axis=2)
    G_first = G[:, :, :1]
    G_last = G[:, :, -1:]
    q_rel = q * jnp.exp(G - G_first)
    k_rel = k * jnp.exp(G_first - G)
    A = jnp.einsum('bnihd,bnjhd->bnhij', q_rel, k_rel)
    causal = jnp.tril(jnp.ones((GLA_CHUNK, GLA_CHUNK), dtype=bool))
    A = jnp.where(causal, A, 0.0)
    o_intra = jnp.einsum('bnhij,bnjhv->bnihv', A, v)
    qg = q * jnp.exp(G)
    kg = k * jnp.exp(G_last - G)
    decay = jnp.exp(G_last[:, :, 0])

    def step(state, inp):
        qg_c, kg_c, v_c, dec = inp
        o = jnp.einsum('bihd,bhdv->bihv', qg_c, state)
        state = dec[..., None] * state + jnp.einsum('bjhd,bjhv->bhdv', kg_c, v_c)
        return state, o

    state0 = jnp.zeros((B, H, dk, v.shape[-1]), jnp.float32)
    xs = (jnp.moveaxis(qg, 1, 0), jnp.moveaxis(kg, 1, 0), jnp.moveaxis(v, 1, 0), jnp.moveaxis(decay, 1, 0))
    _, o_inter = lax.scan(step, state0, xs)
    o = o_intra + jnp.moveaxis(o_inter, 0, 1)
    return o.reshape(B, S, H, v.shape[-1])

def token_mixer(h, w_in, sinks, w_gate, b_gate, gla_norm, w_out):
    B, S, _ = h.shape
    split_at = [int(i) for i in np.cumsum(IN_SPLIT_SIZES)[:-1]]
    qa, ka, va, qb, kb, vb, lr, r, ga, gb = jnp.split(h @ w_in, split_at, axis=-1)
    ya = sliding_window_attention(qa.reshape(B, S, N_Q_HEADS, HEAD_DIM),
                                  ka.reshape(B, S, N_KV_HEADS, HEAD_DIM),
                                  va.reshape(B, S, N_KV_HEADS, HEAD_DIM), sinks)
    log_a = jax.nn.log_sigmoid((lr @ w_gate + b_gate).astype(jnp.float32)) / GLA_GATE_NORMALIZER
    ob = gated_linear_attention(qb.reshape(B, S, GLA_HEADS, GLA_DK),
                                kb.reshape(B, S, GLA_HEADS, GLA_DK),
                                vb.reshape(B, S, GLA_HEADS, GLA_DV),
                                log_a.reshape(B, S, GLA_HEADS, GLA_DK))
    yb = rmsnorm(ob, gla_norm).reshape(B, S, GLA_V_W).astype(h.dtype) * jax.nn.silu(r)
    merged = jax.nn.sigmoid(ga) * ya + jax.nn.sigmoid(gb) * yb
    return merged @ w_out

def setup_inputs(seed: int = 0) -> dict:
    key = jax.random.key(seed)
    ks = jax.random.split(key, 20)

    def w(k, shape, fan_in, gain=1.0):
        return jax.random.normal(k, shape, jnp.float32) * (gain * fan_in ** -0.5)

    def norm_gain(k, shape):
        return 1.0 + 0.02 * jax.random.normal(k, shape, jnp.float32)

    L = DEPTH
    return {
        'x': jax.random.normal(ks[0], (BATCH, SEQ, D_MODEL), jnp.float32),
        'c': jax.random.normal(ks[1], (BATCH, D_MODEL), jnp.float32),
        'ada_w': w(ks[2], (L, D_MODEL, N_MOD * D_MODEL), D_MODEL, 0.5),
        'ada_b': 0.02 * jax.random.normal(ks[3], (L, N_MOD * D_MODEL), jnp.float32),
        'norm1': norm_gain(ks[4], (L, D_MODEL)),
        'ffn1_w_in': w(ks[5], (L, D_MODEL, 2 * D_FF), D_MODEL),
        'ffn1_w_out': w(ks[6], (L, D_FF, D_MODEL), D_FF),
        'norm_mix': norm_gain(ks[7], (L, D_MODEL)),
        'mix_w_in': w(ks[8], (L, D_MODEL, IN_COLS), D_MODEL),
        'attn_sinks': jax.random.normal(ks[9], (L, N_Q_HEADS), jnp.float32),
        'gla_w_gate': w(ks[10], (L, GLA_RANK, GLA_K_W), GLA_RANK),
        'gla_b_gate': 0.1 * jax.random.normal(ks[11], (L, GLA_K_W), jnp.float32),
        'gla_out_norm': norm_gain(ks[12], (L, GLA_DV)),
        'mix_w_out': w(ks[13], (L, D_MODEL, D_MODEL), D_MODEL),
        'norm2': norm_gain(ks[14], (L, D_MODEL)),
        'ffn2_w_in': w(ks[15], (L, D_MODEL, 2 * D_FF), D_MODEL),
        'ffn2_w_out': w(ks[16], (L, D_FF, D_MODEL), D_FF),
        'final_norm': norm_gain(ks[17], (D_MODEL,)),
    }

def reference(x, c, ada_w, ada_b, norm1, ffn1_w_in, ffn1_w_out, norm_mix, mix_w_in,
              attn_sinks, gla_w_gate, gla_b_gate, gla_out_norm, mix_w_out, norm2,
              ffn2_w_in, ffn2_w_out, final_norm):
    cond = jax.nn.silu(c)
    for l in range(DEPTH):
        mod = cond @ ada_w[l] + ada_b[l]
        sh1, sc1, g1, sh2, sc2, g2, sh3, sc3, g3 = jnp.split(mod, N_MOD, axis=-1)
        h = modulate(rmsnorm(x, norm1[l]), sh1, sc1)
        x = x + 0.5 * g1[:, None, :] * swiglu(h, ffn1_w_in[l], ffn1_w_out[l])
        h = modulate(rmsnorm(x, norm_mix[l]), sh2, sc2)
        x = x + g2[:, None, :] * token_mixer(h, mix_w_in[l], attn_sinks[l], gla_w_gate[l],
                                             gla_b_gate[l], gla_out_norm[l], mix_w_out[l])
        h = modulate(rmsnorm(x, norm2[l]), sh3, sc3)
        x = x + 0.5 * g3[:, None, :] * swiglu(h, ffn2_w_in[l], ffn2_w_out[l])
    return rmsnorm(x, final_norm)


_drawn_inputs = setup_inputs


def setup_inputs(seed=0):
    import zlib

    import numpy as np

    out = dict(_drawn_inputs(seed))
    spreads = {}
    factors = {'norm1': 8.0,
     'norm_mix': 8.0,
     'attn_sinks': 64.0,
     'gla_b_gate': 7.801,
     'gla_out_norm': 8.0,
     'norm2': 8.0,
     'final_norm': 8.115}
    for name, (base, spread) in spreads.items():
        noise = np.random.default_rng([zlib.crc32(name.encode()), seed]).standard_normal(out[name].shape)
        drawn = base * np.exp(spread * noise) if base else spread * noise
        out[name] = __import__('jax').numpy.asarray(drawn.astype(out[name].dtype))
    for name, factor in factors.items():
        out[name] = (out[name] * factor).astype(out[name].dtype)
    return out
```

```python
from contextlib import ExitStack

import concourse.bass as bass
from concourse import mybir

F32 = mybir.dt.float32
F32R = mybir.dt.float32r
I32 = mybir.dt.int32
ALU = mybir.AluOpType
ACT = mybir.ActivationFunctionType
AX_X = mybir.AxisListType.X

P = 128
L = 2
D = 1024
KD = D // P
SEQ = 256
T = SEQ // P
D_FF = 2816
FC = 256
NJ = D_FF // FC
HEADS, DH, GROUP = 16, 64, 8
GH, DK, DV, RANK = 4, 128, 256, 16
CH = 16
NC = P // CH
EPS = 1e-6
MASKED = -1e30
RSQRT_SEED = float(0x5F3759DF)

UNIT = 2048
KA = 4
QKV0 = RANK + 2 * 128
N_CHUNK = 13
MIX_UNITS = 2 * N_CHUNK + KD // 2
NS = 3
MQ = MIX_UNITS // NS
NSEQ = 2 * NJ + MQ
ADA_W = 3 * D

C_LKV, C_Q, C_VB, C_KB, C_QB, C_R, C_GB, C_GA = 0, 1, 3, 5, 6, 7, 9, 11
TRANSPOSED = (C_KB, C_QB, C_Q, C_Q + 1)


HEAD_ORDER = [0, 1, 2, 3, 8, 9, 10, 11, 4, 5, 6, 7, 12, 13, 14, 15]


def mix_plan():
    steps = {
        2: [("gate_z",)], 3: [("gate_log",)], 11: [("gate_exp",), ("ks_diff", 0)], 12: [("k_turn",), ("ks_mul", 0)],
        13: [("q_exp",), ("state",)], 22: [("lin_norm",)],
    }
    for r in range(4):
        for at, what in ((14, "a"), (15, "o")):
            steps.setdefault(at + 2 * r, []).append((what, r))
        if r:
            steps.setdefault(12 + 2 * r, []).append(("ks_diff", r))
            steps.setdefault(13 + 2 * r, []).append(("ks_mul", r))
    for i in range(HEADS + 2):
        steps.setdefault(4 + i, []).insert(0, ("head", i))
    steps[4 + HEADS + 2] = [("att_norm",)] + steps.get(4 + HEADS + 2, [])
    plan = []
    for u in range(2 * N_CHUNK):
        plan.append(("unit", u))
        late = u in (11, 13)
        if u % 2 and late:
            plan.append(("evac", u // 2))
        plan += steps.get(u, [])
        if u % 2 and not late:
            plan.append(("evac", u // 2))
        plan.append(("split", u + NS))
        if u >= 1 and u % 3 == 1 and u // 3 < KD:
            plan.append(("ada", u // 3))
    return plan


PLAN = mix_plan()


class Signal:

    def __init__(self, sem, per_layer, before=0, by=1):
        self.sem, self.per_layer, self.before, self.by = sem, per_layer, before, by

    def at(self, layer, n):
        return layer * (self.per_layer * self.by) + (n + self.before) * self.by


class Chain:

    def __init__(self, engine, sem, per_layer):
        self.engine, self.sem, self.per_layer = engine, sem, per_layer
        self.before, self.start, self.n = 0, 0, 0

    def enter(self, layer):
        self.before = self.n
        self.start, self.n = layer * self.per_layer + self.before, 0

    def leave(self):
        assert self.n == self.per_layer, (self.n, self.per_layer)
        self.start, self.n = L * self.per_layer + self.before, 0

    def link(self, ins):
        self.n += 1
        ins.then_inc(self.sem, 1)
        self.engine.wait_ge(self.sem, self.start + self.n)


ACT_CHAIN, DVE_CHAIN = 2, 75


def trunk(nc, x_in, cond_in, w_stream, ada_first, ada_w, ada_bias, gains, sinks, gate_w, gate_b,
          gla_gain, final_gain, out):
    with ExitStack() as ctx:
        def sb(name, shape, dt=F32):
            return ctx.enter_context(nc.sbuf_tensor(name, shape, dt))

        def signal(name, per_layer, before=0, by=1):
            return Signal(ctx.enter_context(nc.semaphore(name)), per_layer, before, by)

        w_raw = [sb(f"w_raw{s}", [P, UNIT]) for s in range(NS)]
        w_hi = [sb(f"w_hi{s}", [P, UNIT], F32R) for s in range(NS)]
        w_lo = [sb(f"w_lo{s}", [P, UNIT], F32R) for s in range(NS)]
        ada_raw = sb("ada_raw", [P, ADA_W])
        ada_acc = sb("ada_acc", [P, 3, D])
        x = sb("x", [P, T, D])
        xn = sb("xn", [P, T, D])
        h_hi = sb("h_hi", [P, KD, SEQ], F32R)
        h_lo = sb("h_lo", [P, KD, SEQ], F32R)
        gate_row = sb("gate_row", [P, D])
        mod_shift = sb("mod_shift", [P, KD])
        mod_scale = sb("mod_scale", [P, KD])
        cond = sb("cond", [P, KD])
        gain_cols = sb("gain_cols", [P, 3 * L + 1, KD])
        ident = sb("ident", [P, P])
        ones = sb("ones", [P, P])
        sum_sq = sb("sum_sq", [P, T])
        rstd = sb("rstd", [P, T])
        newton = sb("newton", [P, 2, 2])
        sink_rows = sb("sink_rows", [P, HEADS])
        gate_weight = sb("gate_weight", [RANK, GH * DK])
        gate_bias = sb("gate_bias", [P, GH])
        gla_gain_row = sb("gla_gain_row", [P, DV])
        att_mask = sb("att_mask", [P, 3 * P])
        gla_mask = sb("gla_mask", [P, P])

        with ExitStack() as ffn_ctx:
            silu_g = ffn_ctx.enter_context(nc.sbuf_tensor("silu_g", [P, T, FC], F32))
            hidden = ffn_ctx.enter_context(nc.sbuf_tensor("hidden", [P, T, FC], F32))
            hid_hi = ffn_ctx.enter_context(nc.sbuf_tensor("hid_hi", [P, 2, SEQ], F32R))
            hid_lo = ffn_ctx.enter_context(nc.sbuf_tensor("hid_lo", [P, 2, SEQ], F32R))
        with ExitStack() as first_ctx:
            ada_stage = [first_ctx.enter_context(nc.sbuf_tensor(f"ada_stage{k}", [P, 2 * D], F32)) for k in range(KD)]
        q_t = sb("q_t", [P, HEADS // 2, SEQ])
        k_t = sb("k_t", [P, SEQ])
        v_att = sb("v_att", [P, T, P])
        qb_t = sb("qb_t", [P, GH, SEQ])
        kb_t = sb("kb_t", [P, GH, SEQ])
        vb = sb("vb", [P, T, GH * DV])
        w_gates = sb("w_gates", [P, T, D])
        z_buf = sb("z_buf", [P, GH, SEQ])
        g_cum = sb("g_cum", [P, GH, SEQ])
        q_state = sb("q_state", [P, GH, P])
        k_state = sb("k_state", [P, GH, P])
        k_state_t = sb("k_state_t", [P, GH * DK])
        state = sb("state", [P, GH * DV])
        a_t = sb("a_t", [P, GH, P])
        lr_t = a_t[:, 0:2, :].rearrange("p h i -> p (h i)")
        k_scaled = sb("k_scaled", [P, 2, NC, P])
        probs = [sb(f"probs{i}", [P, 3 * P]) for i in range(2)]
        probs_t = [sb(f"probs_t{i}", [P, 3 * P]) for i in range(2)]
        gla_ss = sb("gla_ss", [P, T * GH])
        gla_nt = sb("gla_nt", [P, 2, T * GH])
        gla_rstd = sb("gla_rstd", [P, T * GH])
        row_max = sb("row_max", [P, 2])
        neg_max = sb("neg_max", [P, HEADS, 2])
        row_sum = sb("row_sum", [P, HEADS, 2])
        sink_exp = sb("sink_exp", [P, HEADS, 2])
        th_buf = z_buf[:, :, :].rearrange("p h s -> p (h s)").rearrange("p (t n) -> p t n", t=T)

        ps = ctx.enter_context(nc.psum_tensor("ps", [P, 8, 512], F32))
        SUMS, HID, Y = 3, 2, 4
        SCORES, TURNED, LIN = 4, 5, 6

        const_in = signal("const_in", 0, by=16)
        stage_in = [signal(f"stage_in{k}", 0, by=16) for k in range(KD)]
        raw_in = [signal(f"raw_in{s}", NSEQ, by=16) for s in range(NS)]
        ada_in = signal("ada_in", 3 * KD, by=16)
        seeded = [signal(f"seeded{m}", 3, before=1, by=16) for m in range(3)]
        layer_in = signal("layer_in", 4, by=16)
        out_sent = signal("out_sent", 0, by=16)
        made = signal("made", 0)
        acc_cleared = signal("acc_cleared", 3, before=1)
        cond_ready = signal("cond_ready", 0)
        hi_done = [signal(f"hi_done{s}", NSEQ) for s in range(NS)]
        squared = signal("squared", 3 * T)
        normed = signal("normed", 3 * T)
        h_hi_done = signal("h_hi_done", 3 * T)
        silu_done = signal("silu_done", 2 * NJ * T)
        hid_hi_done = signal("hid_hi_done", 2 * NJ)
        gate_row_done = signal("gate_row_done", 6)
        act_chain = ctx.enter_context(nc.semaphore("act_chain"))
        log_done = signal("log_done", 1)
        exps_done = signal("exps_done", 3)
        evac_act = signal("evac_act", 6)
        tanh_done = signal("tanh_done", 6)
        k_state_t_done = signal("k_state_t_done", 1)
        state_done = signal("state_done", 1)
        ks_exp = signal("ks_exp", 4)
        lin_out = signal("lin_out", 4)
        lin_squared = signal("lin_squared", 4)
        probs_done = signal("probs_done", HEADS)
        probs_t_done = signal("probs_t_done", HEADS)
        att_out = signal("att_out", HEADS)
        sink_exp_done = signal("sink_exp_done", 1)
        mrg_hi_done = signal("mrg_hi_done", T)
        lo_done = [signal(f"lo_done{s}", NSEQ, before=1) for s in range(NS)]
        rstd_done = signal("rstd_done", 3)
        h_mod_done = signal("h_mod_done", 3 * T)
        h_ready = signal("h_ready", 3 * T)
        hidden_done = signal("hidden_done", 2 * NJ * T)
        hid_ready = signal("hid_ready", 2 * NJ)
        x_ready = signal("x_ready", 3 * T, before=T)
        stage_used = signal("stage_used", 0)
        ada_used = signal("ada_used", 3 * KD, before=1)
        mods_ready = signal("mods_ready", 3, before=1)
        dve_chain = ctx.enter_context(nc.semaphore("dve_chain"))
        z_done = signal("z_done", 1)
        diffs_done = signal("diffs_done", 2)
        evac_dve = signal("evac_dve", 1)
        k_state_done = signal("k_state_done", 1)
        q_ready = signal("q_ready", 1)
        ks_diff = signal("ks_diff", 4)
        ks_ready = signal("ks_ready", 4)
        a_ready = signal("a_ready", 4)
        th_used = signal("th_used", 6)
        scores_read = signal("scores_read", HEADS)
        soft_ready = signal("soft_ready", HEADS)
        sink_diff = signal("sink_diff", 1)
        merged = signal("merged", T)
        mrg_ready = signal("mrg_ready", T)
        final_done = signal("final_done", 0)
        used = [signal(f"used{s}", NSEQ, before=1) for s in range(NS)]
        gu0_done = signal("gu0_done", 2 * NJ)
        hid_tr = signal("hid_tr", 2 * NJ)
        y0_done = signal("y0_done", 3)
        x_tr = signal("x_tr", 3 * T)
        gate_sum = signal("gate_sum", 6)
        cols_sum = signal("cols_sum", 3, before=1)
        z_mm = signal("z_mm", 1)
        k_state_tr = signal("k_state_tr", 1)
        state_mm = signal("state_mm", 1)
        a_mm = signal("a_mm", 4)
        o_mm = signal("o_mm", 4)
        scores_mm = signal("scores_mm", HEADS)
        turned = signal("turned", HEADS + 1)
        mrg_tr = signal("mrg_tr", T)

        FFN1, MIX, FFN2 = range(3)
        q0 = {FFN1: 0, MIX: NJ, FFN2: NJ + MQ}
        ffn_no = {FFN1: 0, FFN2: 1}
        MADE = 10
        CONSTS = 3

        def bank_of(c):
            return 2 * (c % 2)

        def flat(ap):
            return ap.rearrange("p a b -> p (a b)")

        def chunk_done(engine, layer, c):
            u = 2 * c + 1
            engine.wait_ge(used[u % NS].sem, used[u % NS].at(layer, q0[MIX] + u // NS + 1))

        block = ctx.enter_context(nc.Block())

        @block.sync
        def _(sp):
            sp.dma_start(cond[:, :], cond_in).then_inc(const_in.sem, 16)
            sp.dma_start(gain_cols[:, :, :], gains).then_inc(const_in.sem, 16)
            sp.dma_start(x[:, :, :], x_in).then_inc(const_in.sem, 16)
            for k in range(KD):
                sp.dma_start(ada_stage[k][:, :], ada_first[k]).then_inc(stage_in[k].sem, 16)

            def load(s, layer, q):
                sp.wait_ge(lo_done[s].sem, lo_done[s].at(layer, q))
                sp.dma_start(w_raw[s][:, :], w_stream[s][bass.ds(layer * NSEQ + q, 1)].rearrange("a p n -> p (a n)"))\
                    .then_inc(raw_in[s].sem, 16)

            def load_ada(layer, n):
                sp.wait_ge(ada_used.sem, ada_used.at(layer, n))
                sp.dma_start(ada_raw[:, :], ada_w[bass.ds(layer * (3 * KD) + n, 1)].rearrange("a p n -> p (a n)"))\
                    .then_inc(ada_in.sem, 16)

            def ffn(layer, stage):
                q = q0[stage]
                load(0, layer, q)
                load(1, layer, q)
                load(0, layer, q + 1)
                load(1, layer, q + 1)
                load(2, layer, q)
                load_ada(layer, stage * KD)
                with sp.Fori(1, KD) as j:
                    load(0, layer, q + 1 + j)
                    load(1, layer, q + 1 + j)
                    load(2, layer, q + j)
                    load_ada(layer, stage * KD + j)
                with sp.Fori(KD, NJ - 1) as j:
                    load(0, layer, q + 1 + j)
                    load(1, layer, q + 1 + j)
                    load(2, layer, q + j)
                load(2, layer, q + NJ - 1)

            with sp.Fori(0, L) as layer:
                ffn(layer, FFN1)
                for dst, src in ((sink_rows, sinks), (gate_weight, gate_w), (gate_bias, gate_b), (gla_gain_row, gla_gain)):
                    sp.dma_start(dst[:, :], src[bass.ds(layer, 1)].rearrange("a p n -> p (a n)"))\
                        .then_inc(layer_in.sem, 16)
                for m in range(MQ):
                    for s in range(NS):
                        load(s, layer, q0[MIX] + m)
                    if m < KD:
                        load_ada(layer, MIX * KD + m)
                ffn(layer, FFN2)

            sp.wait_ge(x_ready.sem, x_ready.at(L, 0))
            sp.dma_start(gate_row[:, :], final_gain).then_inc(const_in.sem, 16)
            for t in range(T):
                sp.wait_ge(final_done.sem, t + 1)
                sp.dma_start(out[t * P:(t + 1) * P, :], xn[:, t, :]).then_inc(out_sent.sem, 16)
            sp.wait_ge(out_sent.sem, T * 16)

        @block.gpsimd
        def _(pool):
            def seed(n):
                pool.memset(ada_acc[:, :, :], 0.0).then_inc(acc_cleared.sem, 1)
                pool.wait_ge(acc_cleared.sem, n + 1)
                for m in range(3):
                    pool.dma_start(ada_acc[0:1, m, :], ada_bias[n:n + 1, m, :]).then_inc(seeded[m].sem, 16)

            seed(0)
            pool.memset(ident[:, :], 0.0).then_inc(made.sem, 1)
            pool.memset(ones[:, :], 1.0).then_inc(made.sem, 1)
            pool.memset(att_mask[:, :], 0.0).then_inc(made.sem, 1)
            pool.memset(gla_mask[:, :], 1.0).then_inc(made.sem, 1)
            pool.wait_ge(made.sem, 4)
            pool.affine_select(out=ident[:, :], in_=ident[:, :], compare_op=ALU.not_equal, fill=1.0, base=0,
                               pattern=[[-1, P]], channel_multiplier=1).then_inc(made.sem, 1)
            pool.affine_select(out=att_mask[:, 0:P], in_=att_mask[:, 0:P], compare_op=ALU.is_gt, fill=MASKED,
                               base=0, pattern=[[1, P]], channel_multiplier=-1).then_inc(made.sem, 1)
            for i in (1, 2):
                pool.affine_select(out=att_mask[:, i * P:(i + 1) * P], in_=att_mask[:, i * P:(i + 1) * P],
                                   compare_op=ALU.is_ge, fill=MASKED, base=0, pattern=[[-1, P]],
                                   channel_multiplier=1).then_inc(made.sem, 1)
            pool.affine_select(out=gla_mask[:, :], in_=gla_mask[:, :], compare_op=ALU.is_ge, fill=0.0, base=0,
                               pattern=[[1, P]], channel_multiplier=-1).then_inc(made.sem, 1)
            pool.wait_ge(stage_used.sem, KD)
            pool.memset(k_scaled[:, :, :, :], 0.0).then_inc(made.sem, 1)
            for n in range(3 * L):
                pool.wait_ge(cols_sum.sem, cols_sum.at(0, n))
                seed(n + 1)

        @block.scalar
        def _(act):
            chain = Chain(act, act_chain, ACT_CHAIN)

            def split_hi(s, layer, q):
                act.wait_ge(raw_in[s].sem, raw_in[s].at(layer, q + 1))
                act.wait_ge(used[s].sem, used[s].at(layer, q))
                act.activation(w_hi[s][:, :], w_raw[s][:, :], ACT.Copy).then_inc(hi_done[s].sem, 1)

            def norm(layer, n):
                for t in range(T):
                    act.wait_ge(x_ready.sem, x_ready.at(layer, (n - 1) * T + t + 1))
                    act.activation(xn[:, t, :], x[:, t, :], ACT.Square, accum_out=sum_sq[:, t:t + 1])\
                        .then_inc(squared.sem, 1)
                act.wait_ge(squared.sem, squared.at(layer, (n + 1) * T))
                act.wait_ge(rstd_done.sem, rstd_done.at(layer, n + 1))
                for t in range(T):
                    act.activation(xn[:, t, :], x[:, t, :], ACT.Copy, scale=rstd[:, t:t + 1]).then_inc(normed.sem, 1)

            def prepare(layer, n):
                norm(layer, n)
                for t in range(T):
                    act.wait_ge(h_mod_done.sem, h_mod_done.at(layer, n * T + t + 1))
                    act.activation(h_hi[:, :, t * P:(t + 1) * P],
                                   xn[:, t, :].rearrange("p (k i) -> p k i", k=KD), ACT.Copy)\
                        .then_inc(h_hi_done.sem, 1)

            def gate_half(layer, stage, half):
                act.wait_ge(gate_sum.sem, gate_sum.at(layer, 2 * stage + half + 1))
                act.activation(gate_row[:, half * 512:(half + 1) * 512], ps[:, SUMS, :], ACT.Copy,
                               scale=1.0 if stage == MIX else 0.5).then_inc(gate_row_done.sem, 1)

            def ffn(layer, stage, first):
                q, f = q0[stage], ffn_no[stage]
                if first:
                    split_hi(0, layer, q)
                    split_hi(1, layer, q)
                prepare(layer, stage)

                def hid_part(j):
                    act.wait_ge(hid_tr.sem, hid_tr.at(layer, f * NJ + j + 1))
                    act.wait_ge(used[2].sem, used[2].at(layer, q + j))
                    act.activation(flat(hid_hi[:, :, :]), ps[:, HID, :], ACT.Copy).then_inc(hid_hi_done.sem, 1)

                def silus(j, first=False):
                    for t in range(T):
                        if t == 0:
                            act.wait_ge(gu0_done.sem, gu0_done.at(layer, f * NJ + j + 1))
                        else:
                            act.wait_ge(used[1].sem, used[1].at(layer, q + j + 1))
                        if not first:
                            act.wait_ge(hidden_done.sem, hidden_done.at(layer, (f * NJ + j) * T + t + 1 - T))
                        act.activation(silu_g[:, t, :], ps[:, t, 0:FC], ACT.Silu).then_inc(silu_done.sem, 1)

                split_hi(0, layer, q + 1)
                silus(0, first=True)
                split_hi(1, layer, q + 1)
                split_hi(2, layer, q)
                with act.Fori(1, NJ - 1) as j:
                    hid_part(j - 1)
                    split_hi(0, layer, q + j + 1)
                    silus(j)
                    split_hi(1, layer, q + j + 1)
                    split_hi(2, layer, q + j)
                gate_half(layer, stage, 0)
                hid_part(NJ - 2)
                if stage == FFN1:
                    split_hi(0, layer, q + NJ)
                silus(NJ - 1)
                gate_half(layer, stage, 1)
                if stage == FFN1:
                    split_hi(1, layer, q + NJ)
                split_hi(2, layer, q + NJ - 1)
                hid_part(NJ - 1)

            def mix(layer):
                prepare(layer, MIX)
                n_evac = 0
                split_hi(2, layer, q0[MIX])
                for what, *arg in PLAN:
                    if what == "split":
                        u = arg[0]
                        split_hi(u % NS, layer, q0[MIX] + u // NS)
                    elif what == "evac":
                        c, b = arg[0], bank_of(arg[0])
                        if c == C_QB:
                            continue
                        chunk_done(act, layer, c)
                        if c == C_LKV:
                            act.activation(lr_t[0:RANK], ps[0:RANK, 0, 0:SEQ], ACT.Copy)
                            act.activation(k_t[:, :], ps[:, 0, SEQ:2 * SEQ], ACT.Copy)
                            act.activation(flat(v_att[:, :, :]), ps[:, 1, 0:SEQ], ACT.Copy).then_inc(evac_act.sem, 1)
                        elif c == C_KB:
                            act.activation(flat(kb_t[:, :, :]), flat(ps[:, b:b + 2, :]), ACT.Copy)\
                                .then_inc(evac_act.sem, 1)
                        elif c in (C_Q, C_Q + 1):
                            g = 4 * (c - C_Q)
                            act.activation(flat(q_t[:, g:g + 4, :]), flat(ps[:, b:b + 2, :]), ACT.Copy)\
                                .then_inc(evac_act.sem, 1)
                        elif c in (C_VB, C_VB + 1):
                            o = 512 * (c - C_VB)
                            act.activation(vb[:, :, o:o + 512], ps[:, b:b + 2, :], ACT.Copy).then_inc(evac_act.sem, 1)
                        else:
                            n = c - C_R
                            if n:
                                act.wait_ge(th_used.sem, th_used.at(layer, n))
                            else:
                                act.wait_ge(q_ready.sem, q_ready.at(layer, 1))
                            act.activation(th_buf, ps[:, b:b + 2, :], ACT.Tanh, scale=0.5).then_inc(tanh_done.sem, 1)
                    elif what == "gate_log":
                        act.wait_ge(z_done.sem, z_done.at(layer, 1))
                        chain.link(act.activation(flat(g_cum[:, :, :]), flat(z_buf[:, :, :]), ACT.Abs))
                        chain.link(act.activation(flat(g_cum[:, :, :]), flat(g_cum[:, :, :]), ACT.Exp, scale=-1.0))
                        act.activation(flat(g_cum[:, :, :]), flat(g_cum[:, :, :]), ACT.Ln, bias=1.0)\
                            .then_inc(log_done.sem, 1)
                    elif what == "gate_exp":
                        act.wait_ge(diffs_done.sem, diffs_done.at(layer, 1))
                        act.activation(k_state[:, :, :], k_state[:, :, :], ACT.Exp, scale=1 / 16.0)\
                            .then_inc(exps_done.sem, 1)
                        act.activation(q_state[:, :, :], g_cum[:, :, P:2 * P], ACT.Exp, scale=1 / 16.0)\
                            .then_inc(exps_done.sem, 1)
                        act.wait_ge(diffs_done.sem, diffs_done.at(layer, 2))
                        act.activation(flat(z_buf[:, :, :]), flat(z_buf[:, :, :]), ACT.Exp, scale=1 / 16.0)\
                            .then_inc(exps_done.sem, 1)
                    elif what == "k_turn":
                        act.wait_ge(k_state_tr.sem, k_state_tr.at(layer, 1))
                        act.activation(k_state_t[:, :], ps[:, LIN, :], ACT.Copy).then_inc(k_state_t_done.sem, 1)
                    elif what == "state":
                        act.wait_ge(state_mm.sem, state_mm.at(layer, 1))
                        act.activation(state[:, :], flat(ps[:, LIN:LIN + 2, :]), ACT.Copy).then_inc(state_done.sem, 1)
                    elif what == "ks_diff":
                        act.wait_ge(ks_diff.sem, ks_diff.at(layer, arg[0] + 1))
                        for c in range(NC):
                            part = k_scaled[:, :, c, 0:CH * (c + 1)]
                            last = act.activation(part, part, ACT.Exp, scale=1 / 16.0)
                        last.then_inc(ks_exp.sem, 1)
                    elif what == "o":
                        r = arg[0]
                        t, hp = r // 2, 2 * (r % 2)
                        act.wait_ge(o_mm.sem, o_mm.at(layer, r + 1))
                        act.activation(vb[:, t, hp * DV:(hp + 2) * DV], ps[:, LIN + 1, :], ACT.Copy)\
                            .then_inc(lin_out.sem, 1)
                        act.wait_ge(lin_out.sem, lin_out.at(layer, r + 1))
                        for h in range(2):
                            o = ps[:, LIN + 1, h * DV:(h + 1) * DV]
                            n = t * GH + hp + h
                            last = act.activation(o, o, ACT.Square, accum_out=gla_ss[:, n:n + 1])
                        last.then_inc(lin_squared.sem, 1)
                    elif what == "head":
                        i = arg[0]
                        if i < HEADS:
                            p, h = probs[i % 2], HEAD_ORDER[i]
                            act.wait_ge(soft_ready.sem, soft_ready.at(layer, i + 1))
                            act.activation(p[:, 0:2 * P], p[:, 0:2 * P], ACT.Exp, bias=neg_max[:, h, 0:1],
                                           accum_out=row_sum[:, h, 0:1])
                            act.activation(p[:, 2 * P:3 * P], p[:, 2 * P:3 * P], ACT.Exp, bias=neg_max[:, h, 1:2],
                                           accum_out=row_sum[:, h, 1:2]).then_inc(probs_done.sem, 1)
                        if 2 <= i:
                            h = HEAD_ORDER[i - 2]
                            act.wait_ge(turned.sem, turned.at(layer, i))
                            act.activation(xn[:, :, h * DH:(h + 1) * DH],
                                           ps[:, TURNED, 3 * P:4 * P].rearrange("p (t d) -> p t d", t=T),
                                           ACT.Copy).then_inc(att_out.sem, 1)
                        if 1 <= i <= HEADS:
                            act.wait_ge(turned.sem, turned.at(layer, i))
                            act.activation(probs_t[(i - 1) % 2][:, :], ps[:, TURNED, 0:3 * P], ACT.Copy)\
                                .then_inc(probs_t_done.sem, 1)
                    elif what == "att_norm":
                        act.wait_ge(sink_diff.sem, sink_diff.at(layer, 1))
                        act.activation(flat(sink_exp[:, :, :]), flat(sink_exp[:, :, :]), ACT.Exp)\
                            .then_inc(sink_exp_done.sem, 1)
                for t in range(T):
                    act.wait_ge(mrg_tr.sem, mrg_tr.at(layer, t + 1))
                    act.activation(h_hi[:, :, t * P:(t + 1) * P],
                                   ps[:, 2 * t:2 * t + 2, :].rearrange("p b (k i) -> p (b k) i", i=P), ACT.Copy)\
                        .then_inc(mrg_hi_done.sem, 1)
                for u in range(2 * N_CHUNK, MIX_UNITS - 1):
                    split_hi(u % NS, layer, q0[MIX] + (u + NS) // NS)
                    if u < 2 * N_CHUNK + 2:
                        gate_half(layer, MIX, u - 2 * N_CHUNK)

            act.wait_ge(const_in.sem, CONSTS * 16)
            act.activation(cond[:, :], cond[:, :], ACT.Silu).then_inc(cond_ready.sem, 1)
            with act.Fori(0, L) as layer:
                chain.enter(layer)
                ffn(layer, FFN1, True)
                mix(layer)
                ffn(layer, FFN2, False)
            chain.leave()
            norm(L, 0)

        @block.vector
        def _(dve):
            chain = Chain(dve, dve_chain, DVE_CHAIN)

            def split_lo(s, layer, q):
                dve.wait_ge(hi_done[s].sem, hi_done[s].at(layer, q + 1))
                dve.tensor_tensor(w_lo[s][:, :], w_raw[s][:, :], w_hi[s][:, :].bitcast(F32), ALU.subtract)\
                    .then_inc(lo_done[s].sem, 1)

            def rsqrt(y, v, tmp, sums, width):
                chain.link(dve.tensor_scalar(v, sums, 1.0 / width, EPS, ALU.mult, ALU.add))
                chain.link(dve.tensor_scalar(y.bitcast(I32), v.bitcast(I32), -0.5, RSQRT_SEED, ALU.mult, ALU.add))
                for n in range(3):
                    chain.link(dve.scalar_tensor_tensor(out=tmp, in0=y, scalar=-0.5, in1=y, op0=ALU.mult, op1=ALU.mult))
                    chain.link(dve.tensor_tensor(tmp, tmp, v, ALU.mult))
                    last = dve.scalar_tensor_tensor(out=y, in0=tmp, scalar=1.5, in1=y, op0=ALU.add, op1=ALU.mult)
                    if n < 2:
                        chain.link(last)
                return last

            def norm(layer, n):
                dve.wait_ge(squared.sem, squared.at(layer, (n + 1) * T))
                rsqrt(rstd[:, :], newton[:, 0, :], newton[:, 1, :], sum_sq[:, :], D).then_inc(rstd_done.sem, 1)

            def prepare(layer, n):
                norm(layer, n)
                dve.wait_ge(mods_ready.sem, mods_ready.at(layer, n))
                for t in range(T):
                    dve.wait_ge(x_tr.sem, x_tr.at(layer, n * T + t + 1))
                    for k in range(KD):
                        last = dve.tensor_scalar(xn[:, t, k * P:(k + 1) * P],
                                                 ps[:, 2 * t + k // 4, (k % 4) * P:(k % 4 + 1) * P],
                                                 mod_scale[:, k:k + 1], mod_shift[:, k:k + 1], ALU.mult, ALU.add)
                    last.then_inc(h_mod_done.sem, 1)
                for t in range(T):
                    dve.wait_ge(h_hi_done.sem, h_hi_done.at(layer, n * T + t + 1))
                    part = (slice(None), slice(None), slice(t * P, (t + 1) * P))
                    dve.tensor_tensor(h_lo[part], xn[:, t, :].rearrange("p (k i) -> p k i", k=KD),
                                      h_hi[part].bitcast(F32), ALU.subtract).then_inc(h_ready.sem, 1)

            def residual(layer, stage):
                q_last = q0[stage] + (MQ if stage == MIX else NJ)
                dve.wait_ge(gate_row_done.sem, gate_row_done.at(layer, 2 * stage + 2))
                for t in range(T):
                    if t == 0:
                        dve.wait_ge(y0_done.sem, y0_done.at(layer, stage + 1))
                    else:
                        dve.wait_ge(used[2].sem, used[2].at(layer, q_last))
                    chain.link(dve.tensor_tensor(xn[:, t, :], flat(ps[:, Y + 2 * t:Y + 2 * t + 2, :]), gate_row[:, :],
                                                 ALU.mult))
                    dve.tensor_tensor(x[:, t, :], x[:, t, :], xn[:, t, :], ALU.add).then_inc(x_ready.sem, 1)

            def add_ada(layer, stage, k):
                n = stage * KD + k
                dve.wait_ge(ada_in.sem, ada_in.at(layer, n + 1))
                dve.wait_ge(ada_used.sem, ada_used.at(layer, n))
                col = cond[:, k:k + 1] if isinstance(k, int) else cond[:, bass.ds(k, 1)]
                for m in range(3):
                    last = dve.scalar_tensor_tensor(out=ada_acc[:, m, :], in0=ada_raw[:, m * D:(m + 1) * D], scalar=col,
                                                    in1=ada_acc[:, m, :], op0=ALU.mult, op1=ALU.add)
                last.then_inc(ada_used.sem, 1)

            def take_mods(layer, stage, n_gain):
                dve.wait_ge(cols_sum.sem, cols_sum.at(layer, stage + 1))
                dve.tensor_copy(mod_shift[:, :], ps[:, SUMS, 0:KD])
                gain = gain_cols[:, n_gain:n_gain + 1, :] if isinstance(n_gain, int) else gain_cols[:, bass.ds(n_gain, 1), :]
                dve.scalar_tensor_tensor(out=mod_scale[:, :], in0=ps[:, SUMS, KD:2 * KD], scalar=1.0,
                                         in1=flat(gain), op0=ALU.add, op1=ALU.mult).then_inc(mods_ready.sem, 1)

            def ffn(layer, stage, first):
                q, f = q0[stage], ffn_no[stage]
                if first:
                    split_lo(0, layer, q)
                    split_lo(1, layer, q)
                prepare(layer, stage)

                def hid_part(j):
                    dve.wait_ge(hid_hi_done.sem, hid_hi_done.at(layer, f * NJ + j + 1))
                    dve.tensor_tensor(flat(hid_lo[:, :, :]), ps[:, HID, :], flat(hid_hi[:, :, :]).bitcast(F32),
                                      ALU.subtract).then_inc(hid_ready.sem, 1)

                def products(j):
                    for t in range(T):
                        dve.wait_ge(silu_done.sem, silu_done.at(layer, (f * NJ + j) * T + t + 1))
                        dve.tensor_tensor(hidden[:, t, :], silu_g[:, t, :], ps[:, t, FC:2 * FC], ALU.mult)\
                            .then_inc(hidden_done.sem, 1)

                def step(j):
                    hid_part(j - 1)
                    split_lo(0, layer, q + j + 1)
                    products(j)
                    split_lo(1, layer, q + j + 1)
                    split_lo(2, layer, q + j)

                for m in range(3):
                    dve.wait_ge(seeded[m].sem, seeded[m].at(layer, stage + 1))
                split_lo(0, layer, q + 1)
                products(0)
                split_lo(1, layer, q + 1)
                split_lo(2, layer, q)
                add_ada(layer, stage, 0)
                with dve.Fori(1, KD) as j:
                    step(j)
                    add_ada(layer, stage, j)
                with dve.Fori(KD, NJ - 1) as j:
                    step(j)
                hid_part(NJ - 2)
                if stage == FFN1:
                    split_lo(0, layer, q + NJ)
                products(NJ - 1)
                if stage == FFN1:
                    split_lo(1, layer, q + NJ)
                split_lo(2, layer, q + NJ - 1)
                hid_part(NJ - 1)
                take_mods(layer, stage, layer * 3 + (stage + 1))
                residual(layer, stage)

            def mix(layer):
                prepare(layer, MIX)
                split_lo(2, layer, q0[MIX])
                for m in range(3):
                    dve.wait_ge(seeded[m].sem, seeded[m].at(layer, MIX + 1))
                dve.wait_ge(layer_in.sem, layer_in.at(layer, 4))
                chain.link(dve.tensor_scalar(gla_gain_row[:, :], gla_gain_row[:, :], 0.25, None, ALU.mult))

                for what, *arg in PLAN:
                    if what == "split":
                        u = arg[0]
                        split_lo(u % NS, layer, q0[MIX] + u // NS)
                    elif what == "ada":
                        add_ada(layer, MIX, arg[0])
                    elif what == "evac":
                        c, b = arg[0], bank_of(arg[0])
                        if c == C_QB:
                            chunk_done(dve, layer, c)
                            dve.tensor_scalar(flat(qb_t[:, :, :]), flat(ps[:, b:b + 2, :]), DK ** -0.5, None, ALU.mult)\
                                .then_inc(evac_dve.sem, 1)
                        if c < C_R:
                            continue
                        n, o = c - C_R, 512 * ((c - C_R) % 2)
                        cols = (slice(None), slice(None), slice(o, o + 512))
                        dve.wait_ge(tanh_done.sem, tanh_done.at(layer, n + 1))
                        if c < C_GB:
                            dve.scalar_tensor_tensor(out=w_gates[cols], in0=th_buf, scalar=1.0, in1=ps[:, b:b + 2, :],
                                                     op0=ALU.add, op1=ALU.mult).then_inc(th_used.sem, 1)
                        elif c < C_GA:
                            dve.scalar_tensor_tensor(out=w_gates[cols], in0=th_buf, scalar=1.0, in1=w_gates[cols],
                                                     op0=ALU.add, op1=ALU.mult).then_inc(th_used.sem, 1)
                            dve.wait_ge(th_used.sem, th_used.at(layer, n + 1))
                            for t in range(T):
                                part = w_gates[:, t, o:o + 512].rearrange("p (h v) -> p h v", v=DV)
                                last = dve.tensor_tensor(part, part, gla_gain_row[:, :].rearrange("p (a v) -> p a v", a=1)
                                                         .broadcast_to([P, 512 // DV, DV]), ALU.mult)
                            chain.link(last)
                        else:
                            dve.scalar_tensor_tensor(out=xn[cols], in0=th_buf, scalar=1.0, in1=xn[cols],
                                                     op0=ALU.add, op1=ALU.mult).then_inc(th_used.sem, 1)
                            dve.wait_ge(th_used.sem, th_used.at(layer, n + 1))
                            if c == C_GA:
                                chain.link(dve.tensor_tensor(xn[cols], xn[cols], vb[cols], ALU.add))
                            else:
                                for t in range(T):
                                    dve.tensor_tensor(xn[:, t, 512:D], xn[:, t, 512:D], vb[:, t, 512:D], ALU.add)\
                                        .then_inc(merged.sem, 1)
                    elif what == "gate_z":
                        dve.wait_ge(z_mm.sem, z_mm.at(layer, 1))
                        for h in range(GH):
                            last = dve.tensor_scalar(z_buf[:, h, :], ps[:, LIN + h // 2, (h % 2) * SEQ:(h % 2 + 1) * SEQ],
                                                     gate_bias[:, h:h + 1], None, ALU.add)
                        last.then_inc(z_done.sem, 1)
                    elif what == "gate_log":
                        dve.wait_ge(log_done.sem, log_done.at(layer, 1))
                        chain.link(dve.scalar_tensor_tensor(out=flat(z_buf[:, :, :]), in0=flat(z_buf[:, :, :]), scalar=0.0,
                                                            in1=flat(g_cum[:, :, :]), op0=ALU.min, op1=ALU.subtract))
                        for h in range(GH):
                            for t in range(T):
                                tile = (slice(None), h, slice(t * P, (t + 1) * P))
                                last = dve.tensor_tensor_scan(g_cum[tile], ones[:, :], z_buf[tile], 0.0,
                                                              op0=ALU.mult, op1=ALU.add)
                        chain.link(last)
                        dve.tensor_tensor(k_state[:, :, :], g_cum[:, :, P - 1:P].broadcast_to([P, GH, P]),
                                          g_cum[:, :, 0:P], ALU.subtract).then_inc(diffs_done.sem, 1)
                        by_chunk = flat(g_cum[:, :, :]).rearrange("p (c i) -> p c i", i=CH)
                        dve.tensor_tensor(flat(z_buf[:, :, :]).rearrange("p (c i) -> p c i", i=CH), by_chunk,
                                          by_chunk[:, :, 0:1].broadcast_to([P, GH * SEQ // CH, CH]),
                                          ALU.subtract).then_inc(diffs_done.sem, 1)
                    elif what == "gate_exp":
                        dve.wait_ge(exps_done.sem, exps_done.at(layer, 1))
                        dve.wait_ge(evac_act.sem, evac_act.at(layer, C_KB + 1))
                        dve.tensor_tensor(k_state[:, :, :], k_state[:, :, :], kb_t[:, :, 0:P], ALU.mult)\
                            .then_inc(k_state_done.sem, 1)
                    elif what == "q_exp":
                        dve.wait_ge(exps_done.sem, exps_done.at(layer, 2))
                        dve.wait_ge(evac_dve.sem, evac_dve.at(layer, 1))
                        chain.link(dve.tensor_tensor(q_state[:, :, :], q_state[:, :, :], qb_t[:, :, P:2 * P], ALU.mult))
                        dve.wait_ge(exps_done.sem, exps_done.at(layer, 3))
                        dve.tensor_tensor(flat(qb_t[:, :, :]), flat(qb_t[:, :, :]), flat(z_buf[:, :, :]), ALU.mult)\
                            .then_inc(q_ready.sem, 1)
                    elif what == "ks_diff":
                        r = arg[0]
                        t, hp = r // 2, 2 * (r % 2)
                        if r:
                            dve.wait_ge(a_mm.sem, a_mm.at(layer, r))
                        for c in range(NC):
                            n = CH * (c + 1)
                            at = t * P + c * CH
                            last = dve.tensor_tensor(k_scaled[:, :, c, 0:n],
                                                     g_cum[:, hp:hp + 2, at:at + 1].broadcast_to([P, 2, n]),
                                                     g_cum[:, hp:hp + 2, t * P:t * P + n], ALU.subtract)
                        last.then_inc(ks_diff.sem, 1)
                    elif what == "ks_mul":
                        r = arg[0]
                        t, hp = r // 2, 2 * (r % 2)
                        dve.wait_ge(ks_exp.sem, ks_exp.at(layer, r + 1))
                        for c in range(NC):
                            n = CH * (c + 1)
                            last = dve.tensor_tensor(k_scaled[:, :, c, 0:n], k_scaled[:, :, c, 0:n],
                                                     kb_t[:, hp:hp + 2, t * P:t * P + n], ALU.mult)
                        last.then_inc(ks_ready.sem, 1)
                    elif what == "a":
                        r = arg[0]
                        hp = 2 * (r % 2)
                        dve.wait_ge(a_mm.sem, a_mm.at(layer, r + 1))
                        if r >= 2:
                            dve.wait_ge(o_mm.sem, o_mm.at(layer, r - 1))
                        dve.tensor_tensor(a_t[:, hp:hp + 2, :], ps[:, LIN, 0:2 * P].rearrange("p (h i) -> p h i", h=2),
                                          gla_mask[:, :].rearrange("p (a i) -> p a i", a=1).broadcast_to([P, 2, P]),
                                          ALU.mult).then_inc(a_ready.sem, 1)
                    elif what == "lin_norm":
                        dve.wait_ge(lin_squared.sem, lin_squared.at(layer, 4))
                        chain.link(rsqrt(gla_rstd[:, :], gla_nt[:, 0, :], gla_nt[:, 1, :], gla_ss[:, :], DV))
                        for t in range(T):
                            for h in range(GH):
                                o, w = (b[:, t, h * DV:(h + 1) * DV] for b in (vb, w_gates))
                                last = dve.scalar_tensor_tensor(out=o, in0=o, scalar=gla_rstd[:, t * GH + h:t * GH + h + 1],
                                                                in1=w, op0=ALU.mult, op1=ALU.mult)
                        chain.link(last)
                    elif what == "head" and arg[0] < HEADS:
                        i = arg[0]
                        p, h = probs[i % 2], HEAD_ORDER[i]
                        dve.wait_ge(scores_mm.sem, scores_mm.at(layer, i + 1))
                        if i >= 2:
                            dve.wait_ge(turned.sem, turned.at(layer, i - 1))
                        dve.scalar_tensor_tensor(out=p[:, :], in0=ps[:, SCORES, 0:3 * P], scalar=DH ** -0.5,
                                                 in1=att_mask[:, :], op0=ALU.mult, op1=ALU.add)\
                            .then_inc(scores_read.sem, 1)
                        dve.wait_ge(scores_read.sem, scores_read.at(layer, i + 1))
                        dve.tensor_reduce(row_max[:, 0:1], p[:, 0:2 * P], AX_X, ALU.max)
                        chain.link(dve.tensor_reduce(row_max[:, 1:2], p[:, 2 * P:3 * P], AX_X, ALU.max))
                        dve.tensor_scalar(neg_max[:, h, :], row_max[:, :], sink_rows[:, h:h + 1], -1.0, ALU.max, ALU.mult)\
                            .then_inc(soft_ready.sem, 1)
                    elif what == "att_norm":
                        both = sink_rows[:, :].rearrange("p (h a) -> p h a", a=1).broadcast_to([P, HEADS, 2])
                        dve.wait_ge(soft_ready.sem, soft_ready.at(layer, HEADS))
                        dve.tensor_tensor(sink_exp[:, :, :], neg_max[:, :, :], both, ALU.add).then_inc(sink_diff.sem, 1)
                        dve.wait_ge(sink_exp_done.sem, sink_exp_done.at(layer, 1))
                        chain.link(dve.tensor_tensor(flat(row_sum[:, :, :]), flat(row_sum[:, :, :]),
                                                     flat(sink_exp[:, :, :]), ALU.add))
                        chain.link(dve.reciprocal(flat(sink_exp[:, :, :]), flat(row_sum[:, :, :])))
                        chain.link(dve.tensor_scalar(flat(sink_exp[:, :, :]), flat(sink_exp[:, :, :]), 0.5, None, ALU.mult))
                        dve.wait_ge(att_out.sem, att_out.at(layer, HEADS))
                        for t in range(T):
                            y = xn[:, t, :].rearrange("p (h d) -> p h d", d=DH)
                            inv = sink_exp[:, :, 1 - t:2 - t].broadcast_to([P, HEADS, DH])
                            last = dve.tensor_tensor(y, y, inv, ALU.mult)
                        chain.link(last)
                for t in range(T):
                    dve.wait_ge(mrg_hi_done.sem, mrg_hi_done.at(layer, t + 1))
                    part = (slice(None), slice(None), slice(t * P, (t + 1) * P))
                    dve.tensor_tensor(h_lo[part], ps[:, 2 * t:2 * t + 2, :].rearrange("p b (k i) -> p (b k) i", i=P),
                                      h_hi[part].bitcast(F32), ALU.subtract).then_inc(mrg_ready.sem, 1)
                for u in range(2 * N_CHUNK, MIX_UNITS - 1):
                    split_lo(u % NS, layer, q0[MIX] + (u + NS) // NS)
                take_mods(layer, MIX, layer * 3 + 2)
                residual(layer, MIX)

            for s in range(NS):
                dve.nop().then_inc(lo_done[s].sem, 1)
            dve.nop().then_inc(ada_used.sem, 1)
            dve.wait_ge(const_in.sem, CONSTS * 16)
            for t in range(T):
                dve.nop().then_inc(x_ready.sem, 1)
            dve.wait_ge(cond_ready.sem, 1)
            for m in range(3):
                dve.wait_ge(seeded[m].sem, seeded[m].at(0, 0))
            for k in range(KD):
                dve.wait_ge(stage_in[k].sem, 16)
                if k:
                    dve.wait_ge(stage_used.sem, k)
                for m in (1, 2):
                    last = dve.scalar_tensor_tensor(out=ada_acc[:, m, :], in0=ada_stage[k][:, (m - 1) * D:m * D],
                                                    scalar=cond[:, k:k + 1], in1=ada_acc[:, m, :],
                                                    op0=ALU.mult, op1=ALU.add)
                last.then_inc(stage_used.sem, 1)
            take_mods(0, -1, 0)
            dve.wait_ge(made.sem, MADE)
            with dve.Fori(0, L) as layer:
                chain.enter(layer)
                ffn(layer, FFN1, True)
                mix(layer)
                ffn(layer, FFN2, False)
            chain.leave()
            norm(L, 0)
            dve.wait_ge(const_in.sem, (CONSTS + 1) * 16)
            for t in range(T):
                dve.wait_ge(normed.sem, normed.at(L, t + 1))
                dve.tensor_tensor(xn[:, t, :], xn[:, t, :], gate_row[:, :], ALU.mult).then_inc(final_done.sem, 1)

        @block.tensor
        def _(pe):
            def product(o, lhs, rhs, start, stop, shared=False):
                for n, (a, b) in enumerate(((0, 0), (1, 0), (0, 1))):
                    last = pe.matmul(o, lhs[a], rhs[b], start=start and n == 0, stop=stop and n == 2,
                                     skip_group_check=shared)
                return last

            def unit_ready(s, layer, q):
                pe.wait_ge(lo_done[s].sem, lo_done[s].at(layer, q + 1))

            def prepare(layer, n):
                for t in range(T):
                    pe.wait_ge(normed.sem, normed.at(layer, n * T + t + 1))
                    for k in range(KD):
                        last = pe.transpose(ps[:, 2 * t + k // 4, (k % 4) * P:(k % 4 + 1) * P],
                                            xn[:, t, k * P:(k + 1) * P], ident[:, :])
                    last.then_inc(x_tr.sem, 1)

            def h_tile(k, t):
                return [part[:, k, t * P:(t + 1) * P] for part in (h_hi, h_lo)]

            def w_cols(s, a, b):
                return [part[s][:, a:b] for part in (w_hi, w_lo)]

            def down(s, layer, q, parts, k0, start, stop, last_of_stage=False):
                unit_ready(s, layer, q)
                for t in range(T):
                    for k in range(2):
                        for n in range(2):
                            last = product(ps[:, Y + 2 * t + n, :], [a[:, k0 + k, t * P:(t + 1) * P] for a in parts],
                                           w_cols(s, (2 * k + n) * 512, (2 * k + n + 1) * 512),
                                           start=start and k == 0, stop=stop and k == 1)
                    if last_of_stage and t == 0:
                        last.then_inc(y0_done.sem, 1)
                last.then_inc(used[s].sem, 1)

            def sum_gate(layer, stage, half):
                if half:
                    pe.wait_ge(gate_row_done.sem, gate_row_done.at(layer, 2 * stage + 1))
                else:
                    pe.wait_ge(ada_used.sem, ada_used.at(layer, (stage + 1) * KD))
                pe.matmul(ps[:, SUMS, :], ones[:, :], ada_acc[:, 0, half * 512:(half + 1) * 512], start=True, stop=True)\
                    .then_inc(gate_sum.sem, 1)

            def sum_cols():
                for m in (1, 2):
                    for k in range(KD):
                        last = pe.matmul(ps[:, SUMS, (m - 1) * KD + k:(m - 1) * KD + k + 1],
                                         ada_acc[:, m, k * P:(k + 1) * P], ones[:, 0:1], start=True, stop=True)
                last.then_inc(cols_sum.sem, 1)

            def ffn(layer, stage):
                q, f = q0[stage], ffn_no[stage]
                prepare(layer, stage)

                def up(j, half, first=False):
                    unit_ready(half, layer, q + j)
                    for t in range(T):
                        if half == 0 and first:
                            pe.wait_ge(h_ready.sem, h_ready.at(layer, stage * T + t + 1))
                        elif half == 0:
                            pe.wait_ge(hidden_done.sem, hidden_done.at(layer, (f * NJ + j) * T + t + 1 - T))
                        for k in range(KA):
                            last = product(ps[:, t, :], h_tile(half * KA + k, t), w_cols(half, k * 512, (k + 1) * 512),
                                           start=half == 0 and k == 0, stop=half == 1 and k == KA - 1)
                        if half == 1 and t == 0:
                            last.then_inc(gu0_done.sem, 1)
                    last.then_inc(used[half].sem, 1)

                def turn(j):
                    pe.wait_ge(hidden_done.sem, hidden_done.at(layer, (f * NJ + j + 1) * T))
                    for t in range(T):
                        for k in range(2):
                            last = pe.transpose(ps[:, HID, k * SEQ + t * P:k * SEQ + (t + 1) * P],
                                                hidden[:, t, k * P:(k + 1) * P], ident[:, :])
                    last.then_inc(hid_tr.sem, 1)

                def down_j(j, start, stop):
                    pe.wait_ge(hid_ready.sem, hid_ready.at(layer, f * NJ + j + 1))
                    down(2, layer, q + j, (hid_hi, hid_lo), 0, start, stop, last_of_stage=stop)

                up(0, 0, first=True)
                up(0, 1)
                up(1, 0)
                turn(0)
                up(1, 1)
                down_j(0, True, False)
                with pe.Fori(2, NJ - 1) as j:
                    up(j, 0)
                    turn(j - 1)
                    up(j, 1)
                    down_j(j - 1, False, False)
                up(NJ - 1, 0)
                sum_gate(layer, stage, 0)
                turn(NJ - 2)
                up(NJ - 1, 1)
                sum_gate(layer, stage, 1)
                down_j(NJ - 2, False, False)
                pe.wait_ge(gate_row_done.sem, gate_row_done.at(layer, 2 * stage + 2))
                sum_cols()
                turn(NJ - 1)
                down_j(NJ - 1, False, True)

            def evacuated(layer, c):
                if c == C_QB:
                    pe.wait_ge(evac_dve.sem, evac_dve.at(layer, 1))
                elif c < C_R:
                    pe.wait_ge(evac_act.sem, evac_act.at(layer, c + 1))
                elif c < C_GB:
                    pe.wait_ge(th_used.sem, th_used.at(layer, c - C_R + 1))
                else:
                    pe.wait_ge(tanh_done.sem, tanh_done.at(layer, c - C_R + 1))

            def unit(layer, u):
                c, half, s, b = u // 2, u % 2, u % NS, bank_of(u // 2)
                unit_ready(s, layer, q0[MIX] + u // NS)
                if half == 0 and c >= 2:
                    evacuated(layer, c - 2)
                first, last_k = half == 0, KA - 1
                if c == C_LKV:
                    for n, (o, a) in enumerate(((ps[:, 0, 0:SEQ], 0), (ps[:, 0, SEQ:2 * SEQ], RANK))):
                        for k in range(KA):
                            product(o, w_cols(s, k * QKV0 + a, k * QKV0 + a + P),
                                    [part[:, half * KA + k, :] for part in (h_hi, h_lo)],
                                    start=first and k == 0 and n == 0, stop=half == 1 and k == last_k, shared=True)
                    for t in range(T):
                        for k in range(KA):
                            last = product(ps[:, 1, t * P:(t + 1) * P], h_tile(half * KA + k, t),
                                           w_cols(s, k * QKV0 + RANK + P, (k + 1) * QKV0),
                                           start=first and k == 0 and t == 0, stop=half == 1 and k == last_k, shared=True)
                elif c in TRANSPOSED:
                    for g in range(4):
                        for k in range(KA):
                            last = product(ps[:, b + g // 2, (g % 2) * SEQ:(g % 2 + 1) * SEQ],
                                           w_cols(s, k * 512 + g * P, k * 512 + (g + 1) * P),
                                           [part[:, half * KA + k, :] for part in (h_hi, h_lo)],
                                           start=first and k == 0 and g % 2 == 0, stop=half == 1 and k == last_k,
                                           shared=True)
                else:
                    for t in range(T):
                        for k in range(KA):
                            last = product(ps[:, b + t, :], h_tile(half * KA + k, t), w_cols(s, k * 512, (k + 1) * 512),
                                           start=first and k == 0, stop=half == 1 and k == last_k)
                last.then_inc(used[s].sem, 1)

            def head(layer, i):
                if i < HEADS:
                    h = HEAD_ORDER[i]
                    pe.wait_ge(evac_act.sem, evac_act.at(layer, C_Q + 1 + h % GROUP // 4))
                    if i >= 1:
                        pe.wait_ge(scores_read.sem, scores_read.at(layer, i))
                    rows, g = slice((h // GROUP) * DH, (h // GROUP + 1) * DH), h % GROUP
                    pe.matmul(ps[:, SCORES, 0:SEQ], q_t[rows, g, P:2 * P], k_t[rows, 0:SEQ], start=True, stop=True)
                    pe.matmul(ps[:, SCORES, SEQ:SEQ + P], q_t[rows, g, 0:P], k_t[rows, 0:P], start=True, stop=True)\
                        .then_inc(scores_mm.sem, 1)
                if i >= 2:
                    n = i - 2
                    p, v0 = probs_t[n % 2], (HEAD_ORDER[n] // GROUP) * DH
                    pe.wait_ge(probs_t_done.sem, probs_t_done.at(layer, n + 1))
                    if n >= 1:
                        pe.wait_ge(att_out.sem, att_out.at(layer, n))
                    o = [ps[:, TURNED, 3 * P + t * DH:3 * P + (t + 1) * DH] for t in range(T)]
                    pe.matmul(o[0], p[:, 2 * P:3 * P], v_att[:, 0, v0:v0 + DH], start=True, stop=True)
                    pe.matmul(o[1], p[:, 0:P], v_att[:, 0, v0:v0 + DH], start=True, stop=False)
                    last = pe.matmul(o[1], p[:, P:2 * P], v_att[:, 1, v0:v0 + DH], start=False, stop=True)
                if 1 <= i <= HEADS:
                    pe.wait_ge(probs_done.sem, probs_done.at(layer, i))
                    if i >= 2:
                        pe.wait_ge(probs_t_done.sem, probs_t_done.at(layer, i - 1))
                    for n in range(3):
                        last = pe.transpose(ps[:, TURNED, n * P:(n + 1) * P], probs[(i - 1) % 2][:, n * P:(n + 1) * P],
                                            ident[:, :])
                if i >= 1:
                    last.then_inc(turned.sem, 1)

            def mix(layer):
                prepare(layer, MIX)
                pe.wait_ge(h_ready.sem, h_ready.at(layer, (MIX + 1) * T))
                for what, *arg in PLAN:
                    if what == "unit":
                        unit(layer, arg[0])
                    elif what == "gate_z":
                        pe.wait_ge(evac_act.sem, evac_act.at(layer, 1))
                        pe.wait_ge(layer_in.sem, layer_in.at(layer, 4))
                        for h in range(GH):
                            last = pe.matmul(ps[:, LIN + h // 2, (h % 2) * SEQ:(h % 2 + 1) * SEQ],
                                             gate_weight[:, h * DK:(h + 1) * DK], lr_t[0:RANK], start=True, stop=True)
                        last.then_inc(z_mm.sem, 1)
                    elif what == "k_turn":
                        pe.wait_ge(k_state_done.sem, k_state_done.at(layer, 1))
                        for h in range(GH):
                            last = pe.transpose(ps[:, LIN, h * P:(h + 1) * P], k_state[:, h, :], ident[:, :])
                        last.then_inc(k_state_tr.sem, 1)
                    elif what == "state":
                        pe.wait_ge(k_state_t_done.sem, k_state_t_done.at(layer, 1))
                        pe.wait_ge(evac_act.sem, evac_act.at(layer, C_VB + 2))
                        for h in range(GH):
                            last = pe.matmul(ps[:, LIN + h // 2, (h % 2) * DV:(h % 2 + 1) * DV],
                                             k_state_t[:, h * DK:(h + 1) * DK], vb[:, 0, h * DV:(h + 1) * DV],
                                             start=True, stop=True)
                        last.then_inc(state_mm.sem, 1)
                    elif what == "a":
                        r = arg[0]
                        t, hp = r // 2, 2 * (r % 2)
                        pe.wait_ge(ks_ready.sem, ks_ready.at(layer, r + 1))
                        if r == 0:
                            pe.wait_ge(state_done.sem, state_done.at(layer, 1))
                            pe.wait_ge(q_ready.sem, q_ready.at(layer, 1))
                        else:
                            pe.wait_ge(a_ready.sem, a_ready.at(layer, r))
                        for h in range(2):
                            for c in range(NC):
                                last = pe.matmul(ps[:, LIN, h * P + c * CH:h * P + (c + 1) * CH],
                                                 k_scaled[:, h, c, :],
                                                 qb_t[:, hp + h, t * P + c * CH:t * P + (c + 1) * CH],
                                                 start=True, stop=True)
                        last.then_inc(a_mm.sem, 1)
                    elif what == "o":
                        r = arg[0]
                        t, hp = r // 2, 2 * (r % 2)
                        pe.wait_ge(a_ready.sem, a_ready.at(layer, r + 1))
                        if r:
                            pe.wait_ge(lin_squared.sem, lin_squared.at(layer, r))
                        for h in range(2):
                            o = ps[:, LIN + 1, h * DV:(h + 1) * DV]
                            last = pe.matmul(o, a_t[:, hp + h, :], vb[:, t, (hp + h) * DV:(hp + h + 1) * DV],
                                             start=True, stop=t == 0)
                            if t:
                                last = pe.matmul(o, q_state[:, hp + h, :], state[:, (hp + h) * DV:(hp + h + 1) * DV],
                                                 start=False, stop=True)
                        last.then_inc(o_mm.sem, 1)
                    elif what == "head":
                        head(layer, arg[0])
                for t in range(T):
                    pe.wait_ge(merged.sem, merged.at(layer, t + 1))
                    for k in range(KD):
                        last = pe.transpose(ps[:, 2 * t + k // 4, (k % 4) * P:(k % 4 + 1) * P],
                                            xn[:, t, k * P:(k + 1) * P], ident[:, :])
                    last.then_inc(mrg_tr.sem, 1)
                pe.wait_ge(mrg_ready.sem, mrg_ready.at(layer, T))
                for n in range(KD // 2):
                    u = 2 * N_CHUNK + n
                    down(u % NS, layer, q0[MIX] + u // NS, (h_hi, h_lo), 2 * n, n == 0, n == KD // 2 - 1,
                         last_of_stage=n == KD // 2 - 1)
                    if n < 2:
                        sum_gate(layer, MIX, n)
                    elif n == 2:
                        pe.wait_ge(gate_row_done.sem, gate_row_done.at(layer, 2 * MIX + 2))
                        sum_cols()

            for s in range(NS):
                pe.nop().then_inc(used[s].sem, 1)
            pe.wait_ge(made.sem, MADE)
            pe.wait_ge(stage_used.sem, KD)
            sum_cols()
            with pe.Fori(0, L) as layer:
                ffn(layer, FFN1)
                mix(layer)
                ffn(layer, FFN2)


def kernel(**inputs):
    import numpy as np
    import concourse.bacc as bacc
    from concourse.bass_utils import run_bass_kernel_spmd

    a = {k: np.asarray(v) for k, v in inputs.items()}

    def tiles(w):
        return w.reshape(w.shape[0] // P, P, w.shape[1]).transpose(1, 0, 2)

    stream = np.zeros((NS, L * NSEQ, P, UNIT), np.float32)
    sizes = (HEADS * DH, 2 * DH, 2 * DH, GH * DK, GH * DK, GH * DV, RANK, GH * DV, D, D)
    at = [0]
    for n in sizes:
        at.append(at[-1] + n)
    qa, ka, va, qb, kb, vb, lr, r, ga, gb = (np.arange(s, s + n) for s, n in zip(at, sizes))
    pairs = qa.reshape(2, GROUP, DH).transpose(1, 0, 2).reshape(-1)
    chunks = [np.concatenate([lr, ka, va]), pairs[:512], pairs[512:], vb[:512], vb[512:], kb, qb,
              r[:512], r[512:], gb[:512], gb[512:], ga[:512], ga[512:]]
    for layer in range(L):
        q = layer * NSEQ
        for first, w_in, w_out in ((0, "ffn1_w_in", "ffn1_w_out"), (NJ + MQ, "ffn2_w_in", "ffn2_w_out")):
            up = tiles(a[w_in][layer]).reshape(P, KD, 2, NJ, FC)
            dn = tiles(a[w_out][layer])
            for j in range(NJ):
                both = up[:, :, :, j, :].reshape(P, KD, 2 * FC)
                stream[0, q + first + j] = both[:, :KA].reshape(P, UNIT)
                stream[1, q + first + j] = both[:, KA:].reshape(P, UNIT)
                stream[2, q + first + j] = dn[:, 2 * j:2 * j + 2].reshape(P, UNIT)
        w = tiles(a["mix_w_in"][layer])
        for c, cols in enumerate(chunks):
            for half in range(2):
                u = 2 * c + half
                part = w[:, half * KA:(half + 1) * KA][:, :, cols].reshape(P, -1)
                stream[u % NS, q + NJ + u // NS, :, :part.shape[1]] = part
        w = tiles(a["mix_w_out"][layer])
        for n in range(KD // 2):
            u = 2 * N_CHUNK + n
            stream[u % NS, q + NJ + u // NS] = w[:, 2 * n:2 * n + 2].reshape(P, UNIT)

    ada = [a["ada_w"][layer].reshape(D, 9, D)[:, m] for layer in range(L) for m in range(9)]
    bias = [a["ada_b"][layer].reshape(9, D)[m] for layer in range(L) for m in range(9)]
    nothing = np.zeros((D, D), np.float32)
    ada += [nothing, nothing]
    bias += [nothing[0], nothing[0]]
    ada_first = np.stack([tiles(ada[0]), tiles(ada[1])], axis=2).transpose(1, 0, 2, 3).reshape(KD, P, 2 * D)
    ada_w = np.empty((3 * L, KD, P, 3, D), np.float32)
    ada_bias = np.zeros((3 * L + 1, 3, D), np.float32)
    ada_bias[0, 1:] = bias[:2]
    for g in range(3 * L):
        for m in range(3):
            ada_w[g, :, :, m] = ada[2 + 3 * g + m].reshape(KD, P, D)
            ada_bias[g + 1, m] = bias[2 + 3 * g + m]

    def cols(v):
        return v.reshape(-1, P).T

    gains = [a[n][layer] for layer in range(L) for n in ("norm1", "norm_mix", "norm2")] + [nothing[0]]
    arrays = {
        "x_in": a["x"].reshape(T, P, D).transpose(1, 0, 2),
        "cond_in": cols(a["c"][0]),
        "w_stream": stream,
        "ada_first": ada_first,
        "ada_w": ada_w.reshape(3 * L * KD, P, ADA_W),
        "ada_bias": ada_bias,
        "gains": np.stack([cols(g) for g in gains], axis=1),
        "sinks": np.broadcast_to(a["attn_sinks"][:, None, :], (L, P, HEADS)),
        "gate_w": a["gla_w_gate"],
        "gate_b": np.stack([cols(b) for b in a["gla_b_gate"]]),
        "gla_gain": np.broadcast_to(a["gla_out_norm"][:, None, :], (L, P, DV)),
        "final_gain": np.broadcast_to(a["final_norm"][None, :], (P, D)),
    }
    arrays = {k: np.ascontiguousarray(v) for k, v in arrays.items()}
    nc = bacc.Bacc("TRN2", target_bir_lowering=False, num_devices=1)
    args = [nc.dram_tensor(k, v.shape, mybir.dt.from_np(v.dtype), kind="ExternalInput").ap() for k, v in arrays.items()]
    out = nc.dram_tensor("out", (SEQ, D), F32, kind="ExternalOutput").ap()
    trunk(nc, *args, out)
    r = run_bass_kernel_spmd(nc, [arrays], core_ids=[0])
    return r.results[0]["out"].reshape(1, SEQ, D)
```

```python
from contextlib import ExitStack

import concourse.bass as bass
from concourse import mybir

F32 = mybir.dt.float32
F32R = mybir.dt.float32r
I32 = mybir.dt.int32
ALU = mybir.AluOpType
ACT = mybir.ActivationFunctionType
AX_X = mybir.AxisListType.X

P = 128
L = 2
D = 1024
KD = D // P
SEQ = 256
T = SEQ // P
D_FF = 2816
FC = 256
NJ = D_FF // FC
HEADS, DH, GROUP = 16, 64, 8
GH, DK, DV, RANK = 4, 128, 256, 16
CH = 16
NC = P // CH
EPS = 1e-6
MASKED = -1e30
RSQRT_SEED = float(0x5F3759DF)

UNIT = 2048
KA = 4
QKV0 = RANK + 2 * 128
N_CHUNK = 13
MIX_UNITS = 2 * N_CHUNK + KD // 2
NS = 3
MQ = MIX_UNITS // NS
FFN_UNITS = (NJ, NJ, NJ - 1)
NSEQ = [2 * n + MQ for n in FFN_UNITS]
ADA_W = 3 * D

C_LKV, C_Q, C_VB, C_KB, C_QB, C_R, C_GB, C_GA = 0, 1, 3, 5, 6, 7, 9, 11
TRANSPOSED = (C_KB, C_QB, C_Q, C_Q + 1)


HEAD_ORDER = [0, 1, 2, 3, 8, 9, 10, 11, 4, 5, 6, 7, 12, 13, 14, 15]


ADA_AT = ((0, 0), (2, 2), (4, 5), (7, 8), (10, 11), (13, 14), (16, 17), (19, 20))

SPLIT_FIRST = (3, 20, 21, 22)


def mix_plan():
    steps = {
        2: [("gate_z",)], 3: [("gate_log",)], 11: [("gate_exp",), ("ks_diff", 0)], 12: [("k_turn",), ("ks_mul", 0)],
        13: [("q_exp",), ("state",)], 18: [("lin_rms", 0)],
        22: [("lin_norm", 0), ("lin_rms", 1), ("lin_norm", 1)],
    }
    for r in range(4):
        for at, what in ((14, "a"), (15, "o")):
            steps.setdefault(at + 2 * r, []).append((what, r))
        if r:
            steps.setdefault(12 + 2 * r, []).append(("ks_diff", r))
            steps.setdefault(13 + 2 * r, []).append(("ks_mul", r))
    for i in range(HEADS + 2):
        steps.setdefault(4 + i, []).insert(0, ("head", i))
    steps.setdefault(15, []).append(("att_norm", 0))
    steps[22].insert(0, ("att_norm", 1))
    split_lo = {u: [("split_lo", u + NS - 1)] for u in range(22)}
    split_lo[22] = [("split_lo", 24), ("split_lo", 25)]
    split_lo.update({u: [("split_lo", u + NS)] for u in range(23, 26)})
    plan = []
    for u in range(2 * N_CHUNK):
        plan.append(("unit", u))
        late = u in (11, 13)
        if u == 22:
            plan.append(("split_hi", u + NS))
        if u in SPLIT_FIRST:
            plan += split_lo[u]
        if u % 2 and late:
            plan.append(("evac", u // 2))
        plan += steps.get(u, [])
        if u % 2 and not late:
            plan.append(("evac", u // 2))
        if u not in SPLIT_FIRST and u < 23:
            plan += split_lo[u]
        for k, (two, third) in enumerate(ADA_AT):
            plan += [("ada", k, (0, 1))] * (u == two) + [("ada", k, (2,))] * (u == third)
        if u != 22:
            plan.append(("split_hi", u + NS))
        if u >= 23:
            plan += split_lo[u]
    plan.insert(plan.index(("unit", 2 * N_CHUNK - 1)) + 1, ("merge", 0))
    plan.append(("merge", 1))
    return plan


PLAN = mix_plan()


class Signal:

    def __init__(self, sem, per_layer, before=0, by=1):
        self.sem, self.per_layer, self.before, self.by = sem, per_layer, before, by

    def at(self, layer, n):
        return layer * (self.per_layer * self.by) + (n + self.before) * self.by


class Chain:

    def __init__(self, engine, sem, per_layer):
        self.engine, self.sem, self.per_layer = engine, sem, per_layer
        self.before, self.start, self.n = 0, 0, 0

    def enter(self, layer):
        self.before = self.n
        self.start, self.n = layer * self.per_layer + self.before, 0

    def leave(self):
        assert self.n == self.per_layer, (self.n, self.per_layer)
        self.start, self.n = L * self.per_layer + self.before, 0

    def link(self, ins):
        self.n += 1
        ins.then_inc(self.sem, 1)
        self.engine.wait_ge(self.sem, self.start + self.n)


NEWTON_THREES = (3.0, 12.0, 768.0)
NEWTON_SCALE = 2.0 ** 26

ACT_CHAIN, DVE_CHAIN = 2, 108


def trunk(nc, x_in, cond_in, stream0, stream1, stream2, w_last, ada_first, ada_w, ada_bias, gains, sinks, gate_w, gate_b,
          gla_gain, final_gain, out):
    w_stream = (stream0, stream1, stream2)
    with ExitStack() as ctx:
        def sb(name, shape, dt=F32):
            return ctx.enter_context(nc.sbuf_tensor(name, shape, dt))

        def signal(name, per_layer, before=0, by=1):
            return Signal(ctx.enter_context(nc.semaphore(name)), per_layer, before, by)

        w_raw = [sb(f"w_raw{s}", [P, UNIT]) for s in range(NS)]
        w_hi = [sb(f"w_hi{s}", [P, UNIT], F32R) for s in range(NS)]
        w_lo = [sb(f"w_lo{s}", [P, UNIT], F32R) for s in range(NS)]
        ada_raw = sb("ada_raw", [P, ADA_W])
        ada_acc = sb("ada_acc", [P, 3, D])
        x = sb("x", [P, T, D])
        xn = sb("xn", [P, T, D])
        h_hi = sb("h_hi", [P, KD, SEQ], F32R)
        h_lo = sb("h_lo", [P, KD, SEQ], F32R)
        gate_row = sb("gate_row", [P, D])
        mod_shift = sb("mod_shift", [P, KD])
        mod_scale = sb("mod_scale", [P, KD])
        cond = sb("cond", [P, KD])
        gain_cols = sb("gain_cols", [P, 3 * L + 1, KD])
        ident = sb("ident", [P, P])
        ones = sb("ones", [P, P])
        sum_sq = sb("sum_sq", [P, T])
        rstd = sb("rstd", [P, T])
        newton = sb("newton", [P, 2, 2])
        sink_rows = sb("sink_rows", [P, HEADS])
        gate_weight = sb("gate_weight", [RANK, GH * DK])
        gate_bias = sb("gate_bias", [P, GH])
        gla_gain_row = sb("gla_gain_row", [P, DV])
        att_mask = sb("att_mask", [P, 3 * P])
        gla_mask = sb("gla_mask", [P, P])

        with ExitStack() as ffn_ctx:
            silu_g = ffn_ctx.enter_context(nc.sbuf_tensor("silu_g", [P, T, FC], F32))
            hidden = ffn_ctx.enter_context(nc.sbuf_tensor("hidden", [P, T, FC], F32))
            hid_hi = ffn_ctx.enter_context(nc.sbuf_tensor("hid_hi", [P, 2, SEQ], F32R))
            hid_lo = ffn_ctx.enter_context(nc.sbuf_tensor("hid_lo", [P, 2, SEQ], F32R))
            last_raw = ffn_ctx.enter_context(nc.sbuf_tensor("last_raw", [P, UNIT], F32))
            last_hi = ffn_ctx.enter_context(nc.sbuf_tensor("last_hi", [P, UNIT], F32R))
            last_lo = ffn_ctx.enter_context(nc.sbuf_tensor("last_lo", [P, UNIT], F32R))
        with ExitStack() as first_ctx:
            ada_stage = [first_ctx.enter_context(nc.sbuf_tensor(f"ada_stage{k}", [P, 2 * D], F32)) for k in range(KD)]
            diag = [first_ctx.enter_context(nc.sbuf_tensor(f"diag{t}", [P, P], F32)) for t in range(T)]
        q_t = sb("q_t", [P, HEADS // 2, SEQ])
        k_t = sb("k_t", [P, SEQ])
        v_att = sb("v_att", [P, T, P])
        qb_t = sb("qb_t", [P, GH, SEQ])
        kb_t = sb("kb_t", [P, GH, SEQ])
        vb = sb("vb", [P, T, GH * DV])
        w_gates = sb("w_gates", [P, T, D])
        z_buf = sb("z_buf", [P, GH, SEQ])
        g_cum = sb("g_cum", [P, GH, SEQ])
        q_state = sb("q_state", [P, GH, P])
        k_state = sb("k_state", [P, GH, P])
        k_state_t = sb("k_state_t", [P, GH * DK])
        state = sb("state", [P, GH * DV])
        a_t = sb("a_t", [P, GH, P])
        lr_t = a_t[:, 0:2, :].rearrange("p h i -> p (h i)")
        k_scaled = sb("k_scaled", [P, 2, NC, P])
        probs = [sb(f"probs{i}", [P, 3 * P]) for i in range(2)]
        probs_t = [sb(f"probs_t{i}", [P, 3 * P]) for i in range(2)]
        gla_ss = sb("gla_ss", [P, T * GH])
        gla_nt = sb("gla_nt", [P, 2, T * GH])
        gla_rstd = sb("gla_rstd", [P, T * GH])
        row_max = sb("row_max", [P, 2])
        neg_max = sb("neg_max", [P, HEADS, 2])
        row_sum = sb("row_sum", [P, HEADS, 2])
        sink_exp = sb("sink_exp", [P, HEADS, 2])
        th_buf = z_buf[:, :, :].rearrange("p h s -> p (h s)").rearrange("p (t n) -> p t n", t=T)

        ps = ctx.enter_context(nc.psum_tensor("ps", [P, 8, 512], F32))
        SUMS, HID, Y = 3, 2, 4
        SCORES, TURNED, LIN = 4, 5, 6

        const_in = signal("const_in", 0, by=16)
        stage_in = [signal(f"stage_in{k}", 0, by=16) for k in range(KD)]
        raw_in = [signal(f"raw_in{s}", NSEQ[s], by=16) for s in range(NS)]
        last_in = signal("last_in", 2, by=16)
        ada_in = signal("ada_in", 3 * KD, by=16)
        seeded = [signal(f"seeded{m}", 3, by=16) for m in range(3)]
        layer_in = signal("layer_in", 4, by=16)
        out_sent = signal("out_sent", 0, by=16)
        made = signal("made", 0)
        acc_cleared = signal("acc_cleared", 3)
        keys_cleared = signal("keys_cleared", 0)
        cond_ready = signal("cond_ready", 0)
        hi_done = [signal(f"hi_done{s}", NSEQ[s]) for s in range(NS)]
        last_hi_done = signal("last_hi_done", 2)
        squared = signal("squared", 3 * T)
        h_mod_act = signal("h_mod_act", 3 * T)
        h_hi_done = signal("h_hi_done", 3 * T * 2)
        silu_done = signal("silu_done", 2 * NJ * T)
        hid_hi_done = signal("hid_hi_done", 2 * (NJ + 1))
        gate_row_done = signal("gate_row_done", 6)
        act_chain = ctx.enter_context(nc.semaphore("act_chain"))
        log_done = signal("log_done", 1)
        exps_done = signal("exps_done", 3)
        evac_act = signal("evac_act", 6)
        tanh_done = signal("tanh_done", 6)
        k_state_t_done = signal("k_state_t_done", 1)
        state_done = signal("state_done", 1)
        ks_exp = signal("ks_exp", 4)
        lin_out = signal("lin_out", 4)
        lin_squared = signal("lin_squared", 4)
        probs_done = signal("probs_done", HEADS)
        probs_t_done = signal("probs_t_done", HEADS)
        att_out = signal("att_out", HEADS)
        sink_exp_done = signal("sink_exp_done", 2)
        mrg_hi_done = signal("mrg_hi_done", 2)
        lo_done = [signal(f"lo_done{s}", NSEQ[s], before=1) for s in range(NS)]
        last_lo_done = signal("last_lo_done", 2)
        diag_done = signal("diag_done", 3 * T)
        h_mod_dve = signal("h_mod_dve", 3 * T)
        h_ready = signal("h_ready", 3 * T * 2)
        hidden_done = signal("hidden_done", 2 * NJ * T)
        hid_ready = signal("hid_ready", 2 * (NJ + 1))
        x_ready = signal("x_ready", 3 * T, before=T)
        first_cleared = signal("first_cleared", 0)
        stage_used = signal("stage_used", 0)
        ada_used = signal("ada_used", 3 * KD, before=1)
        mods_ready = signal("mods_ready", 3, before=1)
        dve_chain = ctx.enter_context(nc.semaphore("dve_chain"))
        z_done = signal("z_done", 1)
        diffs_done = signal("diffs_done", 2)
        evac_dve = signal("evac_dve", 1)
        k_state_done = signal("k_state_done", 1)
        q_ready = signal("q_ready", 1)
        ks_diff = signal("ks_diff", 4)
        ks_ready = signal("ks_ready", 4)
        a_ready = signal("a_ready", 4)
        th_used = signal("th_used", 6)
        scores_read = signal("scores_read", HEADS)
        soft_ready = signal("soft_ready", HEADS)
        sink_diff = signal("sink_diff", 2)
        merged = signal("merged", 2)
        mrg_ready = signal("mrg_ready", 2)
        final_done = signal("final_done", 0)
        used = [signal(f"used{s}", NSEQ[s], before=1) for s in range(NS)]
        gu0_done = signal("gu0_done", 2 * NJ)
        hid_tr = signal("hid_tr", 2 * (NJ + 1))
        down_t0 = signal("down_t0", 2)
        last_used = signal("last_used", 2)
        y0_done = signal("y0_done", 3)
        x_tr = signal("x_tr", 3 * T * 2)
        gate_sum = signal("gate_sum", 6)
        cols_sum = signal("cols_sum", 3, before=1)
        z_mm = signal("z_mm", 1)
        k_state_tr = signal("k_state_tr", 1)
        state_mm = signal("state_mm", 1)
        a_mm = signal("a_mm", 4)
        o_mm = signal("o_mm", 4)
        scores_mm = signal("scores_mm", HEADS)
        turned = signal("turned", HEADS + 1)
        mrg_tr = signal("mrg_tr", 2)

        FFN1, MIX, FFN2 = range(3)
        q0 = {FFN1: [0, 0, 0], MIX: list(FFN_UNITS), FFN2: [n + MQ for n in FFN_UNITS]}
        ffn_no = {FFN1: 0, FFN2: 1}
        MADE = 9
        CONSTS = 4

        def bank_of(c):
            return 2 * (c % 2)

        def flat(ap):
            return ap.rearrange("p a b -> p (a b)")

        def chunk_done(engine, layer, c):
            u = 2 * c + 1
            engine.wait_ge(used[u % NS].sem, used[u % NS].at(layer, q0[MIX][u % NS] + u // NS + 1))

        def half_of(buf, t, half):
            return buf[:, half * KA:(half + 1) * KA, t * P:(t + 1) * P]

        def of_heads(ap, b):
            return ap.rearrange("p (a b h) t -> p a b (h t)", a=2, b=2)[:, :, b, :]

        def as_tiles(ap):
            return ap.rearrange("p (k i) -> p k i", i=P)

        block = ctx.enter_context(nc.Block())

        @block.sync
        def _(sp):
            sp.dma_start(cond[:, :], cond_in).then_inc(const_in.sem, 16)
            sp.dma_start(gain_cols[:, :, :], gains).then_inc(const_in.sem, 16)
            sp.dma_start(x[:, :, :], x_in).then_inc(const_in.sem, 16)
            sp.wait_ge(first_cleared.sem, 1)
            sp.dma_start(ada_acc[0:1, 1:3, :], ada_bias[0:1, 1:3, :]).then_inc(const_in.sem, 16)
            for k in range(KD):
                sp.dma_start(ada_stage[k][:, :], ada_first[k]).then_inc(stage_in[k].sem, 16)

            def load(s, layer, q):
                sp.wait_ge(lo_done[s].sem, lo_done[s].at(layer, q))
                sp.dma_start(w_raw[s][:, :], w_stream[s][bass.ds(layer * NSEQ[s] + q, 1)].rearrange("a p n -> p (a n)"))\
                    .then_inc(raw_in[s].sem, 16)

            def load_ada(layer, n):
                sp.wait_ge(ada_used.sem, ada_used.at(layer, n))
                sp.dma_start(ada_raw[:, :], ada_w[bass.ds(layer * (3 * KD) + n, 1)].rearrange("a p n -> p (a n)"))\
                    .then_inc(ada_in.sem, 16)

            def ffn(layer, stage):
                q = q0[stage]
                for s in range(NS):
                    load(s, layer, q[s])
                load(0, layer, q[0] + 1)
                load(1, layer, q[1] + 1)
                load_ada(layer, stage * KD)
                with sp.Fori(1, KD) as j:
                    load(0, layer, q[0] + 1 + j)
                    load(1, layer, q[1] + 1 + j)
                    load(2, layer, q[2] + j)
                    load_ada(layer, stage * KD + j)
                sp.dma_start(last_raw[:, :], w_last[bass.ds(layer * 2 + ffn_no[stage], 1)]
                             .rearrange("a p n -> p (a n)")).then_inc(last_in.sem, 16)
                with sp.Fori(KD, NJ - 1) as j:
                    load(0, layer, q[0] + 1 + j)
                    load(1, layer, q[1] + 1 + j)
                    load(2, layer, q[2] + j)

            with sp.Fori(0, L) as layer:
                ffn(layer, FFN1)
                for dst, src in ((sink_rows, sinks), (gate_weight, gate_w), (gate_bias, gate_b), (gla_gain_row, gla_gain)):
                    sp.dma_start(dst[:, :], src[bass.ds(layer, 1)].rearrange("a p n -> p (a n)"))\
                        .then_inc(layer_in.sem, 16)
                for u in range(2 * NS - 1):
                    load(u % NS, layer, q0[MIX][u % NS] + u // NS)
                load_ada(layer, MIX * KD)
                for what, *arg in PLAN:
                    if what == "split_lo" and arg[0] + NS < MIX_UNITS:
                        u = arg[0] + NS
                        load(u % NS, layer, q0[MIX][u % NS] + u // NS)
                    elif what == "ada" and 2 in arg[1] and arg[0] + 1 < KD:
                        load_ada(layer, MIX * KD + arg[0] + 1)
                ffn(layer, FFN2)

            for s in (0, 1):
                load(s, L, 0)
            sp.wait_ge(x_ready.sem, x_ready.at(L, 0))
            sp.dma_start(gate_row[:, :], final_gain).then_inc(const_in.sem, 16)
            for t in range(T):
                sp.wait_ge(final_done.sem, t + 1)
                sp.dma_start(out[t * P:(t + 1) * P, :], xn[:, t, :]).then_inc(out_sent.sem, 16)
            sp.wait_ge(out_sent.sem, T * 16)

        @block.gpsimd
        def _(pool):
            def seed(n):
                pool.memset(ada_acc[:, :, :], 0.0).then_inc(acc_cleared.sem, 1)
                pool.wait_ge(acc_cleared.sem, n)
                for m in range(3):
                    pool.dma_start(ada_acc[0:1, m, :], ada_bias[n:n + 1, m, :]).then_inc(seeded[m].sem, 16)

            pool.memset(ident[:, :], 0.0).then_inc(made.sem, 1)
            pool.memset(ones[:, :], 1.0).then_inc(made.sem, 1)
            pool.memset(att_mask[:, :], 0.0).then_inc(made.sem, 1)
            pool.memset(gla_mask[:, :], 1.0).then_inc(made.sem, 1)
            pool.wait_ge(made.sem, 4)
            pool.affine_select(out=ident[:, :], in_=ident[:, :], compare_op=ALU.not_equal, fill=1.0, base=0,
                               pattern=[[-1, P]], channel_multiplier=1).then_inc(made.sem, 1)
            pool.affine_select(out=att_mask[:, 0:P], in_=att_mask[:, 0:P], compare_op=ALU.is_gt, fill=MASKED,
                               base=0, pattern=[[1, P]], channel_multiplier=-1).then_inc(made.sem, 1)
            for i in (1, 2):
                pool.affine_select(out=att_mask[:, i * P:(i + 1) * P], in_=att_mask[:, i * P:(i + 1) * P],
                                   compare_op=ALU.is_ge, fill=MASKED, base=0, pattern=[[-1, P]],
                                   channel_multiplier=1).then_inc(made.sem, 1)
            pool.affine_select(out=gla_mask[:, :], in_=gla_mask[:, :], compare_op=ALU.is_ge, fill=0.0, base=0,
                               pattern=[[1, P]], channel_multiplier=-1).then_inc(made.sem, 1)
            pool.wait_ge(stage_used.sem, KD)
            pool.memset(k_scaled[:, :, :, :], 0.0).then_inc(keys_cleared.sem, 1)
            for n in range(3 * L):
                pool.wait_ge(cols_sum.sem, cols_sum.at(0, n))
                seed(n + 1)

        @block.scalar
        def _(act):
            chain = Chain(act, act_chain, ACT_CHAIN)

            def split_hi(s, layer, q):
                act.wait_ge(raw_in[s].sem, raw_in[s].at(layer, q + 1))
                act.wait_ge(used[s].sem, used[s].at(layer, q))
                act.activation(w_hi[s][:, :], w_raw[s][:, :], ACT.Copy).then_inc(hi_done[s].sem, 1)

            def square(layer, n, t):
                act.wait_ge(x_ready.sem, x_ready.at(layer, (n - 1) * T + t + 1))
                act.activation(xn[:, t, :], x[:, t, :], ACT.Square, accum_out=sum_sq[:, t:t + 1])\
                    .then_inc(squared.sem, 1)

            def prepare(layer, n, t):
                act.wait_ge(x_tr.sem, x_tr.at(layer, (n * T + t) * 2 + 2))
                act.wait_ge(mods_ready.sem, mods_ready.at(layer, n))
                for k in range(KA, KD):
                    last = act.activation(xn[:, t, k * P:(k + 1) * P], ps[:, 2 * t + 1, (k - KA) * P:(k - KA + 1) * P],
                                          ACT.Identity, bias=mod_shift[:, k:k + 1], scale=mod_scale[:, k:k + 1])
                last.then_inc(h_mod_act.sem, 1)
                for half, mod in enumerate((h_mod_dve, h_mod_act)):
                    act.wait_ge(mod.sem, mod.at(layer, n * T + t + 1))
                    act.activation(half_of(h_hi, t, half), as_tiles(xn[:, t, half * 512:(half + 1) * 512]), ACT.Copy)\
                        .then_inc(h_hi_done.sem, 1)

            def gate_half(layer, stage, half):
                act.wait_ge(gate_sum.sem, gate_sum.at(layer, 2 * stage + half + 1))
                act.activation(gate_row[:, half * 512:(half + 1) * 512], ps[:, SUMS, :], ACT.Copy,
                               scale=1.0 if stage == MIX else 0.5).then_inc(gate_row_done.sem, 1)

            def ffn(layer, stage):
                q, f = q0[stage], ffn_no[stage]
                def hid_part(j):
                    act.wait_ge(hid_tr.sem, hid_tr.at(layer, f * (NJ + 1) + j + 1))
                    act.wait_ge(used[2].sem, used[2].at(layer, q[2] + j))
                    act.activation(flat(hid_hi[:, :, :]), ps[:, HID, :], ACT.Copy).then_inc(hid_hi_done.sem, 1)

                def last_hid_part(t):
                    act.wait_ge(hid_tr.sem, hid_tr.at(layer, f * (NJ + 1) + NJ + t))
                    if t == 0:
                        act.wait_ge(down_t0.sem, down_t0.at(layer, f + 1))
                    else:
                        act.wait_ge(used[2].sem, used[2].at(layer, q[2] + NJ - 1))
                    act.activation(hid_hi[:, :, t * P:(t + 1) * P],
                                   ps[:, HID, :].rearrange("p (k i) -> p k i", k=2)[:, :, t * P:(t + 1) * P],
                                   ACT.Copy).then_inc(hid_hi_done.sem, 1)

                def silu(j, t, first=False):
                    if t == 0:
                        act.wait_ge(gu0_done.sem, gu0_done.at(layer, f * NJ + j + 1))
                    else:
                        act.wait_ge(used[1].sem, used[1].at(layer, q[1] + j + 1))
                    if not first:
                        act.wait_ge(hidden_done.sem, hidden_done.at(layer, (f * NJ + j) * T + t + 1 - T))
                    act.activation(silu_g[:, t, :], ps[:, t, 0:FC], ACT.Silu).then_inc(silu_done.sem, 1)

                square(layer, stage, 1)
                silu(0, 0, first=True)
                prepare(layer, stage, 1)
                split_hi(0, layer, q[0] + 1)
                silu(0, 1, first=True)
                split_hi(1, layer, q[1] + 1)
                split_hi(2, layer, q[2])
                with act.Fori(1, NJ - 1) as j:
                    hid_part(j - 1)
                    split_hi(0, layer, q[0] + j + 1)
                    for t in range(T):
                        silu(j, t)
                    split_hi(1, layer, q[1] + j + 1)
                    split_hi(2, layer, q[2] + j)
                act.wait_ge(last_in.sem, last_in.at(layer, f + 1))
                act.activation(last_hi[:, :], last_raw[:, :], ACT.Copy).then_inc(last_hi_done.sem, 1)
                gate_half(layer, stage, 0)
                hid_part(NJ - 2)
                split_hi(0, layer, q[0] + NJ)
                for t in range(T):
                    silu(NJ - 1, t)
                split_hi(1, layer, q[1] + NJ)
                last_hid_part(0)
                gate_half(layer, stage, 1)
                square(layer, stage + 1, 0)
                last_hid_part(1)
                if stage == FFN1:
                    split_hi(2, layer, q[2] + NJ - 1)
                prepare(layer, stage + 1, 0)

            def mix(layer):
                square(layer, MIX, 1)
                prepare(layer, MIX, 1)
                for what, *arg in PLAN:
                    if what == "split_hi":
                        u = arg[0]
                        split_hi(u % NS, layer, q0[MIX][u % NS] + u // NS)
                    elif what == "evac":
                        c, b = arg[0], bank_of(arg[0])
                        if c == C_QB:
                            continue
                        chunk_done(act, layer, c)
                        if c == C_LKV:
                            act.activation(lr_t[0:RANK], ps[0:RANK, 0, 0:SEQ], ACT.Copy)
                            act.activation(k_t[:, :], ps[:, 0, SEQ:2 * SEQ], ACT.Copy)
                            act.activation(flat(v_att[:, :, :]), ps[:, 1, 0:SEQ], ACT.Copy).then_inc(evac_act.sem, 1)
                        elif c == C_KB:
                            act.activation(flat(kb_t[:, :, :]), flat(ps[:, b:b + 2, :]), ACT.Copy)\
                                .then_inc(evac_act.sem, 1)
                        elif c in (C_Q, C_Q + 1):
                            g = 4 * (c - C_Q)
                            act.activation(flat(q_t[:, g:g + 4, :]), flat(ps[:, b:b + 2, :]), ACT.Copy)\
                                .then_inc(evac_act.sem, 1)
                        elif c in (C_VB, C_VB + 1):
                            o = 512 * (c - C_VB)
                            act.activation(vb[:, :, o:o + 512], ps[:, b:b + 2, :], ACT.Copy).then_inc(evac_act.sem, 1)
                        else:
                            n = c - C_R
                            if n:
                                act.wait_ge(th_used.sem, th_used.at(layer, n))
                            else:
                                act.wait_ge(q_ready.sem, q_ready.at(layer, 1))
                            act.activation(th_buf, ps[:, b:b + 2, :], ACT.Tanh, scale=0.5).then_inc(tanh_done.sem, 1)
                    elif what == "gate_log":
                        act.wait_ge(z_done.sem, z_done.at(layer, 1))
                        chain.link(act.activation(flat(g_cum[:, :, :]), flat(z_buf[:, :, :]), ACT.Abs))
                        chain.link(act.activation(flat(g_cum[:, :, :]), flat(g_cum[:, :, :]), ACT.Exp, scale=-1.0))
                        act.activation(flat(g_cum[:, :, :]), flat(g_cum[:, :, :]), ACT.Ln, bias=1.0)\
                            .then_inc(log_done.sem, 1)
                    elif what == "gate_exp":
                        act.wait_ge(diffs_done.sem, diffs_done.at(layer, 1))
                        act.activation(k_state[:, :, :], k_state[:, :, :], ACT.Exp, scale=1 / 16.0)\
                            .then_inc(exps_done.sem, 1)
                        act.activation(q_state[:, :, :], g_cum[:, :, P:2 * P], ACT.Exp, scale=1 / 16.0)\
                            .then_inc(exps_done.sem, 1)
                        act.wait_ge(diffs_done.sem, diffs_done.at(layer, 2))
                        act.activation(flat(z_buf[:, :, :]), flat(z_buf[:, :, :]), ACT.Exp, scale=1 / 16.0)\
                            .then_inc(exps_done.sem, 1)
                    elif what == "k_turn":
                        act.wait_ge(k_state_tr.sem, k_state_tr.at(layer, 1))
                        act.activation(k_state_t[:, :], ps[:, LIN, :], ACT.Copy).then_inc(k_state_t_done.sem, 1)
                    elif what == "state":
                        act.wait_ge(state_mm.sem, state_mm.at(layer, 1))
                        act.activation(state[:, :], flat(ps[:, LIN:LIN + 2, :]), ACT.Copy).then_inc(state_done.sem, 1)
                    elif what == "ks_diff":
                        act.wait_ge(ks_diff.sem, ks_diff.at(layer, arg[0] + 1))
                        for c in range(NC):
                            part = k_scaled[:, :, c, 0:CH * (c + 1)]
                            last = act.activation(part, part, ACT.Exp, scale=1 / 16.0)
                        last.then_inc(ks_exp.sem, 1)
                    elif what == "o":
                        r = arg[0]
                        t, hp = r // 2, 2 * (r % 2)
                        act.wait_ge(o_mm.sem, o_mm.at(layer, r + 1))
                        act.activation(vb[:, t, hp * DV:(hp + 2) * DV], ps[:, LIN + 1, :], ACT.Copy)\
                            .then_inc(lin_out.sem, 1)
                        act.wait_ge(lin_out.sem, lin_out.at(layer, r + 1))
                        for h in range(2):
                            o = ps[:, LIN + 1, h * DV:(h + 1) * DV]
                            n = t * GH + hp + h
                            last = act.activation(o, o, ACT.Square, accum_out=gla_ss[:, n:n + 1])
                        last.then_inc(lin_squared.sem, 1)
                    elif what == "head":
                        i = arg[0]
                        if i < HEADS:
                            p, h = probs[i % 2], HEAD_ORDER[i]
                            act.wait_ge(soft_ready.sem, soft_ready.at(layer, i + 1))
                            act.activation(p[:, 0:2 * P], p[:, 0:2 * P], ACT.Exp, bias=neg_max[:, h, 0:1],
                                           accum_out=row_sum[:, h, 0:1])
                            act.activation(p[:, 2 * P:3 * P], p[:, 2 * P:3 * P], ACT.Exp, bias=neg_max[:, h, 1:2],
                                           accum_out=row_sum[:, h, 1:2]).then_inc(probs_done.sem, 1)
                        if 2 <= i:
                            h = HEAD_ORDER[i - 2]
                            act.wait_ge(turned.sem, turned.at(layer, i))
                            act.activation(xn[:, :, h * DH:(h + 1) * DH],
                                           ps[:, TURNED, 3 * P:4 * P].rearrange("p (t d) -> p t d", t=T),
                                           ACT.Copy).then_inc(att_out.sem, 1)
                        if 1 <= i <= HEADS:
                            act.wait_ge(turned.sem, turned.at(layer, i))
                            act.activation(probs_t[(i - 1) % 2][:, :], ps[:, TURNED, 0:3 * P], ACT.Copy)\
                                .then_inc(probs_t_done.sem, 1)
                    elif what == "att_norm":
                        act.wait_ge(sink_diff.sem, sink_diff.at(layer, arg[0] + 1))
                        part = of_heads(sink_exp[:, :, :], arg[0])
                        act.activation(part, part, ACT.Exp)\
                            .then_inc(sink_exp_done.sem, 1)
                    elif what == "merge":
                        half = arg[0]
                        act.wait_ge(mrg_tr.sem, mrg_tr.at(layer, half + 1))
                        for t in range(T):
                            last = act.activation(half_of(h_hi, t, half), as_tiles(ps[:, 2 - 2 * half + t, :]), ACT.Copy)
                        last.then_inc(mrg_hi_done.sem, 1)
                split_hi(2, layer, q0[MIX][2] + MQ - 1)
                gate_half(layer, MIX, 0)
                split_hi(0, layer, q0[FFN2][0])
                gate_half(layer, MIX, 1)
                square(layer, FFN2, 0)
                split_hi(1, layer, q0[FFN2][1])
                prepare(layer, FFN2, 0)

            act.wait_ge(const_in.sem, CONSTS * 16)
            act.activation(cond[:, :], cond[:, :], ACT.Silu).then_inc(cond_ready.sem, 1)
            square(0, 0, 0)
            split_hi(0, 0, 0)
            prepare(0, 0, 0)
            split_hi(1, 0, 0)
            with act.Fori(0, L) as layer:
                chain.enter(layer)
                ffn(layer, FFN1)
                mix(layer)
                ffn(layer, FFN2)
            chain.leave()
            square(L, 0, 1)

        @block.vector
        def _(dve):
            chain = Chain(dve, dve_chain, DVE_CHAIN)

            def split_lo(s, layer, q):
                dve.wait_ge(hi_done[s].sem, hi_done[s].at(layer, q + 1))
                dve.tensor_tensor(w_lo[s][:, :], w_raw[s][:, :], w_hi[s][:, :].bitcast(F32), ALU.subtract)\
                    .then_inc(lo_done[s].sem, 1)

            def rsqrt(y, v, tmp, sums, width):
                chain.link(dve.tensor_scalar(v, sums, 1.0 / width, EPS, ALU.mult, ALU.add))
                chain.link(dve.tensor_scalar(y.bitcast(I32), v.bitcast(I32), -0.5, RSQRT_SEED, ALU.mult, ALU.add))
                for n in range(3):
                    chain.link(dve.scalar_tensor_tensor(out=tmp, in0=y, scalar=-0.5, in1=y, op0=ALU.mult, op1=ALU.mult))
                    chain.link(dve.tensor_tensor(tmp, tmp, v, ALU.mult))
                    last = dve.scalar_tensor_tensor(out=y, in0=tmp, scalar=1.5, in1=y, op0=ALU.add, op1=ALU.mult)
                    if n < 2:
                        chain.link(last)
                return last

            def norm(layer, n, t):
                v, y = newton[:, 0, t:t + 1], rstd[:, t:t + 1]
                r = newton[:, 1, t:t + 1]
                dve.wait_ge(squared.sem, squared.at(layer, n * T + t + 1))
                chain.link(dve.tensor_scalar(v, sum_sq[:, t:t + 1], NEWTON_SCALE / D, NEWTON_SCALE * EPS,
                                             ALU.mult, ALU.add))
                chain.link(dve.tensor_scalar(y.bitcast(I32), v.bitcast(I32), -0.5, RSQRT_SEED - 2.0 ** 31,
                                             ALU.mult, ALU.add))
                for three in NEWTON_THREES:
                    chain.link(dve.scalar_tensor_tensor(out=r, in0=y, scalar=y, in1=v, op0=ALU.mult, op1=ALU.mult))
                    chain.link(dve.scalar_tensor_tensor(out=y, in0=r, scalar=three, in1=y, op0=ALU.subtract,
                                                        op1=ALU.mult))

            def norm_diag(layer, n, t):
                norm(layer, n, t)
                dve.tensor_scalar(diag[t][:, :], ident[:, :], rstd[:, t:t + 1], None, ALU.mult)\
                    .then_inc(diag_done.sem, 1)

            def prepare(layer, n, t):
                dve.wait_ge(mods_ready.sem, mods_ready.at(layer, n))
                dve.wait_ge(x_tr.sem, x_tr.at(layer, (n * T + t) * 2 + 1))
                for k in range(KA):
                    last = dve.tensor_scalar(xn[:, t, k * P:(k + 1) * P], ps[:, 2 * t, k * P:(k + 1) * P],
                                             mod_scale[:, k:k + 1], mod_shift[:, k:k + 1], ALU.mult, ALU.add)
                last.then_inc(h_mod_dve.sem, 1)
                for half in range(2):
                    dve.wait_ge(h_hi_done.sem, h_hi_done.at(layer, (n * T + t) * 2 + half + 1))
                    dve.tensor_tensor(half_of(h_lo, t, half), as_tiles(xn[:, t, half * 512:(half + 1) * 512]),
                                      half_of(h_hi, t, half).bitcast(F32), ALU.subtract).then_inc(h_ready.sem, 1)

            def residual(layer, stage, t):
                if t == 0:
                    dve.wait_ge(gate_row_done.sem, gate_row_done.at(layer, 2 * stage + 2))
                    dve.wait_ge(y0_done.sem, y0_done.at(layer, stage + 1))
                elif stage == MIX:
                    dve.wait_ge(used[2].sem, used[2].at(layer, q0[MIX][2] + MQ))
                else:
                    dve.wait_ge(last_used.sem, last_used.at(layer, ffn_no[stage] + 1))
                chain.link(dve.tensor_tensor(xn[:, t, :], flat(ps[:, Y + 2 * t:Y + 2 * t + 2, :]), gate_row[:, :],
                                             ALU.mult))
                dve.tensor_tensor(x[:, t, :], x[:, t, :], xn[:, t, :], ALU.add).then_inc(x_ready.sem, 1)

            def next_stage(layer, stage):
                take_mods(layer, stage, layer * 3 + (stage + 1))
                prepare(layer, stage + 1, 0)
                residual(layer, stage, 1)

            def add_ada(layer, stage, k, vectors=(0, 1, 2)):
                n = stage * KD + k
                dve.wait_ge(ada_in.sem, ada_in.at(layer, n + 1))
                dve.wait_ge(ada_used.sem, ada_used.at(layer, n))
                col = cond[:, k:k + 1] if isinstance(k, int) else cond[:, bass.ds(k, 1)]
                for m in vectors:
                    last = dve.scalar_tensor_tensor(out=ada_acc[:, m, :], in0=ada_raw[:, m * D:(m + 1) * D], scalar=col,
                                                    in1=ada_acc[:, m, :], op0=ALU.mult, op1=ALU.add)
                if 2 in vectors:
                    last.then_inc(ada_used.sem, 1)

            def take_mods(layer, stage, n_gain):
                dve.wait_ge(cols_sum.sem, cols_sum.at(layer, stage + 1))
                dve.tensor_copy(mod_shift[:, :], ps[:, SUMS, 0:KD])
                gain = gain_cols[:, n_gain:n_gain + 1, :] if isinstance(n_gain, int) else gain_cols[:, bass.ds(n_gain, 1), :]
                dve.scalar_tensor_tensor(out=mod_scale[:, :], in0=ps[:, SUMS, KD:2 * KD], scalar=1.0,
                                         in1=flat(gain), op0=ALU.add, op1=ALU.mult).then_inc(mods_ready.sem, 1)

            def ffn(layer, stage):
                q, f = q0[stage], ffn_no[stage]
                def hid_part(j):
                    dve.wait_ge(hid_hi_done.sem, hid_hi_done.at(layer, f * (NJ + 1) + j + 1))
                    dve.tensor_tensor(flat(hid_lo[:, :, :]), ps[:, HID, :], flat(hid_hi[:, :, :]).bitcast(F32),
                                      ALU.subtract).then_inc(hid_ready.sem, 1)

                def last_hid_part(t):
                    dve.wait_ge(hid_hi_done.sem, hid_hi_done.at(layer, f * (NJ + 1) + NJ + t))
                    rows = (slice(None), slice(None), slice(t * P, (t + 1) * P))
                    dve.tensor_tensor(hid_lo[rows], ps[:, HID, :].rearrange("p (k i) -> p k i", k=2)[rows],
                                      hid_hi[rows].bitcast(F32), ALU.subtract).then_inc(hid_ready.sem, 1)

                def gated(j, t):
                    dve.wait_ge(silu_done.sem, silu_done.at(layer, (f * NJ + j) * T + t + 1))
                    dve.tensor_tensor(hidden[:, t, :], silu_g[:, t, :], ps[:, t, FC:2 * FC], ALU.mult)\
                        .then_inc(hidden_done.sem, 1)

                def step(j):
                    hid_part(j - 1)
                    split_lo(0, layer, q[0] + j + 1)
                    for t in range(T):
                        gated(j, t)
                    split_lo(1, layer, q[1] + j + 1)
                    split_lo(2, layer, q[2] + j)

                norm_diag(layer, stage, 1)
                gated(0, 0)
                prepare(layer, stage, 1)
                for m in range(3):
                    dve.wait_ge(seeded[m].sem, seeded[m].at(layer, stage + 1))
                split_lo(0, layer, q[0] + 1)
                gated(0, 1)
                split_lo(1, layer, q[1] + 1)
                split_lo(2, layer, q[2])
                add_ada(layer, stage, 0)
                with dve.Fori(1, KD) as j:
                    step(j)
                    add_ada(layer, stage, j)
                with dve.Fori(KD, NJ - 1) as j:
                    step(j)
                dve.wait_ge(last_hi_done.sem, last_hi_done.at(layer, f + 1))
                dve.tensor_tensor(last_lo[:, :], last_raw[:, :], last_hi[:, :].bitcast(F32), ALU.subtract)\
                    .then_inc(last_lo_done.sem, 1)
                hid_part(NJ - 2)
                split_lo(0, layer, q[0] + NJ)
                for t in range(T):
                    gated(NJ - 1, t)
                last_hid_part(0)
                split_lo(1, layer, q[1] + NJ)
                residual(layer, stage, 0)
                norm_diag(layer, stage + 1, 0)
                last_hid_part(1)
                next_stage(layer, stage)

            def mix(layer):
                norm_diag(layer, MIX, 1)
                prepare(layer, MIX, 1)
                for m in range(3):
                    dve.wait_ge(seeded[m].sem, seeded[m].at(layer, MIX + 1))
                dve.wait_ge(layer_in.sem, layer_in.at(layer, 4))
                chain.link(dve.tensor_scalar(gla_gain_row[:, :], gla_gain_row[:, :], 0.25, None, ALU.mult))

                for what, *arg in PLAN:
                    if what == "split_lo":
                        u = arg[0]
                        split_lo(u % NS, layer, q0[MIX][u % NS] + u // NS)
                    elif what == "ada":
                        add_ada(layer, MIX, *arg)
                    elif what == "evac":
                        c, b = arg[0], bank_of(arg[0])
                        if c == C_QB:
                            chunk_done(dve, layer, c)
                            dve.tensor_scalar(flat(qb_t[:, :, :]), flat(ps[:, b:b + 2, :]), DK ** -0.5, None, ALU.mult)\
                                .then_inc(evac_dve.sem, 1)
                        if c < C_R:
                            continue
                        n, o = c - C_R, 512 * ((c - C_R) % 2)
                        cols = (slice(None), slice(None), slice(o, o + 512))
                        dve.wait_ge(tanh_done.sem, tanh_done.at(layer, n + 1))
                        if c < C_GB:
                            dve.scalar_tensor_tensor(out=w_gates[cols], in0=th_buf, scalar=1.0, in1=ps[:, b:b + 2, :],
                                                     op0=ALU.add, op1=ALU.mult).then_inc(th_used.sem, 1)
                        elif c < C_GA:
                            dve.scalar_tensor_tensor(out=w_gates[cols], in0=th_buf, scalar=1.0, in1=w_gates[cols],
                                                     op0=ALU.add, op1=ALU.mult).then_inc(th_used.sem, 1)
                            dve.wait_ge(th_used.sem, th_used.at(layer, n + 1))
                            for t in range(T):
                                part = w_gates[:, t, o:o + 512].rearrange("p (h v) -> p h v", v=DV)
                                last = dve.tensor_tensor(part, part, gla_gain_row[:, :].rearrange("p (a v) -> p a v", a=1)
                                                         .broadcast_to([P, 512 // DV, DV]), ALU.mult)
                            chain.link(last)
                        else:
                            dve.scalar_tensor_tensor(out=xn[cols], in0=th_buf, scalar=1.0, in1=xn[cols],
                                                     op0=ALU.add, op1=ALU.mult).then_inc(th_used.sem, 1)
                            dve.wait_ge(th_used.sem, th_used.at(layer, n + 1))
                            dve.tensor_tensor(xn[cols], xn[cols], vb[cols], ALU.add).then_inc(merged.sem, 1)
                    elif what == "gate_z":
                        dve.wait_ge(z_mm.sem, z_mm.at(layer, 1))
                        for h in range(GH):
                            last = dve.tensor_scalar(z_buf[:, h, :], ps[:, LIN + h // 2, (h % 2) * SEQ:(h % 2 + 1) * SEQ],
                                                     gate_bias[:, h:h + 1], None, ALU.add)
                        last.then_inc(z_done.sem, 1)
                    elif what == "gate_log":
                        dve.wait_ge(log_done.sem, log_done.at(layer, 1))
                        chain.link(dve.scalar_tensor_tensor(out=flat(z_buf[:, :, :]), in0=flat(z_buf[:, :, :]), scalar=0.0,
                                                            in1=flat(g_cum[:, :, :]), op0=ALU.min, op1=ALU.subtract))
                        for h in range(GH):
                            for t in range(T):
                                tile = (slice(None), h, slice(t * P, (t + 1) * P))
                                last = dve.tensor_tensor_scan(g_cum[tile], ones[:, :], z_buf[tile], 0.0,
                                                              op0=ALU.mult, op1=ALU.add)
                        chain.link(last)
                        dve.tensor_tensor(k_state[:, :, :], g_cum[:, :, P - 1:P].broadcast_to([P, GH, P]),
                                          g_cum[:, :, 0:P], ALU.subtract).then_inc(diffs_done.sem, 1)
                        by_chunk = flat(g_cum[:, :, :]).rearrange("p (c i) -> p c i", i=CH)
                        dve.tensor_tensor(flat(z_buf[:, :, :]).rearrange("p (c i) -> p c i", i=CH), by_chunk,
                                          by_chunk[:, :, 0:1].broadcast_to([P, GH * SEQ // CH, CH]),
                                          ALU.subtract).then_inc(diffs_done.sem, 1)
                    elif what == "gate_exp":
                        dve.wait_ge(exps_done.sem, exps_done.at(layer, 1))
                        dve.wait_ge(evac_act.sem, evac_act.at(layer, C_KB + 1))
                        dve.tensor_tensor(k_state[:, :, :], k_state[:, :, :], kb_t[:, :, 0:P], ALU.mult)\
                            .then_inc(k_state_done.sem, 1)
                    elif what == "q_exp":
                        dve.wait_ge(exps_done.sem, exps_done.at(layer, 2))
                        dve.wait_ge(evac_dve.sem, evac_dve.at(layer, 1))
                        chain.link(dve.tensor_tensor(q_state[:, :, :], q_state[:, :, :], qb_t[:, :, P:2 * P], ALU.mult))
                        dve.wait_ge(exps_done.sem, exps_done.at(layer, 3))
                        dve.tensor_tensor(flat(qb_t[:, :, :]), flat(qb_t[:, :, :]), flat(z_buf[:, :, :]), ALU.mult)\
                            .then_inc(q_ready.sem, 1)
                    elif what == "ks_diff":
                        r = arg[0]
                        t, hp = r // 2, 2 * (r % 2)
                        if r:
                            dve.wait_ge(a_mm.sem, a_mm.at(layer, r))
                        else:
                            dve.wait_ge(keys_cleared.sem, 1)
                        for c in range(NC):
                            n = CH * (c + 1)
                            at = t * P + c * CH
                            last = dve.tensor_tensor(k_scaled[:, :, c, 0:n],
                                                     g_cum[:, hp:hp + 2, at:at + 1].broadcast_to([P, 2, n]),
                                                     g_cum[:, hp:hp + 2, t * P:t * P + n], ALU.subtract)
                        last.then_inc(ks_diff.sem, 1)
                    elif what == "ks_mul":
                        r = arg[0]
                        t, hp = r // 2, 2 * (r % 2)
                        dve.wait_ge(ks_exp.sem, ks_exp.at(layer, r + 1))
                        for c in range(NC):
                            n = CH * (c + 1)
                            last = dve.tensor_tensor(k_scaled[:, :, c, 0:n], k_scaled[:, :, c, 0:n],
                                                     kb_t[:, hp:hp + 2, t * P:t * P + n], ALU.mult)
                        last.then_inc(ks_ready.sem, 1)
                    elif what == "a":
                        r = arg[0]
                        hp = 2 * (r % 2)
                        dve.wait_ge(a_mm.sem, a_mm.at(layer, r + 1))
                        if r >= 2:
                            dve.wait_ge(o_mm.sem, o_mm.at(layer, r - 1))
                        dve.tensor_tensor(a_t[:, hp:hp + 2, :], ps[:, LIN, 0:2 * P].rearrange("p (h i) -> p h i", h=2),
                                          gla_mask[:, :].rearrange("p (a i) -> p a i", a=1).broadcast_to([P, 2, P]),
                                          ALU.mult).then_inc(a_ready.sem, 1)
                    elif what == "lin_rms":
                        t = arg[0]
                        heads = slice(t * GH, (t + 1) * GH)
                        dve.wait_ge(lin_squared.sem, lin_squared.at(layer, 2 * t + 2))
                        chain.link(rsqrt(gla_rstd[:, heads], gla_nt[:, 0, heads], gla_nt[:, 1, heads], gla_ss[:, heads], DV))
                    elif what == "lin_norm":
                        t = arg[0]
                        for h in range(GH):
                            o, w = (b[:, t, h * DV:(h + 1) * DV] for b in (vb, w_gates))
                            last = dve.scalar_tensor_tensor(out=o, in0=o, scalar=gla_rstd[:, t * GH + h:t * GH + h + 1],
                                                            in1=w, op0=ALU.mult, op1=ALU.mult)
                        chain.link(last)
                    elif what == "head" and arg[0] < HEADS:
                        i = arg[0]
                        p, h = probs[i % 2], HEAD_ORDER[i]
                        dve.wait_ge(scores_mm.sem, scores_mm.at(layer, i + 1))
                        if i >= 2:
                            dve.wait_ge(turned.sem, turned.at(layer, i - 1))
                        dve.scalar_tensor_tensor(out=p[:, :], in0=ps[:, SCORES, 0:3 * P], scalar=DH ** -0.5,
                                                 in1=att_mask[:, :], op0=ALU.mult, op1=ALU.add)\
                            .then_inc(scores_read.sem, 1)
                        dve.wait_ge(scores_read.sem, scores_read.at(layer, i + 1))
                        dve.tensor_reduce(row_max[:, 0:1], p[:, 0:2 * P], AX_X, ALU.max)
                        chain.link(dve.tensor_reduce(row_max[:, 1:2], p[:, 2 * P:3 * P], AX_X, ALU.max))
                        dve.tensor_scalar(neg_max[:, h, :], row_max[:, :], sink_rows[:, h:h + 1], -1.0, ALU.max, ALU.mult)\
                            .then_inc(soft_ready.sem, 1)
                    elif what == "att_norm":
                        b = arg[0]
                        both = sink_rows[:, :].rearrange("p (a b h) -> p a b h", a=2, b=2)[:, :, b, :]
                        both = both.rearrange("p a (h t) -> p a h t", t=1).broadcast_to([P, 2, 4, 2])
                        negs = neg_max[:, :, :].rearrange("p (a b h) t -> p a b h t", a=2, b=2)[:, :, b]
                        diff = sink_exp[:, :, :].rearrange("p (a b h) t -> p a b h t", a=2, b=2)[:, :, b]
                        part = of_heads(sink_exp[:, :, :], b)
                        dve.wait_ge(soft_ready.sem, soft_ready.at(layer, (b + 1) * HEADS // 2))
                        dve.tensor_tensor(diff, negs, both, ALU.add).then_inc(sink_diff.sem, 1)
                        dve.wait_ge(sink_exp_done.sem, sink_exp_done.at(layer, b + 1))
                        chain.link(dve.tensor_tensor(part, of_heads(row_sum[:, :, :], b), part, ALU.add))
                        chain.link(dve.reciprocal(part, part))
                        chain.link(dve.tensor_scalar(part, part, 0.5, None, ALU.mult))
                        dve.wait_ge(att_out.sem, att_out.at(layer, (b + 1) * HEADS // 2))
                        for t in range(T):
                            y = xn[:, t, :].rearrange("p (a b h d) -> p a b h d", a=2, b=2, d=DH)[:, :, b]
                            last = dve.tensor_tensor(y, y, diff[:, :, :, 1 - t:2 - t].broadcast_to([P, 2, 4, DH]), ALU.mult)
                        chain.link(last)
                    elif what == "merge":
                        half = arg[0]
                        dve.wait_ge(mrg_hi_done.sem, mrg_hi_done.at(layer, half + 1))
                        for t in range(T):
                            last = dve.tensor_tensor(half_of(h_lo, t, half), as_tiles(ps[:, 2 - 2 * half + t, :]),
                                                     half_of(h_hi, t, half).bitcast(F32), ALU.subtract)
                        last.then_inc(mrg_ready.sem, 1)
                split_lo(2, layer, q0[MIX][2] + MQ - 1)
                split_lo(0, layer, q0[FFN2][0])
                residual(layer, MIX, 0)
                norm_diag(layer, FFN2, 0)
                split_lo(1, layer, q0[FFN2][1])
                next_stage(layer, MIX)

            dve.memset(ada_acc[:, 1:3, :], 0.0).then_inc(first_cleared.sem, 1)
            for s in range(NS):
                dve.nop().then_inc(lo_done[s].sem, 1)
            dve.nop().then_inc(ada_used.sem, 1)
            dve.wait_ge(const_in.sem, CONSTS * 16)
            for t in range(T):
                dve.nop().then_inc(x_ready.sem, 1)
            dve.wait_ge(made.sem, MADE)
            norm_diag(0, 0, 0)
            dve.wait_ge(cond_ready.sem, 1)
            for k in range(KD):
                dve.wait_ge(stage_in[k].sem, 16)
                if k:
                    dve.wait_ge(stage_used.sem, k)
                for m in (1, 2):
                    last = dve.scalar_tensor_tensor(out=ada_acc[:, m, :], in0=ada_stage[k][:, (m - 1) * D:m * D],
                                                    scalar=cond[:, k:k + 1], in1=ada_acc[:, m, :],
                                                    op0=ALU.mult, op1=ALU.add)
                last.then_inc(stage_used.sem, 1)
            split_lo(0, 0, 0)
            take_mods(0, -1, 0)
            prepare(0, 0, 0)
            split_lo(1, 0, 0)
            with dve.Fori(0, L) as layer:
                chain.enter(layer)
                ffn(layer, FFN1)
                mix(layer)
                ffn(layer, FFN2)
            chain.leave()
            dve.wait_ge(const_in.sem, (CONSTS + 1) * 16)
            for t in range(T):
                if t:
                    norm(L, 0, t)
                dve.scalar_tensor_tensor(out=xn[:, t, :], in0=x[:, t, :], scalar=rstd[:, t:t + 1], in1=gate_row[:, :],
                                         op0=ALU.mult, op1=ALU.mult).then_inc(final_done.sem, 1)

        @block.tensor
        def _(pe):
            def product(o, lhs, rhs, start, stop, shared=False):
                for n, (a, b) in enumerate(((0, 0), (1, 0), (0, 1))):
                    last = pe.matmul(o, lhs[a], rhs[b], start=start and n == 0, stop=stop and n == 2,
                                     skip_group_check=shared)
                return last

            def unit_ready(s, layer, q):
                pe.wait_ge(lo_done[s].sem, lo_done[s].at(layer, q + 1))

            def prepare(layer, n, t):
                pe.wait_ge(diag_done.sem, diag_done.at(layer, n * T + t + 1))
                for half in range(2):
                    for k in range(KA):
                        o = (half * KA + k) * P
                        last = pe.matmul(ps[:, 2 * t + half, k * P:(k + 1) * P], x[:, t, o:o + P], diag[t][:, :],
                                         start=True, stop=True)
                    last.then_inc(x_tr.sem, 1)

            def h_is_ready(layer, n, t, half):
                pe.wait_ge(h_ready.sem, h_ready.at(layer, (n * T + t) * 2 + half + 1))

            def h_tile(k, t):
                return [part[:, k, t * P:(t + 1) * P] for part in (h_hi, h_lo)]

            def w_cols(s, a, b):
                return [part[s][:, a:b] for part in (w_hi, w_lo)]

            def down(t, parts, w, k0, start, stop):
                for k in range(2):
                    for n in range(2):
                        o = (2 * k + n) * 512
                        last = product(ps[:, Y + 2 * t + n, :], [a[:, k0 + k, t * P:(t + 1) * P] for a in parts],
                                       [part[:, o:o + 512] for part in w], start=start and k == 0, stop=stop and k == 1)
                return last

            def sum_gate(layer, stage, half):
                if half:
                    pe.wait_ge(gate_row_done.sem, gate_row_done.at(layer, 2 * stage + 1))
                else:
                    pe.wait_ge(ada_used.sem, ada_used.at(layer, (stage + 1) * KD))
                pe.matmul(ps[:, SUMS, :], ones[:, :], ada_acc[:, 0, half * 512:(half + 1) * 512], start=True, stop=True)\
                    .then_inc(gate_sum.sem, 1)

            def sum_cols():
                for m in (1, 2):
                    for k in range(KD):
                        last = pe.matmul(ps[:, SUMS, (m - 1) * KD + k:(m - 1) * KD + k + 1],
                                         ada_acc[:, m, k * P:(k + 1) * P], ones[:, 0:1], start=True, stop=True)
                last.then_inc(cols_sum.sem, 1)

            def ffn(layer, stage):
                q, f = q0[stage], ffn_no[stage]

                def up(j, half, t):
                    for k in range(KA):
                        last = product(ps[:, t, :], h_tile(half * KA + k, t), w_cols(half, k * 512, (k + 1) * 512),
                                       start=half == 0 and k == 0, stop=half == 1 and k == KA - 1)
                    if t == 1:
                        last.then_inc(used[half].sem, 1)
                    elif half == 1:
                        last.then_inc(gu0_done.sem, 1)

                def up0(j):
                    unit_ready(0, layer, q[0] + j)
                    for t in range(T):
                        pe.wait_ge(hidden_done.sem, hidden_done.at(layer, (f * NJ + j) * T + t + 1 - T))
                        up(j, 0, t)

                def up1(j):
                    unit_ready(1, layer, q[1] + j)
                    for t in range(T):
                        up(j, 1, t)

                def turn(j, t):
                    pe.wait_ge(hidden_done.sem, hidden_done.at(layer, (f * NJ + j) * T + t + 1))
                    for k in range(2):
                        last = pe.transpose(ps[:, HID, k * SEQ + t * P:k * SEQ + (t + 1) * P],
                                            hidden[:, t, k * P:(k + 1) * P], ident[:, :])
                    return last

                def turns(j):
                    turn(j, 0)
                    turn(j, 1).then_inc(hid_tr.sem, 1)

                def downs(j, start):
                    pe.wait_ge(hid_ready.sem, hid_ready.at(layer, f * (NJ + 1) + j + 1))
                    unit_ready(2, layer, q[2] + j)
                    for t in range(T):
                        last = down(t, (hid_hi, hid_lo), (w_hi[2], w_lo[2]), 0, start, False)
                    last.then_inc(used[2].sem, 1)

                for t in range(T):
                    for half in range(2):
                        if t == 0:
                            unit_ready(half, layer, q[half])
                        elif half == 0:
                            prepare(layer, stage, 1)
                        h_is_ready(layer, stage, t, half)
                        up(0, half, t)
                up0(1)
                turns(0)
                up1(1)
                downs(0, True)
                with pe.Fori(2, NJ - 1) as j:
                    up0(j)
                    turns(j - 1)
                    up1(j)
                    downs(j - 1, False)
                up0(NJ - 1)
                sum_gate(layer, stage, 0)
                turns(NJ - 2)
                up1(NJ - 1)
                pe.wait_ge(hid_ready.sem, hid_ready.at(layer, f * (NJ + 1) + NJ - 1))
                turn(NJ - 1, 0).then_inc(hid_tr.sem, 1)
                unit_ready(2, layer, q[2] + NJ - 2)
                down(0, (hid_hi, hid_lo), (w_hi[2], w_lo[2]), 0, False, False).then_inc(down_t0.sem, 1)
                sum_gate(layer, stage, 1)
                pe.wait_ge(last_lo_done.sem, last_lo_done.at(layer, f + 1))
                pe.wait_ge(hid_ready.sem, hid_ready.at(layer, f * (NJ + 1) + NJ))
                down(0, (hid_hi, hid_lo), (last_hi, last_lo), 0, False, True).then_inc(y0_done.sem, 1)
                down(1, (hid_hi, hid_lo), (w_hi[2], w_lo[2]), 0, False, False).then_inc(used[2].sem, 1)
                turn(NJ - 1, 1).then_inc(hid_tr.sem, 1)
                pe.wait_ge(gate_row_done.sem, gate_row_done.at(layer, 2 * stage + 2))
                sum_cols()
                prepare(layer, stage + 1, 0)
                pe.wait_ge(hid_ready.sem, hid_ready.at(layer, f * (NJ + 1) + NJ + 1))
                down(1, (hid_hi, hid_lo), (last_hi, last_lo), 0, False, True).then_inc(last_used.sem, 1)

            def evacuated(layer, c):
                if c == C_QB:
                    pe.wait_ge(evac_dve.sem, evac_dve.at(layer, 1))
                elif c < C_R:
                    pe.wait_ge(evac_act.sem, evac_act.at(layer, c + 1))
                elif c < C_GB:
                    pe.wait_ge(th_used.sem, th_used.at(layer, c - C_R + 1))
                else:
                    pe.wait_ge(tanh_done.sem, tanh_done.at(layer, c - C_R + 1))

            def turn_merged(layer, half):
                pe.wait_ge(merged.sem, merged.at(layer, half + 1))
                for t in range(T):
                    for k in range(KA):
                        last = pe.transpose(ps[:, 2 - 2 * half + t, k * P:(k + 1) * P],
                                            xn[:, t, half * 512 + k * P:half * 512 + (k + 1) * P], ident[:, :])
                last.then_inc(mrg_tr.sem, 1)

            def att_v(half, t):
                for k in range(KA):
                    last = product(ps[:, 1, t * P:(t + 1) * P], h_tile(half * KA + k, t),
                                   w_cols(half, k * QKV0 + RANK + P, (k + 1) * QKV0),
                                   start=half == 0 and k == 0 and t == 0, stop=half == 1 and k == KA - 1, shared=True)
                return last

            def unit(layer, u):
                c, half, s, b = u // 2, u % 2, u % NS, bank_of(u // 2)
                unit_ready(s, layer, q0[MIX][s] + u // NS)
                if half == 0 and c >= 2:
                    evacuated(layer, c - 2)
                first, last_k = half == 0, KA - 1
                if c == C_LKV:
                    for n, (o, a) in enumerate(((ps[:, 0, 0:SEQ], 0), (ps[:, 0, SEQ:2 * SEQ], RANK))):
                        for k in range(KA):
                            product(o, w_cols(s, k * QKV0 + a, k * QKV0 + a + P),
                                    [part[:, half * KA + k, :] for part in (h_hi, h_lo)],
                                    start=first and k == 0 and n == 0, stop=half == 1 and k == last_k, shared=True)
                    last = att_v(half, 1)
                elif c in TRANSPOSED:
                    for g in range(4):
                        for k in range(KA):
                            last = product(ps[:, b + g // 2, (g % 2) * SEQ:(g % 2 + 1) * SEQ],
                                           w_cols(s, k * 512 + g * P, k * 512 + (g + 1) * P),
                                           [part[:, half * KA + k, :] for part in (h_hi, h_lo)],
                                           start=first and k == 0 and g % 2 == 0, stop=half == 1 and k == last_k,
                                           shared=True)
                else:
                    for t in range(T):
                        if t == 1 and u == 2 * N_CHUNK - 1:
                            turn_merged(layer, 0)
                        for k in range(KA):
                            last = product(ps[:, b + t, :], h_tile(half * KA + k, t), w_cols(s, k * 512, (k + 1) * 512),
                                           start=first and k == 0, stop=half == 1 and k == last_k)
                last.then_inc(used[s].sem, 1)

            def head(layer, i):
                if i < HEADS:
                    h = HEAD_ORDER[i]
                    pe.wait_ge(evac_act.sem, evac_act.at(layer, C_Q + 1 + h % GROUP // 4))
                    if i >= 1:
                        pe.wait_ge(scores_read.sem, scores_read.at(layer, i))
                    rows, g = slice((h // GROUP) * DH, (h // GROUP + 1) * DH), h % GROUP
                    pe.matmul(ps[:, SCORES, 0:SEQ], q_t[rows, g, P:2 * P], k_t[rows, 0:SEQ], start=True, stop=True)
                    pe.matmul(ps[:, SCORES, SEQ:SEQ + P], q_t[rows, g, 0:P], k_t[rows, 0:P], start=True, stop=True)\
                        .then_inc(scores_mm.sem, 1)
                if i >= 2:
                    n = i - 2
                    p, v0 = probs_t[n % 2], (HEAD_ORDER[n] // GROUP) * DH
                    pe.wait_ge(probs_t_done.sem, probs_t_done.at(layer, n + 1))
                    if n >= 1:
                        pe.wait_ge(att_out.sem, att_out.at(layer, n))
                    o = [ps[:, TURNED, 3 * P + t * DH:3 * P + (t + 1) * DH] for t in range(T)]
                    pe.matmul(o[0], p[:, 2 * P:3 * P], v_att[:, 0, v0:v0 + DH], start=True, stop=True)
                    pe.matmul(o[1], p[:, 0:P], v_att[:, 0, v0:v0 + DH], start=True, stop=False)
                    last = pe.matmul(o[1], p[:, P:2 * P], v_att[:, 1, v0:v0 + DH], start=False, stop=True)
                if 1 <= i <= HEADS:
                    pe.wait_ge(probs_done.sem, probs_done.at(layer, i))
                    if i >= 2:
                        pe.wait_ge(probs_t_done.sem, probs_t_done.at(layer, i - 1))
                    for n in range(3):
                        last = pe.transpose(ps[:, TURNED, n * P:(n + 1) * P], probs[(i - 1) % 2][:, n * P:(n + 1) * P],
                                            ident[:, :])
                if i >= 1:
                    last.then_inc(turned.sem, 1)

            def mix(layer):
                h_is_ready(layer, MIX, 0, 1)
                for half in range(2):
                    unit_ready(half, layer, q0[MIX][half])
                    att_v(half, 0)
                prepare(layer, MIX, 1)
                h_is_ready(layer, MIX, 1, 1)
                for what, *arg in PLAN:
                    if what == "unit":
                        unit(layer, arg[0])
                    elif what == "gate_z":
                        pe.wait_ge(evac_act.sem, evac_act.at(layer, 1))
                        pe.wait_ge(layer_in.sem, layer_in.at(layer, 4))
                        for h in range(GH):
                            last = pe.matmul(ps[:, LIN + h // 2, (h % 2) * SEQ:(h % 2 + 1) * SEQ],
                                             gate_weight[:, h * DK:(h + 1) * DK], lr_t[0:RANK], start=True, stop=True)
                        last.then_inc(z_mm.sem, 1)
                    elif what == "k_turn":
                        pe.wait_ge(k_state_done.sem, k_state_done.at(layer, 1))
                        for h in range(GH):
                            last = pe.transpose(ps[:, LIN, h * P:(h + 1) * P], k_state[:, h, :], ident[:, :])
                        last.then_inc(k_state_tr.sem, 1)
                    elif what == "state":
                        pe.wait_ge(k_state_t_done.sem, k_state_t_done.at(layer, 1))
                        pe.wait_ge(evac_act.sem, evac_act.at(layer, C_VB + 2))
                        for h in range(GH):
                            last = pe.matmul(ps[:, LIN + h // 2, (h % 2) * DV:(h % 2 + 1) * DV],
                                             k_state_t[:, h * DK:(h + 1) * DK], vb[:, 0, h * DV:(h + 1) * DV],
                                             start=True, stop=True)
                        last.then_inc(state_mm.sem, 1)
                    elif what == "a":
                        r = arg[0]
                        t, hp = r // 2, 2 * (r % 2)
                        pe.wait_ge(ks_ready.sem, ks_ready.at(layer, r + 1))
                        if r == 0:
                            pe.wait_ge(state_done.sem, state_done.at(layer, 1))
                            pe.wait_ge(q_ready.sem, q_ready.at(layer, 1))
                        else:
                            pe.wait_ge(a_ready.sem, a_ready.at(layer, r))
                        for h in range(2):
                            for c in range(NC):
                                last = pe.matmul(ps[:, LIN, h * P + c * CH:h * P + (c + 1) * CH],
                                                 k_scaled[:, h, c, :],
                                                 qb_t[:, hp + h, t * P + c * CH:t * P + (c + 1) * CH],
                                                 start=True, stop=True)
                        last.then_inc(a_mm.sem, 1)
                    elif what == "o":
                        r = arg[0]
                        t, hp = r // 2, 2 * (r % 2)
                        pe.wait_ge(a_ready.sem, a_ready.at(layer, r + 1))
                        if r:
                            pe.wait_ge(lin_squared.sem, lin_squared.at(layer, r))
                        for h in range(2):
                            o = ps[:, LIN + 1, h * DV:(h + 1) * DV]
                            last = pe.matmul(o, a_t[:, hp + h, :], vb[:, t, (hp + h) * DV:(hp + h + 1) * DV],
                                             start=True, stop=t == 0)
                            if t:
                                last = pe.matmul(o, q_state[:, hp + h, :], state[:, (hp + h) * DV:(hp + h + 1) * DV],
                                                 start=False, stop=True)
                        last.then_inc(o_mm.sem, 1)
                    elif what == "head":
                        head(layer, arg[0])

                def out_unit(n, tiles):
                    u = 2 * N_CHUNK + n
                    unit_ready(u % NS, layer, q0[MIX][u % NS] + u // NS)
                    for t in tiles:
                        last = down(t, (h_hi, h_lo), (w_hi[u % NS], w_lo[u % NS]), 2 * n, n == 0, n == KD // 2 - 1)
                        if t == 1:
                            last.then_inc(used[u % NS].sem, 1)
                    return last

                pe.wait_ge(mrg_ready.sem, mrg_ready.at(layer, 1))
                out_unit(0, (0, 1))
                turn_merged(layer, 1)
                out_unit(1, (0, 1))
                sum_gate(layer, MIX, 0)
                pe.wait_ge(mrg_ready.sem, mrg_ready.at(layer, 2))
                out_unit(2, (0,))
                sum_gate(layer, MIX, 1)
                out_unit(3, (0,)).then_inc(y0_done.sem, 1)
                out_unit(2, (1,))
                pe.wait_ge(gate_row_done.sem, gate_row_done.at(layer, 2 * MIX + 2))
                sum_cols()
                prepare(layer, FFN2, 0)
                out_unit(3, (1,))

            for s in range(NS):
                pe.nop().then_inc(used[s].sem, 1)
            pe.wait_ge(made.sem, MADE)
            prepare(0, 0, 0)
            pe.wait_ge(stage_used.sem, KD)
            sum_cols()
            with pe.Fori(0, L) as layer:
                ffn(layer, FFN1)
                mix(layer)
                ffn(layer, FFN2)


def kernel(**inputs):
    import numpy as np
    import concourse.bacc as bacc
    from concourse.bass_utils import run_bass_kernel_spmd

    a = {k: np.asarray(v) for k, v in inputs.items()}

    def tiles(w):
        return w.reshape(w.shape[0] // P, P, w.shape[1]).transpose(1, 0, 2)

    stream = [np.zeros((L * n + 1, P, UNIT), np.float32) for n in NSEQ]
    last = np.empty((L * 2, P, UNIT), np.float32)
    sizes = (HEADS * DH, 2 * DH, 2 * DH, GH * DK, GH * DK, GH * DV, RANK, GH * DV, D, D)
    at = [0]
    for n in sizes:
        at.append(at[-1] + n)
    qa, ka, va, qb, kb, vb, lr, r, ga, gb = (np.arange(s, s + n) for s, n in zip(at, sizes))
    pairs = qa.reshape(2, GROUP, DH).transpose(1, 0, 2).reshape(-1)
    chunks = [np.concatenate([lr, ka, va]), pairs[:512], pairs[512:], vb[:512], vb[512:], kb, qb,
              r[:512], r[512:], gb[:512], gb[512:], ga[:512], ga[512:]]
    for layer in range(L):
        base = [layer * n for n in NSEQ]
        for f, (w_in, w_out) in enumerate((("ffn1_w_in", "ffn1_w_out"), ("ffn2_w_in", "ffn2_w_out"))):
            up = tiles(a[w_in][layer]).reshape(P, KD, 2, NJ, FC)
            dn = tiles(a[w_out][layer])
            first = [b + f * (n + MQ) for b, n in zip(base, FFN_UNITS)]
            for j in range(NJ):
                both = up[:, :, :, j, :].reshape(P, KD, 2 * FC)
                stream[0][first[0] + j] = both[:, :KA].reshape(P, UNIT)
                stream[1][first[1] + j] = both[:, KA:].reshape(P, UNIT)
                rows = dn[:, 2 * j:2 * j + 2].reshape(P, UNIT)
                if j < NJ - 1:
                    stream[2][first[2] + j] = rows
                else:
                    last[2 * layer + f] = rows
        first = [b + n for b, n in zip(base, FFN_UNITS)]
        w = tiles(a["mix_w_in"][layer])
        for c, cols in enumerate(chunks):
            for half in range(2):
                u = 2 * c + half
                part = w[:, half * KA:(half + 1) * KA][:, :, cols].reshape(P, -1)
                stream[u % NS][first[u % NS] + u // NS, :, :part.shape[1]] = part
        w = tiles(a["mix_w_out"][layer])
        for n in range(KD // 2):
            u = 2 * N_CHUNK + n
            stream[u % NS][first[u % NS] + u // NS] = w[:, 2 * n:2 * n + 2].reshape(P, UNIT)

    ada = [a["ada_w"][layer].reshape(D, 9, D)[:, m] for layer in range(L) for m in range(9)]
    bias = [a["ada_b"][layer].reshape(9, D)[m] for layer in range(L) for m in range(9)]
    nothing = np.zeros((D, D), np.float32)
    ada += [nothing, nothing]
    bias += [nothing[0], nothing[0]]
    ada_first = np.stack([tiles(ada[0]), tiles(ada[1])], axis=2).transpose(1, 0, 2, 3).reshape(KD, P, 2 * D)
    ada_w = np.empty((3 * L, KD, P, 3, D), np.float32)
    ada_bias = np.zeros((3 * L + 1, 3, D), np.float32)
    ada_bias[0, 1:] = bias[:2]
    for g in range(3 * L):
        for m in range(3):
            ada_w[g, :, :, m] = ada[2 + 3 * g + m].reshape(KD, P, D)
            ada_bias[g + 1, m] = bias[2 + 3 * g + m]

    def cols(v):
        return v.reshape(-1, P).T

    gains = [a[n][layer] for layer in range(L) for n in ("norm1", "norm_mix", "norm2")] + [nothing[0]]
    arrays = {
        "x_in": a["x"].reshape(T, P, D).transpose(1, 0, 2),
        "cond_in": cols(a["c"][0]),
        "stream0": stream[0],
        "stream1": stream[1],
        "stream2": stream[2],
        "w_last": last,
        "ada_first": ada_first,
        "ada_w": ada_w.reshape(3 * L * KD, P, ADA_W),
        "ada_bias": ada_bias,
        "gains": np.stack([cols(g) for g in gains], axis=1),
        "sinks": np.broadcast_to(a["attn_sinks"][:, None, :], (L, P, HEADS)),
        "gate_w": a["gla_w_gate"],
        "gate_b": np.stack([cols(b) for b in a["gla_b_gate"]]),
        "gla_gain": np.broadcast_to(a["gla_out_norm"][:, None, :], (L, P, DV)),
        "final_gain": np.broadcast_to(a["final_norm"][None, :], (P, D)),
    }
    arrays = {k: np.ascontiguousarray(v) for k, v in arrays.items()}
    nc = bacc.Bacc("TRN2", target_bir_lowering=False, num_devices=1)
    args = [nc.dram_tensor(k, v.shape, mybir.dt.from_np(v.dtype), kind="ExternalInput").ap() for k, v in arrays.items()]
    out = nc.dram_tensor("out", (SEQ, D), F32, kind="ExternalOutput").ap()
    trunk(nc, *args, out)
    r = run_bass_kernel_spmd(nc, [arrays], core_ids=[0])
    return r.results[0]["out"].reshape(1, SEQ, D)
```

```python
from contextlib import ExitStack

import concourse.bass as bass
from concourse import mybir

F32 = mybir.dt.float32
F32R = mybir.dt.float32r
I32 = mybir.dt.int32
ALU = mybir.AluOpType
ACT = mybir.ActivationFunctionType
AX_X = mybir.AxisListType.X

P = 128
L = 2
D = 1024
KD = D // P
SEQ = 256
T = SEQ // P
D_FF = 2816
FC = 256
NJ = D_FF // FC
HEADS, DH, GROUP = 16, 64, 8
GH, DK, DV, RANK = 4, 128, 256, 16
CH = 16
NC = P // CH
EPS = 1e-6
MASKED = -1e30
RSQRT_SEED = float(0x5F3759DF)

UNIT = 2048
KA = 4
QKV0 = RANK + 2 * 128
N_CHUNK = 13
MIX_UNITS = 2 * N_CHUNK + KD // 2
NS = 3
MQ = MIX_UNITS // NS
FFN_UNITS = (NJ, NJ, NJ - 1)
NSEQ = [2 * n + MQ for n in FFN_UNITS]
ADA_W = 3 * D

C_VB0, C_LKV, C_Q, C_VB1, C_KB, C_QB, C_R, C_GB, C_GA = 0, 1, 2, 4, 5, 6, 7, 9, 11
TRANSPOSED = (C_KB, C_QB, C_Q, C_Q + 1)


def mix_width(u):
    return KA * QKV0 if u // 2 == C_LKV else UNIT


HEAD_ORDER = [0, 1, 2, 3, 8, 9, 10, 11, 4, 5, 6, 7, 12, 13, 14, 15]


ADA_AT = ((0, 0), (2, 2), (4, 4), (6, 7), (9, 9), (11, 12), (14, 15), (17, 18))

SPLIT_FIRST = (5, 11, 22)


def mix_plan():
    steps = {
        4: [("gate_z",)], 5: [("gate_log",)], 11: [("gate_exp",), ("ks_diff", 0)], 12: [("k_turn",), ("ks_mul", 0)],
        13: [("q_exp",), ("state",)], 18: [("lin_rms", 0)],
        22: [("lin_norm", 0), ("lin_rms", 1), ("lin_norm", 1)],
    }
    for r in range(4):
        for at, what in ((14, "a"), (15, "o")):
            steps.setdefault(at + 2 * r, []).append((what, r))
        if r:
            steps.setdefault(12 + 2 * r, []).append(("ks_diff", r))
            steps.setdefault(13 + 2 * r, []).append(("ks_mul", r))
    for i in range(HEADS + 2):
        steps.setdefault(6 + i, []).insert(0, ("head", i))
    steps[20].append(("att_norm", 0))
    steps[24] = [("att_norm", 1)]
    split_lo = {u: [("split_lo", u + NS - 1)] for u in range(22)}
    split_lo[22] = [("split_lo", 24), ("split_lo", 25)]
    split_lo.update({23: [("split_lo", 26)], 24: [], 25: [("split_lo", 27), ("split_lo", 28)]})
    plan = []
    for u in range(2 * N_CHUNK):
        plan.append(("unit", u))
        late = u in (11, 13)
        if u == 22:
            plan.append(("split_hi", u + NS))
        if u in SPLIT_FIRST:
            plan += split_lo[u]
        if u % 2 and late:
            plan.append(("evac", u // 2))
        plan += steps.get(u, [])
        if u % 2 and not late:
            plan.append(("evac", u // 2))
        if u not in SPLIT_FIRST and u < 23:
            plan += split_lo[u]
        for k, (two, third) in enumerate(ADA_AT):
            plan += [("ada", k, (0, 1))] * (u == two) + [("ada", k, (2,))] * (u == third)
        if u != 22:
            plan.append(("split_hi", u + NS))
        if u >= 23:
            plan += split_lo[u]
    plan.insert(plan.index(("unit", 2 * N_CHUNK - 1)) + 1, ("merge", 0))
    plan.append(("merge", 1))
    return plan


PLAN = mix_plan()


class Signal:

    def __init__(self, sem, per_layer, before=0, by=1):
        self.sem, self.per_layer, self.before, self.by = sem, per_layer, before, by

    def at(self, layer, n):
        return layer * (self.per_layer * self.by) + (n + self.before) * self.by


class Chain:

    def __init__(self, engine, sem, per_layer):
        self.engine, self.sem, self.per_layer = engine, sem, per_layer
        self.before, self.start, self.n = 0, 0, 0

    def enter(self, layer):
        self.before = self.n
        self.start, self.n = layer * self.per_layer + self.before, 0

    def leave(self):
        assert self.n == self.per_layer, (self.n, self.per_layer)
        self.start, self.n = L * self.per_layer + self.before, 0

    def link(self, ins):
        self.n += 1
        ins.then_inc(self.sem, 1)
        self.engine.wait_ge(self.sem, self.start + self.n)


NEWTON_THREES = (3.0, 12.0, 768.0)
NEWTON_SCALE = 2.0 ** 26

ACT_CHAIN, DVE_CHAIN = 2, 106


def trunk(nc, x_in, cond_in, stream0, stream1, stream2, w_last, ada_first, ada_w, ada_bias, gains, sinks, gate_w, gate_b,
          gla_gain, final_gain, out):
    w_stream = (stream0, stream1, stream2)
    with ExitStack() as ctx:
        def sb(name, shape, dt=F32):
            return ctx.enter_context(nc.sbuf_tensor(name, shape, dt))

        def signal(name, per_layer, before=0, by=1):
            return Signal(ctx.enter_context(nc.semaphore(name)), per_layer, before, by)

        w_raw = [sb(f"w_raw{s}", [P, UNIT]) for s in range(NS)]
        w_hi = [sb(f"w_hi{s}", [P, UNIT], F32R) for s in range(NS)]
        w_lo = [sb(f"w_lo{s}", [P, UNIT], F32R) for s in range(NS)]
        ada_raw = sb("ada_raw", [P, ADA_W])
        ada_acc = sb("ada_acc", [P, 3, D])
        x = sb("x", [P, T, D])
        xn = sb("xn", [P, T, D])
        h_hi = sb("h_hi", [P, KD, SEQ], F32R)
        h_lo = sb("h_lo", [P, KD, SEQ], F32R)
        gate_row = sb("gate_row", [P, D])
        mod_shift = sb("mod_shift", [P, KD])
        mod_scale = sb("mod_scale", [P, KD])
        cond = sb("cond", [P, KD])
        gain_cols = sb("gain_cols", [P, 3 * L + 1, KD])
        ident = sb("ident", [P, P])
        ones = sb("ones", [P, P])
        sum_sq = sb("sum_sq", [P, T])
        rstd = sb("rstd", [P, T])
        newton = sb("newton", [P, 2, 2])
        sink_rows = sb("sink_rows", [P, HEADS])
        gate_weight = sb("gate_weight", [RANK, GH * DK])
        gate_bias = sb("gate_bias", [P, GH])
        gla_gain_row = sb("gla_gain_row", [P, DV])
        att_mask = sb("att_mask", [P, 3 * P])
        gla_mask = sb("gla_mask", [P, P])

        with ExitStack() as ffn_ctx:
            silu_g = ffn_ctx.enter_context(nc.sbuf_tensor("silu_g", [P, T, FC], F32))
            hidden = ffn_ctx.enter_context(nc.sbuf_tensor("hidden", [P, T, FC], F32))
            hid_hi = ffn_ctx.enter_context(nc.sbuf_tensor("hid_hi", [P, 2, SEQ], F32R))
            hid_lo = ffn_ctx.enter_context(nc.sbuf_tensor("hid_lo", [P, 2, SEQ], F32R))
            last_raw = ffn_ctx.enter_context(nc.sbuf_tensor("last_raw", [P, UNIT], F32))
            last_hi = ffn_ctx.enter_context(nc.sbuf_tensor("last_hi", [P, UNIT], F32R))
            last_lo = ffn_ctx.enter_context(nc.sbuf_tensor("last_lo", [P, UNIT], F32R))
        with ExitStack() as first_ctx:
            ada_stage = [first_ctx.enter_context(nc.sbuf_tensor(f"ada_stage{k}", [P, 2 * D], F32)) for k in range(KD)]
            diag = [first_ctx.enter_context(nc.sbuf_tensor(f"diag{t}", [P, P], F32)) for t in range(T)]
        q_t = sb("q_t", [P, HEADS // 2, SEQ])
        k_t = sb("k_t", [P, SEQ])
        v_att = sb("v_att", [P, T, P])
        qb_t = sb("qb_t", [P, GH, SEQ])
        kb_t = sb("kb_t", [P, GH, SEQ])
        vb = sb("vb", [P, T, GH * DV])
        w_gates = sb("w_gates", [P, T, D])
        z_buf = sb("z_buf", [P, GH, SEQ])
        g_cum = sb("g_cum", [P, GH, SEQ])
        q_state = sb("q_state", [P, GH, P])
        k_state = sb("k_state", [P, GH, P])
        k_state_t = sb("k_state_t", [P, GH * DK])
        state = sb("state", [P, GH * DV])
        a_t = sb("a_t", [P, GH, P])
        lr_t = a_t[:, 0:2, :].rearrange("p h i -> p (h i)")
        k_scaled = sb("k_scaled", [P, 2, NC, P])
        probs = [sb(f"probs{i}", [P, 3 * P]) for i in range(2)]
        probs_t = [sb(f"probs_t{i}", [P, 3 * P]) for i in range(2)]
        gla_ss = sb("gla_ss", [P, T * GH])
        gla_nt = sb("gla_nt", [P, 2, T * GH])
        gla_rstd = sb("gla_rstd", [P, T * GH])
        row_max = sb("row_max", [P, 2])
        neg_max = sb("neg_max", [P, HEADS, 2])
        row_sum = sb("row_sum", [P, HEADS, 2])
        sink_exp = sb("sink_exp", [P, HEADS, 2])
        th_buf = z_buf[:, :, :].rearrange("p h s -> p (h s)").rearrange("p (t n) -> p t n", t=T)

        ps = ctx.enter_context(nc.psum_tensor("ps", [P, 8, 512], F32))
        SUMS, HID, Y = 3, 2, 4
        SCORES, TURNED, LIN = 4, 5, 6

        HID_PARTS = NJ + 2
        const_in = signal("const_in", 0, by=16)
        stage_in = [signal(f"stage_in{k}", 0, by=16) for k in range(KD)]
        raw_in = [signal(f"raw_in{s}", NSEQ[s], by=16) for s in range(NS)]
        last_in = signal("last_in", 2, by=16)
        ada_in = signal("ada_in", 3 * KD, by=16)
        seeded = [signal(f"seeded{m}", 3, by=16) for m in range(3)]
        layer_in = signal("layer_in", 4, by=16)
        out_sent = signal("out_sent", 0, by=16)
        made = signal("made", 0)
        acc_cleared = signal("acc_cleared", 3)
        keys_cleared = signal("keys_cleared", 0)
        gain_done = signal("gain_done", 2)
        cond_ready = signal("cond_ready", 0)
        hi_done = [signal(f"hi_done{s}", NSEQ[s]) for s in range(NS)]
        half_hi_done = signal("half_hi_done", 2)
        last_hi_done = signal("last_hi_done", 2)
        squared = signal("squared", 3 * T)
        h_mod_act = signal("h_mod_act", 3 * T)
        h_hi_done = signal("h_hi_done", 3 * T * 2)
        silu_done = signal("silu_done", 2 * NJ * T)
        hid_hi_done = signal("hid_hi_done", 2 * HID_PARTS)
        gate_row_done = signal("gate_row_done", 6)
        act_chain = ctx.enter_context(nc.semaphore("act_chain"))
        log_done = signal("log_done", 1)
        exps_done = signal("exps_done", 3)
        evac_act = signal("evac_act", 6)
        tanh_done = signal("tanh_done", 6)
        k_state_t_done = signal("k_state_t_done", 1)
        state_done = signal("state_done", 1)
        ks_exp = signal("ks_exp", 4)
        lin_out = signal("lin_out", 4)
        lin_squared = signal("lin_squared", 4)
        probs_done = signal("probs_done", HEADS)
        probs_t_done = signal("probs_t_done", HEADS)
        att_out = signal("att_out", HEADS)
        sink_exp_done = signal("sink_exp_done", 2)
        mrg_hi_done = signal("mrg_hi_done", 2)
        lo_done = [signal(f"lo_done{s}", NSEQ[s], before=1) for s in range(NS)]
        last_lo_done = signal("last_lo_done", 2)
        diag_done = signal("diag_done", 3 * T)
        h_mod_dve = signal("h_mod_dve", 3 * T)
        h_ready = signal("h_ready", 3 * T * 2)
        hidden_done = signal("hidden_done", 2 * NJ * T)
        hid_ready = signal("hid_ready", 2 * HID_PARTS)
        x_ready = signal("x_ready", 3 * T, before=T)
        first_cleared = signal("first_cleared", 0)
        stage_used = signal("stage_used", 0)
        ada_used = signal("ada_used", 3 * KD, before=1)
        mods_ready = signal("mods_ready", 3, before=1)
        dve_chain = ctx.enter_context(nc.semaphore("dve_chain"))
        z_done = signal("z_done", 1)
        diffs_done = signal("diffs_done", 2)
        evac_dve = signal("evac_dve", 1)
        k_state_done = signal("k_state_done", 1)
        q_ready = signal("q_ready", 1)
        ks_diff = signal("ks_diff", 4)
        ks_ready = signal("ks_ready", 4)
        a_ready = signal("a_ready", 4)
        th_used = signal("th_used", 6)
        scores_read = signal("scores_read", HEADS)
        soft_ready = signal("soft_ready", HEADS)
        sink_diff = signal("sink_diff", 2)
        merged = signal("merged", 2)
        mrg_ready = signal("mrg_ready", 2)
        final_done = signal("final_done", 0)
        used = [signal(f"used{s}", NSEQ[s], before=1) for s in range(NS)]
        gu0_done = signal("gu0_done", 2 * NJ)
        hid_tr = signal("hid_tr", 2 * HID_PARTS)
        down_t0 = signal("down_t0", 2)
        last_used = signal("last_used", 2)
        y0_done = signal("y0_done", 3)
        x_tr = signal("x_tr", 3 * T * 2)
        gate_sum = signal("gate_sum", 6)
        cols_sum = signal("cols_sum", 3, before=1)
        z_mm = signal("z_mm", 1)
        k_state_tr = signal("k_state_tr", 1)
        state_mm = signal("state_mm", 1)
        a_mm = signal("a_mm", 4)
        o_mm = signal("o_mm", 4)
        scores_mm = signal("scores_mm", HEADS)
        turned = signal("turned", HEADS + 1)
        mrg_tr = signal("mrg_tr", 2)

        FFN1, MIX, FFN2 = range(3)
        q0 = {FFN1: [0, 0, 0], MIX: list(FFN_UNITS), FFN2: [n + MQ for n in FFN_UNITS]}
        ffn_no = {FFN1: 0, FFN2: 1}
        MADE = 9
        CONSTS = 4

        def bank_of(c):
            return 2 * (c % 2)

        def flat(ap):
            return ap.rearrange("p a b -> p (a b)")

        def chunk_done(engine, layer, c):
            u = 2 * c + 1
            engine.wait_ge(used[u % NS].sem, used[u % NS].at(layer, q0[MIX][u % NS] + u // NS + 1))

        def hid_no(f, j, t=1):
            if isinstance(j, int) and j == 0:
                return f * HID_PARTS + 1 + t
            if isinstance(j, int) and j == NJ - 1:
                return f * HID_PARTS + NJ + 1 + t
            return f * HID_PARTS + j + 2

        def hid_bank(j, t):
            return ps[:, 1 if (j, t) == (0, 0) else HID, :].rearrange("p (k i) -> p k i", k=2)[:, :, t * P:(t + 1) * P]

        def half_of(buf, t, half):
            return buf[:, half * KA:(half + 1) * KA, t * P:(t + 1) * P]

        def as_tiles(ap):
            return ap.rearrange("p (k i) -> p k i", i=P)

        block = ctx.enter_context(nc.Block())

        @block.sync
        def _(sp):
            sp.dma_start(cond[:, :], cond_in).then_inc(const_in.sem, 16)
            sp.dma_start(gain_cols[:, :, :], gains).then_inc(const_in.sem, 16)
            sp.dma_start(x[:, :, :], x_in).then_inc(const_in.sem, 16)
            sp.wait_ge(first_cleared.sem, 1)
            sp.dma_start(ada_acc[0:1, 1:3, :], ada_bias[0:1, 1:3, :]).then_inc(const_in.sem, 16)
            for k in range(KD):
                sp.dma_start(ada_stage[k][:, :], ada_first[k]).then_inc(stage_in[k].sem, 16)

            def load(s, layer, q, width=UNIT):
                sp.wait_ge(lo_done[s].sem, lo_done[s].at(layer, q))
                sp.dma_start(w_raw[s][:, 0:width],
                             w_stream[s][bass.ds(layer * NSEQ[s] + q, 1)].rearrange("a p n -> p (a n)")[:, 0:width])\
                    .then_inc(raw_in[s].sem, 16)

            def load_ada(layer, n):
                sp.wait_ge(ada_used.sem, ada_used.at(layer, n))
                sp.dma_start(ada_raw[:, :], ada_w[bass.ds(layer * (3 * KD) + n, 1)].rearrange("a p n -> p (a n)"))\
                    .then_inc(ada_in.sem, 16)

            def ffn(layer, stage):
                q = q0[stage]
                for s in range(NS):
                    load(s, layer, q[s])
                load(0, layer, q[0] + 1)
                load(1, layer, q[1] + 1)
                load_ada(layer, stage * KD)
                with sp.Fori(1, KD) as j:
                    load(0, layer, q[0] + 1 + j)
                    load(1, layer, q[1] + 1 + j)
                    load(2, layer, q[2] + j)
                    load_ada(layer, stage * KD + j)
                sp.dma_start(last_raw[:, :], w_last[bass.ds(layer * 2 + ffn_no[stage], 1)]
                             .rearrange("a p n -> p (a n)")).then_inc(last_in.sem, 16)
                with sp.Fori(KD, NJ - 1) as j:
                    load(0, layer, q[0] + 1 + j)
                    load(1, layer, q[1] + 1 + j)
                    load(2, layer, q[2] + j)

            with sp.Fori(0, L) as layer:
                ffn(layer, FFN1)
                for dst, src in ((sink_rows, sinks), (gate_weight, gate_w), (gate_bias, gate_b), (gla_gain_row, gla_gain)):
                    sp.dma_start(dst[:, :], src[bass.ds(layer, 1)].rearrange("a p n -> p (a n)"))\
                        .then_inc(layer_in.sem, 16)
                for u in range(2 * NS - 1):
                    load(u % NS, layer, q0[MIX][u % NS] + u // NS, mix_width(u))
                load_ada(layer, MIX * KD)
                for what, *arg in PLAN:
                    if what == "split_lo" and arg[0] + NS < MIX_UNITS:
                        u = arg[0] + NS
                        load(u % NS, layer, q0[MIX][u % NS] + u // NS)
                    elif what == "ada" and 2 in arg[1] and arg[0] + 1 < KD:
                        load_ada(layer, MIX * KD + arg[0] + 1)
                ffn(layer, FFN2)

            for s in (0, 1):
                load(s, L, 0)
            sp.wait_ge(ada_used.sem, ada_used.at(L, 0))
            sp.dma_start(ada_raw[:, 0:D], final_gain).then_inc(const_in.sem, 16)
            for t in range(T):
                for half in range(2):
                    cols = slice(half * D // 2, (half + 1) * D // 2)
                    sp.wait_ge(final_done.sem, 2 * t + half + 1)
                    sp.dma_start(out[t * P:(t + 1) * P, cols], xn[:, t, cols]).then_inc(out_sent.sem, 16)
            sp.wait_ge(out_sent.sem, 2 * T * 16)

        @block.gpsimd
        def _(pool):
            def seed(n):
                pool.memset(ada_acc[:, :, :], 0.0).then_inc(acc_cleared.sem, 1)
                pool.wait_ge(acc_cleared.sem, n)
                for m in range(3):
                    pool.dma_start(ada_acc[0:1, m, :], ada_bias[n:n + 1, m, :]).then_inc(seeded[m].sem, 16)

            pool.memset(ident[:, :], 0.0).then_inc(made.sem, 1)
            pool.memset(ones[:, :], 1.0).then_inc(made.sem, 1)
            pool.memset(att_mask[:, :], 0.0).then_inc(made.sem, 1)
            pool.memset(gla_mask[:, :], 1.0).then_inc(made.sem, 1)
            pool.wait_ge(made.sem, 4)
            pool.affine_select(out=ident[:, :], in_=ident[:, :], compare_op=ALU.not_equal, fill=1.0, base=0,
                               pattern=[[-1, P]], channel_multiplier=1).then_inc(made.sem, 1)
            pool.affine_select(out=att_mask[:, 0:P], in_=att_mask[:, 0:P], compare_op=ALU.is_gt, fill=MASKED,
                               base=0, pattern=[[1, P]], channel_multiplier=-1).then_inc(made.sem, 1)
            for i in (1, 2):
                pool.affine_select(out=att_mask[:, i * P:(i + 1) * P], in_=att_mask[:, i * P:(i + 1) * P],
                                   compare_op=ALU.is_ge, fill=MASKED, base=0, pattern=[[-1, P]],
                                   channel_multiplier=1).then_inc(made.sem, 1)
            pool.affine_select(out=gla_mask[:, :], in_=gla_mask[:, :], compare_op=ALU.is_ge, fill=0.0, base=0,
                               pattern=[[1, P]], channel_multiplier=-1).then_inc(made.sem, 1)
            pool.wait_ge(stage_used.sem, KD)
            pool.memset(k_scaled[:, :, :, :], 0.0).then_inc(keys_cleared.sem, 1)
            for n in range(3 * L):
                if (n - 1) % 3 == MIX:
                    layer = n // 3
                    for half in range(2):
                        pool.wait_ge(th_used.sem, th_used.at(layer, C_GB + half - C_R + 1))
                        for t in range(T):
                            part = w_gates[:, t, half * 512:(half + 1) * 512].rearrange("p (h v) -> p h v", v=DV)
                            last = pool.tensor_tensor(part, part, gla_gain_row[:, :].rearrange("p (a v) -> p a v", a=1)
                                                      .broadcast_to([P, 512 // DV, DV]), ALU.mult)
                        last.then_inc(gain_done.sem, 1)
                pool.wait_ge(cols_sum.sem, cols_sum.at(0, n))
                seed(n + 1)

        @block.scalar
        def _(act):
            chain = Chain(act, act_chain, ACT_CHAIN)

            def split_hi(s, layer, q, width=UNIT):
                act.wait_ge(raw_in[s].sem, raw_in[s].at(layer, q + 1))
                act.wait_ge(used[s].sem, used[s].at(layer, q))
                act.activation(w_hi[s][:, 0:width], w_raw[s][:, 0:width], ACT.Copy).then_inc(hi_done[s].sem, 1)

            def square(layer, n, t):
                act.wait_ge(x_ready.sem, x_ready.at(layer, (n - 1) * T + t + 1))
                act.activation(xn[:, t, :], x[:, t, :], ACT.Square, accum_out=sum_sq[:, t:t + 1])\
                    .then_inc(squared.sem, 1)

            def prepare(layer, n, t):
                act.wait_ge(x_tr.sem, x_tr.at(layer, (n * T + t) * 2 + 2))
                act.wait_ge(mods_ready.sem, mods_ready.at(layer, n))
                for half, mod in enumerate((h_mod_dve, h_mod_act)):
                    for k in range(KA + 2 * half, KA + 2 * half + 2):
                        last = act.activation(xn[:, t, k * P:(k + 1) * P],
                                              ps[:, 2 * t + 1, (k - KA) * P:(k - KA + 1) * P], ACT.Identity,
                                              bias=mod_shift[:, k:k + 1], scale=mod_scale[:, k:k + 1])
                    if half == 1:
                        last.then_inc(h_mod_act.sem, 1)
                    act.wait_ge(mod.sem, mod.at(layer, n * T + t + 1))
                    act.activation(half_of(h_hi, t, half), as_tiles(xn[:, t, half * 512:(half + 1) * 512]), ACT.Copy)\
                        .then_inc(h_hi_done.sem, 1)

            def gate_half(layer, stage, half):
                act.wait_ge(gate_sum.sem, gate_sum.at(layer, 2 * stage + half + 1))
                act.activation(gate_row[:, half * 512:(half + 1) * 512], ps[:, SUMS, :], ACT.Copy,
                               scale=1.0 if stage == MIX else 0.5).then_inc(gate_row_done.sem, 1)

            def ffn(layer, stage):
                q, f = q0[stage], ffn_no[stage]
                def hid_part(j):
                    act.wait_ge(hid_tr.sem, hid_tr.at(layer, hid_no(f, j)))
                    act.wait_ge(used[2].sem, used[2].at(layer, q[2] + j))
                    act.activation(flat(hid_hi[:, :, :]), ps[:, HID, :], ACT.Copy).then_inc(hid_hi_done.sem, 1)

                def hid_tile(j, t):
                    act.wait_ge(hid_tr.sem, hid_tr.at(layer, hid_no(f, j, t)))
                    if j and t == 0:
                        act.wait_ge(down_t0.sem, down_t0.at(layer, f + 1))
                    elif j:
                        act.wait_ge(used[2].sem, used[2].at(layer, q[2] + NJ - 1))
                    act.activation(hid_hi[:, :, t * P:(t + 1) * P], hid_bank(j, t), ACT.Copy)\
                        .then_inc(hid_hi_done.sem, 1)

                def silu(j, t, first=False):
                    if t == 0:
                        act.wait_ge(gu0_done.sem, gu0_done.at(layer, f * NJ + j + 1))
                    else:
                        act.wait_ge(used[1].sem, used[1].at(layer, q[1] + j + 1))
                    if not first:
                        act.wait_ge(hidden_done.sem, hidden_done.at(layer, (f * NJ + j) * T + t + 1 - T))
                    act.activation(silu_g[:, t, :], ps[:, t, 0:FC], ACT.Silu).then_inc(silu_done.sem, 1)

                split_hi(2, layer, q[2])
                square(layer, stage, 1)
                silu(0, 0, first=True)
                hid_tile(0, 0)
                prepare(layer, stage, 1)
                act.wait_ge(raw_in[0].sem, raw_in[0].at(layer, q[0] + 2))
                act.wait_ge(used[0].sem, used[0].at(layer, q[0] + 1))
                for half, done in enumerate((half_hi_done, hi_done[0])):
                    cols = slice(half * UNIT // 2, (half + 1) * UNIT // 2)
                    act.activation(w_hi[0][:, cols], w_raw[0][:, cols], ACT.Copy).then_inc(done.sem, 1)
                silu(0, 1, first=True)
                split_hi(1, layer, q[1] + 1)

                def step(j):
                    split_hi(0, layer, q[0] + j + 1)
                    for t in range(T):
                        silu(j, t)
                    split_hi(1, layer, q[1] + j + 1)
                    split_hi(2, layer, q[2] + j)

                hid_tile(0, 1)
                step(1)
                with act.Fori(2, NJ - 1) as j:
                    hid_part(j - 1)
                    step(j)
                act.wait_ge(last_in.sem, last_in.at(layer, f + 1))
                act.activation(last_hi[:, :], last_raw[:, :], ACT.Copy).then_inc(last_hi_done.sem, 1)
                gate_half(layer, stage, 0)
                hid_part(NJ - 2)
                split_hi(0, layer, q[0] + NJ)
                for t in range(T):
                    silu(NJ - 1, t)
                split_hi(1, layer, q[1] + NJ)
                hid_tile(NJ - 1, 0)
                gate_half(layer, stage, 1)
                square(layer, stage + 1, 0)
                hid_tile(NJ - 1, 1)
                if stage == FFN1:
                    split_hi(2, layer, q[2] + NJ - 1, mix_width(2))
                prepare(layer, stage + 1, 0)

            def mix(layer):
                square(layer, MIX, 1)
                prepare(layer, MIX, 1)
                for what, *arg in PLAN:
                    if what == "split_hi":
                        u = arg[0]
                        split_hi(u % NS, layer, q0[MIX][u % NS] + u // NS, mix_width(u))
                    elif what == "evac":
                        c, b = arg[0], bank_of(arg[0])
                        if c == C_QB:
                            continue
                        chunk_done(act, layer, c)
                        if c == C_LKV:
                            act.activation(lr_t[0:RANK], ps[0:RANK, b, 0:SEQ], ACT.Copy)
                            act.activation(k_t[:, :], ps[:, b, SEQ:2 * SEQ], ACT.Copy)
                            act.activation(flat(v_att[:, :, :]), ps[:, b + 1, 0:SEQ], ACT.Copy).then_inc(evac_act.sem, 1)
                        elif c == C_KB:
                            act.activation(flat(kb_t[:, :, :]), flat(ps[:, b:b + 2, :]), ACT.Copy)\
                                .then_inc(evac_act.sem, 1)
                        elif c in (C_Q, C_Q + 1):
                            g = 4 * (c - C_Q)
                            act.activation(flat(q_t[:, g:g + 4, :]), flat(ps[:, b:b + 2, :]), ACT.Copy)\
                                .then_inc(evac_act.sem, 1)
                        elif c in (C_VB0, C_VB1):
                            o = 0 if c == C_VB0 else 512
                            act.activation(vb[:, :, o:o + 512], ps[:, b:b + 2, :], ACT.Copy).then_inc(evac_act.sem, 1)
                        else:
                            n = c - C_R
                            if n:
                                act.wait_ge(th_used.sem, th_used.at(layer, n))
                            else:
                                act.wait_ge(q_ready.sem, q_ready.at(layer, 1))
                            act.activation(th_buf, ps[:, b:b + 2, :], ACT.Tanh, scale=0.5).then_inc(tanh_done.sem, 1)
                    elif what == "gate_log":
                        act.wait_ge(z_done.sem, z_done.at(layer, 1))
                        chain.link(act.activation(flat(g_cum[:, :, :]), flat(z_buf[:, :, :]), ACT.Abs))
                        chain.link(act.activation(flat(g_cum[:, :, :]), flat(g_cum[:, :, :]), ACT.Exp, scale=-1.0))
                        act.activation(flat(g_cum[:, :, :]), flat(g_cum[:, :, :]), ACT.Ln, bias=1.0)\
                            .then_inc(log_done.sem, 1)
                    elif what == "gate_exp":
                        act.wait_ge(diffs_done.sem, diffs_done.at(layer, 1))
                        act.activation(k_state[:, :, :], k_state[:, :, :], ACT.Exp, scale=1 / 16.0)\
                            .then_inc(exps_done.sem, 1)
                        act.activation(q_state[:, :, :], g_cum[:, :, P:2 * P], ACT.Exp, scale=1 / 16.0)\
                            .then_inc(exps_done.sem, 1)
                        act.wait_ge(diffs_done.sem, diffs_done.at(layer, 2))
                        act.activation(flat(z_buf[:, :, :]), flat(z_buf[:, :, :]), ACT.Exp, scale=1 / 16.0)\
                            .then_inc(exps_done.sem, 1)
                    elif what == "k_turn":
                        act.wait_ge(k_state_tr.sem, k_state_tr.at(layer, 1))
                        act.activation(k_state_t[:, :], ps[:, LIN, :], ACT.Copy).then_inc(k_state_t_done.sem, 1)
                    elif what == "state":
                        act.wait_ge(state_mm.sem, state_mm.at(layer, 1))
                        act.activation(state[:, :], flat(ps[:, LIN:LIN + 2, :]), ACT.Copy).then_inc(state_done.sem, 1)
                    elif what == "ks_diff":
                        act.wait_ge(ks_diff.sem, ks_diff.at(layer, arg[0] + 1))
                        for c in range(NC):
                            part = k_scaled[:, :, c, 0:CH * (c + 1)]
                            last = act.activation(part, part, ACT.Exp, scale=1 / 16.0)
                        last.then_inc(ks_exp.sem, 1)
                    elif what == "o":
                        r = arg[0]
                        t, hp = r // 2, 2 * (r % 2)
                        act.wait_ge(o_mm.sem, o_mm.at(layer, r + 1))
                        act.activation(vb[:, t, hp * DV:(hp + 2) * DV], ps[:, LIN + 1, :], ACT.Copy)\
                            .then_inc(lin_out.sem, 1)
                        act.wait_ge(lin_out.sem, lin_out.at(layer, r + 1))
                        for h in range(2):
                            o = ps[:, LIN + 1, h * DV:(h + 1) * DV]
                            n = t * GH + hp + h
                            last = act.activation(o, o, ACT.Square, accum_out=gla_ss[:, n:n + 1])
                        last.then_inc(lin_squared.sem, 1)
                    elif what == "head":
                        i = arg[0]
                        if i < HEADS:
                            p, h = probs[i % 2], HEAD_ORDER[i]
                            act.wait_ge(soft_ready.sem, soft_ready.at(layer, i + 1))
                            act.activation(p[:, 0:2 * P], p[:, 0:2 * P], ACT.Exp, bias=neg_max[:, h, 0:1],
                                           accum_out=row_sum[:, h, 0:1])
                            act.activation(p[:, 2 * P:3 * P], p[:, 2 * P:3 * P], ACT.Exp, bias=neg_max[:, h, 1:2],
                                           accum_out=row_sum[:, h, 1:2]).then_inc(probs_done.sem, 1)
                        if 2 <= i:
                            h = HEAD_ORDER[i - 2]
                            act.wait_ge(turned.sem, turned.at(layer, i))
                            act.activation(xn[:, :, h * DH:(h + 1) * DH],
                                           ps[:, TURNED, 3 * P:4 * P].rearrange("p (t d) -> p t d", t=T),
                                           ACT.Copy).then_inc(att_out.sem, 1)
                        if 1 <= i <= HEADS:
                            act.wait_ge(turned.sem, turned.at(layer, i))
                            act.activation(probs_t[(i - 1) % 2][:, :], ps[:, TURNED, 0:3 * P], ACT.Copy)\
                                .then_inc(probs_t_done.sem, 1)
                    elif what == "att_norm":
                        act.wait_ge(sink_diff.sem, sink_diff.at(layer, arg[0] + 1))
                        part = sink_exp[:, arg[0] * 8:(arg[0] + 1) * 8, :]
                        act.activation(part, part, ACT.Exp)\
                            .then_inc(sink_exp_done.sem, 1)
                    elif what == "merge":
                        half = arg[0]
                        act.wait_ge(mrg_tr.sem, mrg_tr.at(layer, half + 1))
                        for t in range(T):
                            last = act.activation(half_of(h_hi, t, half), as_tiles(ps[:, 2 - 2 * half + t, :]), ACT.Copy)
                        last.then_inc(mrg_hi_done.sem, 1)
                split_hi(2, layer, q0[MIX][2] + MQ - 1)
                gate_half(layer, MIX, 0)
                split_hi(0, layer, q0[FFN2][0])
                gate_half(layer, MIX, 1)
                square(layer, FFN2, 0)
                split_hi(1, layer, q0[FFN2][1])
                prepare(layer, FFN2, 0)

            act.wait_ge(const_in.sem, CONSTS * 16)
            act.activation(cond[:, :], cond[:, :], ACT.Silu).then_inc(cond_ready.sem, 1)
            square(0, 0, 0)
            split_hi(0, 0, 0)
            prepare(0, 0, 0)
            split_hi(1, 0, 0)
            with act.Fori(0, L) as layer:
                chain.enter(layer)
                ffn(layer, FFN1)
                mix(layer)
                ffn(layer, FFN2)
            chain.leave()
            square(L, 0, 1)

        @block.vector
        def _(dve):
            chain = Chain(dve, dve_chain, DVE_CHAIN)

            def split_lo(s, layer, q, width=UNIT):
                dve.wait_ge(hi_done[s].sem, hi_done[s].at(layer, q + 1))
                dve.tensor_tensor(w_lo[s][:, 0:width], w_raw[s][:, 0:width], w_hi[s][:, 0:width].bitcast(F32),
                                  ALU.subtract)\
                    .then_inc(lo_done[s].sem, 1)

            def rsqrt(y, v, tmp, sums, width):
                chain.link(dve.tensor_scalar(v, sums, 1.0 / width, EPS, ALU.mult, ALU.add))
                chain.link(dve.tensor_scalar(y.bitcast(I32), v.bitcast(I32), -0.5, RSQRT_SEED, ALU.mult, ALU.add))
                for n in range(3):
                    chain.link(dve.scalar_tensor_tensor(out=tmp, in0=y, scalar=-0.5, in1=y, op0=ALU.mult, op1=ALU.mult))
                    chain.link(dve.tensor_tensor(tmp, tmp, v, ALU.mult))
                    last = dve.scalar_tensor_tensor(out=y, in0=tmp, scalar=1.5, in1=y, op0=ALU.add, op1=ALU.mult)
                    if n < 2:
                        chain.link(last)
                return last

            def norm(layer, n, t):
                v, y = newton[:, 0, t:t + 1], rstd[:, t:t + 1]
                r = newton[:, 1, t:t + 1]
                dve.wait_ge(squared.sem, squared.at(layer, n * T + t + 1))
                chain.link(dve.tensor_scalar(v, sum_sq[:, t:t + 1], NEWTON_SCALE / D, NEWTON_SCALE * EPS,
                                             ALU.mult, ALU.add))
                chain.link(dve.tensor_scalar(y.bitcast(I32), v.bitcast(I32), -0.5, RSQRT_SEED - 2.0 ** 31,
                                             ALU.mult, ALU.add))
                for three in NEWTON_THREES:
                    chain.link(dve.scalar_tensor_tensor(out=r, in0=y, scalar=y, in1=v, op0=ALU.mult, op1=ALU.mult))
                    chain.link(dve.scalar_tensor_tensor(out=y, in0=r, scalar=three, in1=y, op0=ALU.subtract,
                                                        op1=ALU.mult))

            def norm_diag(layer, n, t):
                norm(layer, n, t)
                dve.tensor_scalar(diag[t][:, :], ident[:, :], rstd[:, t:t + 1], None, ALU.mult)\
                    .then_inc(diag_done.sem, 1)

            def modulate(layer, n, t):
                dve.wait_ge(mods_ready.sem, mods_ready.at(layer, n))
                dve.wait_ge(x_tr.sem, x_tr.at(layer, (n * T + t) * 2 + 1))
                for k in range(KA):
                    last = dve.tensor_scalar(xn[:, t, k * P:(k + 1) * P], ps[:, 2 * t, k * P:(k + 1) * P],
                                             mod_scale[:, k:k + 1], mod_shift[:, k:k + 1], ALU.mult, ALU.add)
                last.then_inc(h_mod_dve.sem, 1)

            def second_part(layer, n, t, half):
                dve.wait_ge(h_hi_done.sem, h_hi_done.at(layer, (n * T + t) * 2 + half + 1))
                dve.tensor_tensor(half_of(h_lo, t, half), as_tiles(xn[:, t, half * 512:(half + 1) * 512]),
                                  half_of(h_hi, t, half).bitcast(F32), ALU.subtract).then_inc(h_ready.sem, 1)

            def prepare(layer, n, t):
                modulate(layer, n, t)
                for half in range(2):
                    second_part(layer, n, t, half)

            def gate_y(layer, stage, t):
                if t == 0:
                    dve.wait_ge(gate_row_done.sem, gate_row_done.at(layer, 2 * stage + 2))
                    dve.wait_ge(y0_done.sem, y0_done.at(layer, stage + 1))
                elif stage == MIX:
                    dve.wait_ge(used[2].sem, used[2].at(layer, q0[MIX][2] + MQ))
                else:
                    dve.wait_ge(last_used.sem, last_used.at(layer, ffn_no[stage] + 1))
                chain.link(dve.tensor_tensor(xn[:, t, :], flat(ps[:, Y + 2 * t:Y + 2 * t + 2, :]), gate_row[:, :],
                                             ALU.mult))

            def add_to_x(t):
                dve.tensor_tensor(x[:, t, :], x[:, t, :], xn[:, t, :], ALU.add).then_inc(x_ready.sem, 1)

            def next_stage(layer, stage):
                take_mods(layer, stage, layer * 3 + (stage + 1))
                modulate(layer, stage + 1, 0)
                second_part(layer, stage + 1, 0, 0)
                gate_y(layer, stage, 1)
                second_part(layer, stage + 1, 0, 1)
                add_to_x(1)

            def add_ada(layer, stage, k, vectors=(0, 1, 2)):
                n = stage * KD + k
                dve.wait_ge(ada_in.sem, ada_in.at(layer, n + 1))
                dve.wait_ge(ada_used.sem, ada_used.at(layer, n))
                col = cond[:, k:k + 1] if isinstance(k, int) else cond[:, bass.ds(k, 1)]
                for m in vectors:
                    last = dve.scalar_tensor_tensor(out=ada_acc[:, m, :], in0=ada_raw[:, m * D:(m + 1) * D], scalar=col,
                                                    in1=ada_acc[:, m, :], op0=ALU.mult, op1=ALU.add)
                if 2 in vectors:
                    last.then_inc(ada_used.sem, 1)

            def take_mods(layer, stage, n_gain):
                dve.wait_ge(cols_sum.sem, cols_sum.at(layer, stage + 1))
                dve.tensor_copy(mod_shift[:, :], ps[:, SUMS, 0:KD])
                gain = gain_cols[:, n_gain:n_gain + 1, :] if isinstance(n_gain, int) else gain_cols[:, bass.ds(n_gain, 1), :]
                dve.scalar_tensor_tensor(out=mod_scale[:, :], in0=ps[:, SUMS, KD:2 * KD], scalar=1.0,
                                         in1=flat(gain), op0=ALU.add, op1=ALU.mult).then_inc(mods_ready.sem, 1)

            def ffn(layer, stage):
                q, f = q0[stage], ffn_no[stage]
                def hid_part(j):
                    dve.wait_ge(hid_hi_done.sem, hid_hi_done.at(layer, hid_no(f, j)))
                    dve.tensor_tensor(flat(hid_lo[:, :, :]), ps[:, HID, :], flat(hid_hi[:, :, :]).bitcast(F32),
                                      ALU.subtract).then_inc(hid_ready.sem, 1)

                def hid_tile(j, t):
                    dve.wait_ge(hid_hi_done.sem, hid_hi_done.at(layer, hid_no(f, j, t)))
                    rows = (slice(None), slice(None), slice(t * P, (t + 1) * P))
                    dve.tensor_tensor(hid_lo[rows], hid_bank(j, t), hid_hi[rows].bitcast(F32), ALU.subtract)\
                        .then_inc(hid_ready.sem, 1)

                def gated(j, t):
                    dve.wait_ge(silu_done.sem, silu_done.at(layer, (f * NJ + j) * T + t + 1))
                    dve.tensor_tensor(hidden[:, t, :], silu_g[:, t, :], ps[:, t, FC:2 * FC], ALU.mult)\
                        .then_inc(hidden_done.sem, 1)

                def step(j):
                    split_lo(0, layer, q[0] + j + 1)
                    for t in range(T):
                        gated(j, t)
                    split_lo(1, layer, q[1] + j + 1)
                    split_lo(2, layer, q[2] + j)

                norm_diag(layer, stage, 1)
                gated(0, 0)
                split_lo(2, layer, q[2])
                hid_tile(0, 0)
                prepare(layer, stage, 1)
                for m in range(3):
                    dve.wait_ge(seeded[m].sem, seeded[m].at(layer, stage + 1))
                for half in range(2):
                    if half == 0:
                        dve.wait_ge(half_hi_done.sem, half_hi_done.at(layer, f + 1))
                    else:
                        dve.wait_ge(hi_done[0].sem, hi_done[0].at(layer, q[0] + 2))
                    cols = slice(half * UNIT // 2, (half + 1) * UNIT // 2)
                    last = dve.tensor_tensor(w_lo[0][:, cols], w_raw[0][:, cols], w_hi[0][:, cols].bitcast(F32),
                                             ALU.subtract)
                last.then_inc(lo_done[0].sem, 1)
                gated(0, 1)
                split_lo(1, layer, q[1] + 1)
                add_ada(layer, stage, 0)
                hid_tile(0, 1)
                step(1)
                add_ada(layer, stage, 1)
                with dve.Fori(2, KD) as j:
                    hid_part(j - 1)
                    step(j)
                    add_ada(layer, stage, j)
                with dve.Fori(KD, NJ - 1) as j:
                    hid_part(j - 1)
                    step(j)
                dve.wait_ge(last_hi_done.sem, last_hi_done.at(layer, f + 1))
                dve.tensor_tensor(last_lo[:, :], last_raw[:, :], last_hi[:, :].bitcast(F32), ALU.subtract)\
                    .then_inc(last_lo_done.sem, 1)
                hid_part(NJ - 2)
                split_lo(0, layer, q[0] + NJ)
                for t in range(T):
                    gated(NJ - 1, t)
                hid_tile(NJ - 1, 0)
                split_lo(1, layer, q[1] + NJ)
                gate_y(layer, stage, 0)
                add_to_x(0)
                norm_diag(layer, stage + 1, 0)
                hid_tile(NJ - 1, 1)
                next_stage(layer, stage)

            def mix(layer):
                norm_diag(layer, MIX, 1)
                prepare(layer, MIX, 1)
                for m in range(3):
                    dve.wait_ge(seeded[m].sem, seeded[m].at(layer, MIX + 1))
                dve.wait_ge(layer_in.sem, layer_in.at(layer, 4))
                chain.link(dve.tensor_scalar(gla_gain_row[:, :], gla_gain_row[:, :], 0.25, None, ALU.mult))

                for what, *arg in PLAN:
                    if what == "split_lo":
                        u = arg[0]
                        split_lo(u % NS, layer, q0[MIX][u % NS] + u // NS, mix_width(u))
                    elif what == "ada":
                        add_ada(layer, MIX, *arg)
                    elif what == "evac":
                        c, b = arg[0], bank_of(arg[0])
                        if c == C_QB:
                            chunk_done(dve, layer, c)
                            dve.tensor_scalar(flat(qb_t[:, :, :]), flat(ps[:, b:b + 2, :]), DK ** -0.5, None, ALU.mult)\
                                .then_inc(evac_dve.sem, 1)
                        if c < C_R:
                            continue
                        n, o = c - C_R, 512 * ((c - C_R) % 2)
                        cols = (slice(None), slice(None), slice(o, o + 512))
                        dve.wait_ge(tanh_done.sem, tanh_done.at(layer, n + 1))
                        if c < C_GB:
                            dve.scalar_tensor_tensor(out=w_gates[cols], in0=th_buf, scalar=1.0, in1=ps[:, b:b + 2, :],
                                                     op0=ALU.add, op1=ALU.mult).then_inc(th_used.sem, 1)
                        elif c < C_GA:
                            dve.scalar_tensor_tensor(out=w_gates[cols], in0=th_buf, scalar=1.0, in1=w_gates[cols],
                                                     op0=ALU.add, op1=ALU.mult).then_inc(th_used.sem, 1)
                        else:
                            dve.scalar_tensor_tensor(out=xn[cols], in0=th_buf, scalar=1.0, in1=xn[cols],
                                                     op0=ALU.add, op1=ALU.mult).then_inc(th_used.sem, 1)
                            dve.wait_ge(th_used.sem, th_used.at(layer, n + 1))
                            dve.tensor_tensor(xn[cols], xn[cols], vb[cols], ALU.add).then_inc(merged.sem, 1)
                    elif what == "gate_z":
                        dve.wait_ge(z_mm.sem, z_mm.at(layer, 1))
                        for h in range(GH):
                            last = dve.tensor_scalar(z_buf[:, h, :], ps[:, LIN + h // 2, (h % 2) * SEQ:(h % 2 + 1) * SEQ],
                                                     gate_bias[:, h:h + 1], None, ALU.add)
                        last.then_inc(z_done.sem, 1)
                    elif what == "gate_log":
                        dve.wait_ge(log_done.sem, log_done.at(layer, 1))
                        chain.link(dve.scalar_tensor_tensor(out=flat(z_buf[:, :, :]), in0=flat(z_buf[:, :, :]), scalar=0.0,
                                                            in1=flat(g_cum[:, :, :]), op0=ALU.min, op1=ALU.subtract))
                        for h in range(GH):
                            for t in range(T):
                                tile = (slice(None), h, slice(t * P, (t + 1) * P))
                                last = dve.tensor_tensor_scan(g_cum[tile], ones[:, :], z_buf[tile], 0.0,
                                                              op0=ALU.mult, op1=ALU.add)
                        chain.link(last)
                        dve.tensor_tensor(k_state[:, :, :], g_cum[:, :, P - 1:P].broadcast_to([P, GH, P]),
                                          g_cum[:, :, 0:P], ALU.subtract).then_inc(diffs_done.sem, 1)
                        by_chunk = flat(g_cum[:, :, :]).rearrange("p (c i) -> p c i", i=CH)
                        dve.tensor_tensor(flat(z_buf[:, :, :]).rearrange("p (c i) -> p c i", i=CH), by_chunk,
                                          by_chunk[:, :, 0:1].broadcast_to([P, GH * SEQ // CH, CH]),
                                          ALU.subtract).then_inc(diffs_done.sem, 1)
                    elif what == "gate_exp":
                        dve.wait_ge(exps_done.sem, exps_done.at(layer, 1))
                        dve.wait_ge(evac_act.sem, evac_act.at(layer, C_KB + 1))
                        dve.tensor_tensor(k_state[:, :, :], k_state[:, :, :], kb_t[:, :, 0:P], ALU.mult)\
                            .then_inc(k_state_done.sem, 1)
                    elif what == "q_exp":
                        dve.wait_ge(exps_done.sem, exps_done.at(layer, 2))
                        dve.wait_ge(evac_dve.sem, evac_dve.at(layer, 1))
                        chain.link(dve.tensor_tensor(q_state[:, :, :], q_state[:, :, :], qb_t[:, :, P:2 * P], ALU.mult))
                        dve.wait_ge(exps_done.sem, exps_done.at(layer, 3))
                        dve.tensor_tensor(flat(qb_t[:, :, :]), flat(qb_t[:, :, :]), flat(z_buf[:, :, :]), ALU.mult)\
                            .then_inc(q_ready.sem, 1)
                    elif what == "ks_diff":
                        r = arg[0]
                        t, hp = r // 2, 2 * (r % 2)
                        if r:
                            dve.wait_ge(a_mm.sem, a_mm.at(layer, r))
                        else:
                            dve.wait_ge(keys_cleared.sem, 1)
                        for c in range(NC):
                            n = CH * (c + 1)
                            at = t * P + c * CH
                            last = dve.tensor_tensor(k_scaled[:, :, c, 0:n],
                                                     g_cum[:, hp:hp + 2, at:at + 1].broadcast_to([P, 2, n]),
                                                     g_cum[:, hp:hp + 2, t * P:t * P + n], ALU.subtract)
                        last.then_inc(ks_diff.sem, 1)
                    elif what == "ks_mul":
                        r = arg[0]
                        t, hp = r // 2, 2 * (r % 2)
                        dve.wait_ge(ks_exp.sem, ks_exp.at(layer, r + 1))
                        for c in range(NC):
                            n = CH * (c + 1)
                            last = dve.tensor_tensor(k_scaled[:, :, c, 0:n], k_scaled[:, :, c, 0:n],
                                                     kb_t[:, hp:hp + 2, t * P:t * P + n], ALU.mult)
                        last.then_inc(ks_ready.sem, 1)
                    elif what == "a":
                        r = arg[0]
                        hp = 2 * (r % 2)
                        dve.wait_ge(a_mm.sem, a_mm.at(layer, r + 1))
                        if r >= 2:
                            dve.wait_ge(o_mm.sem, o_mm.at(layer, r - 1))
                        dve.tensor_tensor(a_t[:, hp:hp + 2, :], ps[:, LIN, 0:2 * P].rearrange("p (h i) -> p h i", h=2),
                                          gla_mask[:, :].rearrange("p (a i) -> p a i", a=1).broadcast_to([P, 2, P]),
                                          ALU.mult).then_inc(a_ready.sem, 1)
                    elif what == "lin_rms":
                        t = arg[0]
                        heads = slice(t * GH, (t + 1) * GH)
                        dve.wait_ge(lin_squared.sem, lin_squared.at(layer, 2 * t + 2))
                        chain.link(rsqrt(gla_rstd[:, heads], gla_nt[:, 0, heads], gla_nt[:, 1, heads], gla_ss[:, heads], DV))
                    elif what == "lin_norm":
                        t = arg[0]
                        dve.wait_ge(gain_done.sem, gain_done.at(layer, 2))
                        for h in range(GH):
                            o, w = (b[:, t, h * DV:(h + 1) * DV] for b in (vb, w_gates))
                            last = dve.scalar_tensor_tensor(out=o, in0=o, scalar=gla_rstd[:, t * GH + h:t * GH + h + 1],
                                                            in1=w, op0=ALU.mult, op1=ALU.mult)
                        chain.link(last)
                    elif what == "head" and arg[0] < HEADS:
                        i = arg[0]
                        p, h = probs[i % 2], HEAD_ORDER[i]
                        dve.wait_ge(scores_mm.sem, scores_mm.at(layer, i + 1))
                        if i >= 2:
                            dve.wait_ge(turned.sem, turned.at(layer, i - 1))
                        dve.scalar_tensor_tensor(out=p[:, :], in0=ps[:, SCORES, 0:3 * P], scalar=DH ** -0.5,
                                                 in1=att_mask[:, :], op0=ALU.mult, op1=ALU.add)\
                            .then_inc(scores_read.sem, 1)
                        dve.wait_ge(scores_read.sem, scores_read.at(layer, i + 1))
                        dve.tensor_reduce(row_max[:, 0:1], p[:, 0:2 * P], AX_X, ALU.max)
                        chain.link(dve.tensor_reduce(row_max[:, 1:2], p[:, 2 * P:3 * P], AX_X, ALU.max))
                        dve.tensor_scalar(neg_max[:, h, :], row_max[:, :], sink_rows[:, h:h + 1], -1.0, ALU.max, ALU.mult)\
                            .then_inc(soft_ready.sem, 1)
                    elif what == "att_norm":
                        heads = slice(arg[0] * 8, (arg[0] + 1) * 8)
                        done = 12 if arg[0] == 0 else HEADS
                        sinks_twice = sink_rows[:, heads].rearrange("p (h t) -> p h t", t=1).broadcast_to([P, 8, 2])
                        part = sink_exp[:, heads, :]
                        dve.wait_ge(soft_ready.sem, soft_ready.at(layer, done))
                        dve.tensor_tensor(part, neg_max[:, heads, :], sinks_twice, ALU.add).then_inc(sink_diff.sem, 1)
                        dve.wait_ge(sink_exp_done.sem, sink_exp_done.at(layer, arg[0] + 1))
                        chain.link(dve.tensor_tensor(part, row_sum[:, heads, :], part, ALU.add))
                        chain.link(dve.reciprocal(part, part))
                        chain.link(dve.tensor_scalar(part, part, 0.5, None, ALU.mult))
                        dve.wait_ge(att_out.sem, att_out.at(layer, done))
                        for t in range(T):
                            y = xn[:, t, arg[0] * 512:(arg[0] + 1) * 512].rearrange("p (h d) -> p h d", d=DH)
                            last = dve.tensor_tensor(y, y, sink_exp[:, heads, 1 - t:2 - t].broadcast_to([P, 8, DH]), ALU.mult)
                        chain.link(last)
                    elif what == "merge":
                        half = arg[0]
                        dve.wait_ge(mrg_hi_done.sem, mrg_hi_done.at(layer, half + 1))
                        for t in range(T):
                            last = dve.tensor_tensor(half_of(h_lo, t, half), as_tiles(ps[:, 2 - 2 * half + t, :]),
                                                     half_of(h_hi, t, half).bitcast(F32), ALU.subtract)
                        last.then_inc(mrg_ready.sem, 1)
                split_lo(2, layer, q0[MIX][2] + MQ - 1)
                split_lo(0, layer, q0[FFN2][0])
                gate_y(layer, MIX, 0)
                add_to_x(0)
                norm_diag(layer, FFN2, 0)
                split_lo(1, layer, q0[FFN2][1])
                next_stage(layer, MIX)

            dve.memset(ada_acc[:, 1:3, :], 0.0).then_inc(first_cleared.sem, 1)
            for s in range(NS):
                dve.nop().then_inc(lo_done[s].sem, 1)
            dve.nop().then_inc(ada_used.sem, 1)
            dve.wait_ge(const_in.sem, CONSTS * 16)
            for t in range(T):
                dve.nop().then_inc(x_ready.sem, 1)
            dve.wait_ge(made.sem, MADE)
            norm_diag(0, 0, 0)
            dve.wait_ge(cond_ready.sem, 1)
            for k in range(KD):
                dve.wait_ge(stage_in[k].sem, 16)
                if k:
                    dve.wait_ge(stage_used.sem, k)
                for m in (1, 2):
                    last = dve.scalar_tensor_tensor(out=ada_acc[:, m, :], in0=ada_stage[k][:, (m - 1) * D:m * D],
                                                    scalar=cond[:, k:k + 1], in1=ada_acc[:, m, :],
                                                    op0=ALU.mult, op1=ALU.add)
                last.then_inc(stage_used.sem, 1)
            split_lo(0, 0, 0)
            take_mods(0, -1, 0)
            prepare(0, 0, 0)
            split_lo(1, 0, 0)
            with dve.Fori(0, L) as layer:
                chain.enter(layer)
                ffn(layer, FFN1)
                mix(layer)
                ffn(layer, FFN2)
            chain.leave()
            dve.wait_ge(const_in.sem, (CONSTS + 1) * 16)
            dve.wait_ge(h_ready.sem, h_ready.at(L, 2))
            for t in range(T):
                if t:
                    norm(L, 0, t)
                for half in range(2):
                    cols = slice(half * D // 2, (half + 1) * D // 2)
                    dve.scalar_tensor_tensor(out=xn[:, t, cols], in0=x[:, t, cols], scalar=rstd[:, t:t + 1],
                                             in1=ada_raw[:, cols], op0=ALU.mult, op1=ALU.mult).then_inc(final_done.sem, 1)

        @block.tensor
        def _(pe):
            def product(o, lhs, rhs, start, stop, shared=False):
                for n, (a, b) in enumerate(((0, 0), (1, 0), (0, 1))):
                    last = pe.matmul(o, lhs[a], rhs[b], start=start and n == 0, stop=stop and n == 2,
                                     skip_group_check=shared)
                return last

            def unit_ready(s, layer, q):
                pe.wait_ge(lo_done[s].sem, lo_done[s].at(layer, q + 1))

            def prepare(layer, n, t):
                pe.wait_ge(diag_done.sem, diag_done.at(layer, n * T + t + 1))
                for half in range(2):
                    for k in range(KA):
                        o = (half * KA + k) * P
                        last = pe.matmul(ps[:, 2 * t + half, k * P:(k + 1) * P], x[:, t, o:o + P], diag[t][:, :],
                                         start=True, stop=True)
                    last.then_inc(x_tr.sem, 1)

            def h_is_ready(layer, n, t, half):
                pe.wait_ge(h_ready.sem, h_ready.at(layer, (n * T + t) * 2 + half + 1))

            def h_tile(k, t):
                return [part[:, k, t * P:(t + 1) * P] for part in (h_hi, h_lo)]

            def w_cols(s, a, b):
                return [part[s][:, a:b] for part in (w_hi, w_lo)]

            def down(t, parts, w, k0, start, stop, sums=False):
                for k in range(2):
                    for n in range(2):
                        if sums:
                            sum_cols(2 * k + n)
                        o = (2 * k + n) * 512
                        last = product(ps[:, Y + 2 * t + n, :], [a[:, k0 + k, t * P:(t + 1) * P] for a in parts],
                                       [part[:, o:o + 512] for part in w], start=start and k == 0, stop=stop and k == 1)
                return last

            def sum_gate(layer, stage, half):
                if half:
                    pe.wait_ge(gate_row_done.sem, gate_row_done.at(layer, 2 * stage + 1))
                else:
                    pe.wait_ge(ada_used.sem, ada_used.at(layer, (stage + 1) * KD))
                pe.matmul(ps[:, SUMS, :], ones[:, :], ada_acc[:, 0, half * 512:(half + 1) * 512], start=True, stop=True)\
                    .then_inc(gate_sum.sem, 1)

            def sum_cols(quarter):
                for i in range(quarter * KD // 2, (quarter + 1) * KD // 2):
                    m, k = 1 + i // KD, i % KD
                    last = pe.matmul(ps[:, SUMS, i:i + 1], ada_acc[:, m, k * P:(k + 1) * P], ones[:, 0:1],
                                     start=True, stop=True)
                if quarter == 3:
                    last.then_inc(cols_sum.sem, 1)

            def ffn(layer, stage):
                q, f = q0[stage], ffn_no[stage]

                def up(j, half, t):
                    for k in range(KA):
                        last = product(ps[:, t, :], h_tile(half * KA + k, t), w_cols(half, k * 512, (k + 1) * 512),
                                       start=half == 0 and k == 0, stop=half == 1 and k == KA - 1)
                    if t == 1:
                        last.then_inc(used[half].sem, 1)
                    elif half == 1:
                        last.then_inc(gu0_done.sem, 1)

                def up0(j):
                    unit_ready(0, layer, q[0] + j)
                    for t in range(T):
                        pe.wait_ge(hidden_done.sem, hidden_done.at(layer, (f * NJ + j) * T + t + 1 - T))
                        up(j, 0, t)

                def up1(j):
                    unit_ready(1, layer, q[1] + j)
                    for t in range(T):
                        up(j, 1, t)

                def turn(j, t, bank=HID):
                    pe.wait_ge(hidden_done.sem, hidden_done.at(layer, (f * NJ + j) * T + t + 1))
                    for k in range(2):
                        last = pe.transpose(ps[:, bank, k * SEQ + t * P:k * SEQ + (t + 1) * P],
                                            hidden[:, t, k * P:(k + 1) * P], ident[:, :])
                    return last

                def turns(j):
                    turn(j, 0)
                    turn(j, 1).then_inc(hid_tr.sem, 1)

                def hid_is_ready(j, t=1):
                    pe.wait_ge(hid_ready.sem, hid_ready.at(layer, hid_no(f, j, t)))

                def downs(j):
                    hid_is_ready(j)
                    unit_ready(2, layer, q[2] + j)
                    for t in range(T):
                        last = down(t, (hid_hi, hid_lo), (w_hi[2], w_lo[2]), 0, False, False)
                    last.then_inc(used[2].sem, 1)

                for half in range(2):
                    unit_ready(half, layer, q[half])
                    h_is_ready(layer, stage, 0, half)
                    up(0, half, 0)
                prepare(layer, stage, 1)
                turn(0, 0, bank=1).then_inc(hid_tr.sem, 1)
                unit_ready(2, layer, q[2])
                hid_is_ready(0, 0)
                down(0, (hid_hi, hid_lo), (w_hi[2], w_lo[2]), 0, True, False)
                for half in range(2):
                    h_is_ready(layer, stage, 1, half)
                    up(0, half, 1)
                up0(1)
                turn(0, 1).then_inc(hid_tr.sem, 1)
                up1(1)
                hid_is_ready(0, 1)
                down(1, (hid_hi, hid_lo), (w_hi[2], w_lo[2]), 0, True, False).then_inc(used[2].sem, 1)
                with pe.Fori(2, NJ - 1) as j:
                    up0(j)
                    turns(j - 1)
                    up1(j)
                    downs(j - 1)
                up0(NJ - 1)
                sum_gate(layer, stage, 0)
                turns(NJ - 2)
                up1(NJ - 1)
                hid_is_ready(NJ - 2)
                turn(NJ - 1, 0).then_inc(hid_tr.sem, 1)
                unit_ready(2, layer, q[2] + NJ - 2)
                down(0, (hid_hi, hid_lo), (w_hi[2], w_lo[2]), 0, False, False).then_inc(down_t0.sem, 1)
                sum_gate(layer, stage, 1)
                pe.wait_ge(last_lo_done.sem, last_lo_done.at(layer, f + 1))
                hid_is_ready(NJ - 1, 0)
                down(0, (hid_hi, hid_lo), (last_hi, last_lo), 0, False, True).then_inc(y0_done.sem, 1)
                pe.wait_ge(gate_row_done.sem, gate_row_done.at(layer, 2 * stage + 2))
                down(1, (hid_hi, hid_lo), (w_hi[2], w_lo[2]), 0, False, False, sums=True).then_inc(used[2].sem, 1)
                turn(NJ - 1, 1).then_inc(hid_tr.sem, 1)
                prepare(layer, stage + 1, 0)
                hid_is_ready(NJ - 1, 1)
                down(1, (hid_hi, hid_lo), (last_hi, last_lo), 0, False, True).then_inc(last_used.sem, 1)

            def evacuated(layer, c):
                if c == C_QB:
                    pe.wait_ge(evac_dve.sem, evac_dve.at(layer, 1))
                elif c < C_R:
                    pe.wait_ge(evac_act.sem, evac_act.at(layer, c + 1))
                elif c < C_GB:
                    pe.wait_ge(th_used.sem, th_used.at(layer, c - C_R + 1))
                else:
                    pe.wait_ge(tanh_done.sem, tanh_done.at(layer, c - C_R + 1))

            def turn_merged(layer, half):
                pe.wait_ge(merged.sem, merged.at(layer, half + 1))
                for t in range(T):
                    for k in range(KA):
                        last = pe.transpose(ps[:, 2 - 2 * half + t, k * P:(k + 1) * P],
                                            xn[:, t, half * 512 + k * P:half * 512 + (k + 1) * P], ident[:, :])
                last.then_inc(mrg_tr.sem, 1)

            def unit(layer, u, tiles=(0, 1)):
                c, half, s, b = u // 2, u % 2, u % NS, bank_of(u // 2)
                unit_ready(s, layer, q0[MIX][s] + u // NS)
                if half == 0 and c >= 2:
                    evacuated(layer, c - 2)
                first, last_k = half == 0, KA - 1
                if c == C_LKV:
                    for n, (o, a) in enumerate(((ps[:, b, 0:SEQ], 0), (ps[:, b, SEQ:2 * SEQ], RANK))):
                        for k in range(KA):
                            product(o, w_cols(s, k * QKV0 + a, k * QKV0 + a + P),
                                    [part[:, half * KA + k, :] for part in (h_hi, h_lo)],
                                    start=first and k == 0 and n == 0, stop=half == 1 and k == last_k, shared=True)
                    for t in range(T):
                        for k in range(KA):
                            last = product(ps[:, b + 1, t * P:(t + 1) * P], h_tile(half * KA + k, t),
                                           w_cols(s, k * QKV0 + RANK + P, (k + 1) * QKV0),
                                           start=first and k == 0 and t == 0, stop=half == 1 and k == last_k, shared=True)
                elif c in TRANSPOSED:
                    for g in range(4):
                        for k in range(KA):
                            last = product(ps[:, b + g // 2, (g % 2) * SEQ:(g % 2 + 1) * SEQ],
                                           w_cols(s, k * 512 + g * P, k * 512 + (g + 1) * P),
                                           [part[:, half * KA + k, :] for part in (h_hi, h_lo)],
                                           start=first and k == 0 and g % 2 == 0, stop=half == 1 and k == last_k,
                                           shared=True)
                else:
                    for t in tiles:
                        if t == 1 and u == 2 * N_CHUNK - 1:
                            turn_merged(layer, 0)
                        for k in range(KA):
                            last = product(ps[:, b + t, :], h_tile(half * KA + k, t), w_cols(s, k * 512, (k + 1) * 512),
                                           start=first and k == 0, stop=half == 1 and k == last_k)
                if 1 in tiles:
                    last.then_inc(used[s].sem, 1)

            def head(layer, i):
                if i < HEADS:
                    h = HEAD_ORDER[i]
                    pe.wait_ge(evac_act.sem, evac_act.at(layer, C_Q + 1 + h % GROUP // 4))
                    if i >= 1:
                        pe.wait_ge(scores_read.sem, scores_read.at(layer, i))
                    rows, g = slice((h // GROUP) * DH, (h // GROUP + 1) * DH), h % GROUP
                    pe.matmul(ps[:, SCORES, 0:SEQ], q_t[rows, g, P:2 * P], k_t[rows, 0:SEQ], start=True, stop=True)
                    pe.matmul(ps[:, SCORES, SEQ:SEQ + P], q_t[rows, g, 0:P], k_t[rows, 0:P], start=True, stop=True)\
                        .then_inc(scores_mm.sem, 1)
                if i >= 2:
                    n = i - 2
                    p, v0 = probs_t[n % 2], (HEAD_ORDER[n] // GROUP) * DH
                    pe.wait_ge(probs_t_done.sem, probs_t_done.at(layer, n + 1))
                    if n >= 1:
                        pe.wait_ge(att_out.sem, att_out.at(layer, n))
                    o = [ps[:, TURNED, 3 * P + t * DH:3 * P + (t + 1) * DH] for t in range(T)]
                    pe.matmul(o[0], p[:, 2 * P:3 * P], v_att[:, 0, v0:v0 + DH], start=True, stop=True)
                    pe.matmul(o[1], p[:, 0:P], v_att[:, 0, v0:v0 + DH], start=True, stop=False)
                    last = pe.matmul(o[1], p[:, P:2 * P], v_att[:, 1, v0:v0 + DH], start=False, stop=True)
                if 1 <= i <= HEADS:
                    pe.wait_ge(probs_done.sem, probs_done.at(layer, i))
                    if i >= 2:
                        pe.wait_ge(probs_t_done.sem, probs_t_done.at(layer, i - 1))
                    for n in range(3):
                        last = pe.transpose(ps[:, TURNED, n * P:(n + 1) * P], probs[(i - 1) % 2][:, n * P:(n + 1) * P],
                                            ident[:, :])
                if i >= 1:
                    last.then_inc(turned.sem, 1)

            def mix(layer):
                for t in range(T):
                    if t == 1:
                        prepare(layer, MIX, 1)
                    for half in range(2):
                        h_is_ready(layer, MIX, t, half)
                        unit(layer, half, (t,))
                for what, *arg in PLAN:
                    if what == "unit" and arg[0] >= 2:
                        unit(layer, arg[0])
                    elif what == "gate_z":
                        pe.wait_ge(evac_act.sem, evac_act.at(layer, C_LKV + 1))
                        pe.wait_ge(layer_in.sem, layer_in.at(layer, 4))
                        for h in range(GH):
                            last = pe.matmul(ps[:, LIN + h // 2, (h % 2) * SEQ:(h % 2 + 1) * SEQ],
                                             gate_weight[:, h * DK:(h + 1) * DK], lr_t[0:RANK], start=True, stop=True)
                        last.then_inc(z_mm.sem, 1)
                    elif what == "k_turn":
                        pe.wait_ge(k_state_done.sem, k_state_done.at(layer, 1))
                        for h in range(GH):
                            last = pe.transpose(ps[:, LIN, h * P:(h + 1) * P], k_state[:, h, :], ident[:, :])
                        last.then_inc(k_state_tr.sem, 1)
                    elif what == "state":
                        pe.wait_ge(k_state_t_done.sem, k_state_t_done.at(layer, 1))
                        pe.wait_ge(evac_act.sem, evac_act.at(layer, C_VB1 + 1))
                        for h in range(GH):
                            last = pe.matmul(ps[:, LIN + h // 2, (h % 2) * DV:(h % 2 + 1) * DV],
                                             k_state_t[:, h * DK:(h + 1) * DK], vb[:, 0, h * DV:(h + 1) * DV],
                                             start=True, stop=True)
                        last.then_inc(state_mm.sem, 1)
                    elif what == "a":
                        r = arg[0]
                        t, hp = r // 2, 2 * (r % 2)
                        pe.wait_ge(ks_ready.sem, ks_ready.at(layer, r + 1))
                        if r == 0:
                            pe.wait_ge(state_done.sem, state_done.at(layer, 1))
                            pe.wait_ge(q_ready.sem, q_ready.at(layer, 1))
                        else:
                            pe.wait_ge(a_ready.sem, a_ready.at(layer, r))
                        for h in range(2):
                            for c in range(NC):
                                last = pe.matmul(ps[:, LIN, h * P + c * CH:h * P + (c + 1) * CH],
                                                 k_scaled[:, h, c, :],
                                                 qb_t[:, hp + h, t * P + c * CH:t * P + (c + 1) * CH],
                                                 start=True, stop=True)
                        last.then_inc(a_mm.sem, 1)
                    elif what == "o":
                        r = arg[0]
                        t, hp = r // 2, 2 * (r % 2)
                        pe.wait_ge(a_ready.sem, a_ready.at(layer, r + 1))
                        if r:
                            pe.wait_ge(lin_squared.sem, lin_squared.at(layer, r))
                        for h in range(2):
                            o = ps[:, LIN + 1, h * DV:(h + 1) * DV]
                            last = pe.matmul(o, a_t[:, hp + h, :], vb[:, t, (hp + h) * DV:(hp + h + 1) * DV],
                                             start=True, stop=t == 0)
                            if t:
                                last = pe.matmul(o, q_state[:, hp + h, :], state[:, (hp + h) * DV:(hp + h + 1) * DV],
                                                 start=False, stop=True)
                        last.then_inc(o_mm.sem, 1)
                    elif what == "head":
                        head(layer, arg[0])

                def out_unit(n, tiles):
                    u = 2 * N_CHUNK + n
                    unit_ready(u % NS, layer, q0[MIX][u % NS] + u // NS)
                    for t in tiles:
                        last = down(t, (h_hi, h_lo), (w_hi[u % NS], w_lo[u % NS]), 2 * n, n == 0, n == KD // 2 - 1)
                        if t == 1:
                            last.then_inc(used[u % NS].sem, 1)
                    return last

                pe.wait_ge(mrg_ready.sem, mrg_ready.at(layer, 1))
                out_unit(0, (0, 1))
                turn_merged(layer, 1)
                out_unit(1, (0, 1))
                sum_gate(layer, MIX, 0)
                pe.wait_ge(mrg_ready.sem, mrg_ready.at(layer, 2))
                out_unit(2, (0,))
                sum_gate(layer, MIX, 1)
                out_unit(3, (0,)).then_inc(y0_done.sem, 1)
                pe.wait_ge(gate_row_done.sem, gate_row_done.at(layer, 2 * MIX + 2))
                out_unit(2, (1,))
                for quarter in range(4):
                    sum_cols(quarter)
                prepare(layer, FFN2, 0)
                out_unit(3, (1,))

            for s in range(NS):
                pe.nop().then_inc(used[s].sem, 1)
            pe.wait_ge(made.sem, MADE)
            prepare(0, 0, 0)
            pe.wait_ge(stage_used.sem, KD)
            for quarter in range(4):
                sum_cols(quarter)
            with pe.Fori(0, L) as layer:
                ffn(layer, FFN1)
                mix(layer)
                ffn(layer, FFN2)


def kernel(**inputs):
    import numpy as np
    import concourse.bacc as bacc
    from concourse.bass_utils import run_bass_kernel_spmd

    a = {k: np.asarray(v) for k, v in inputs.items()}

    def tiles(w):
        return w.reshape(w.shape[0] // P, P, w.shape[1]).transpose(1, 0, 2)

    stream = [np.zeros((L * n + 1, P, UNIT), np.float32) for n in NSEQ]
    last = np.empty((L * 2, P, UNIT), np.float32)
    sizes = (HEADS * DH, 2 * DH, 2 * DH, GH * DK, GH * DK, GH * DV, RANK, GH * DV, D, D)
    at = [0]
    for n in sizes:
        at.append(at[-1] + n)
    qa, ka, va, qb, kb, vb, lr, r, ga, gb = (np.arange(s, s + n) for s, n in zip(at, sizes))
    pairs = qa.reshape(2, GROUP, DH).transpose(1, 0, 2).reshape(-1)
    chunks = [vb[:512], np.concatenate([lr, ka, va]), pairs[:512], pairs[512:], vb[512:], kb, qb,
              r[:512], r[512:], gb[:512], gb[512:], ga[:512], ga[512:]]
    for layer in range(L):
        base = [layer * n for n in NSEQ]
        for f, (w_in, w_out) in enumerate((("ffn1_w_in", "ffn1_w_out"), ("ffn2_w_in", "ffn2_w_out"))):
            up = tiles(a[w_in][layer]).reshape(P, KD, 2, NJ, FC)
            dn = tiles(a[w_out][layer])
            first = [b + f * (n + MQ) for b, n in zip(base, FFN_UNITS)]
            for j in range(NJ):
                both = up[:, :, :, j, :].reshape(P, KD, 2 * FC)
                stream[0][first[0] + j] = both[:, :KA].reshape(P, UNIT)
                stream[1][first[1] + j] = both[:, KA:].reshape(P, UNIT)
                rows = dn[:, 2 * j:2 * j + 2].reshape(P, UNIT)
                if j < NJ - 1:
                    stream[2][first[2] + j] = rows
                else:
                    last[2 * layer + f] = rows
        first = [b + n for b, n in zip(base, FFN_UNITS)]
        w = tiles(a["mix_w_in"][layer])
        for c, cols in enumerate(chunks):
            for half in range(2):
                u = 2 * c + half
                part = w[:, half * KA:(half + 1) * KA][:, :, cols].reshape(P, -1)
                stream[u % NS][first[u % NS] + u // NS, :, :part.shape[1]] = part
        w = tiles(a["mix_w_out"][layer])
        for n in range(KD // 2):
            u = 2 * N_CHUNK + n
            stream[u % NS][first[u % NS] + u // NS] = w[:, 2 * n:2 * n + 2].reshape(P, UNIT)

    ada = [a["ada_w"][layer].reshape(D, 9, D)[:, m] for layer in range(L) for m in range(9)]
    bias = [a["ada_b"][layer].reshape(9, D)[m] for layer in range(L) for m in range(9)]
    nothing = np.zeros((D, D), np.float32)
    ada += [nothing, nothing]
    bias += [nothing[0], nothing[0]]
    ada_first = np.stack([tiles(ada[0]), tiles(ada[1])], axis=2).transpose(1, 0, 2, 3).reshape(KD, P, 2 * D)
    ada_w = np.empty((3 * L, KD, P, 3, D), np.float32)
    ada_bias = np.zeros((3 * L + 1, 3, D), np.float32)
    ada_bias[0, 1:] = bias[:2]
    for g in range(3 * L):
        for m in range(3):
            ada_w[g, :, :, m] = ada[2 + 3 * g + m].reshape(KD, P, D)
            ada_bias[g + 1, m] = bias[2 + 3 * g + m]

    def cols(v):
        return v.reshape(-1, P).T

    gains = [a[n][layer] for layer in range(L) for n in ("norm1", "norm_mix", "norm2")] + [nothing[0]]
    arrays = {
        "x_in": a["x"].reshape(T, P, D).transpose(1, 0, 2),
        "cond_in": cols(a["c"][0]),
        "stream0": stream[0],
        "stream1": stream[1],
        "stream2": stream[2],
        "w_last": last,
        "ada_first": ada_first,
        "ada_w": ada_w.reshape(3 * L * KD, P, ADA_W),
        "ada_bias": ada_bias,
        "gains": np.stack([cols(g) for g in gains], axis=1),
        "sinks": np.broadcast_to(a["attn_sinks"][:, None, :], (L, P, HEADS)),
        "gate_w": a["gla_w_gate"],
        "gate_b": np.stack([cols(b) for b in a["gla_b_gate"]]),
        "gla_gain": np.broadcast_to(a["gla_out_norm"][:, None, :], (L, P, DV)),
        "final_gain": np.broadcast_to(a["final_norm"][None, :], (P, D)),
    }
    arrays = {k: np.ascontiguousarray(v) for k, v in arrays.items()}
    nc = bacc.Bacc("TRN2", target_bir_lowering=False, num_devices=1)
    args = [nc.dram_tensor(k, v.shape, mybir.dt.from_np(v.dtype), kind="ExternalInput").ap() for k, v in arrays.items()]
    out = nc.dram_tensor("out", (SEQ, D), F32, kind="ExternalOutput").ap()
    trunk(nc, *args, out)
    r = run_bass_kernel_spmd(nc, [arrays], core_ids=[0])
    return r.results[0]["out"].reshape(1, SEQ, D)
```
